# Optimizing a Trainium2 kernel written in Bass

```python
import math
import jax
import jax.numpy as jnp
from jax import lax
import numpy as np

D_MODEL = 1024
BATCH = 1
SEQ = 128
DEPTH = 4
DEC_BATCH = 1
DEC_SEQ = 128
PAST_LEN = 128

GRID_W = 64
N_MIXERS = 4
N_LAYERS_FOURIER = (DEPTH + 3) // 4
N_LAYERS_NA = (DEPTH + 2) // 4
N_LAYERS_GMLP = (DEPTH + 1) // 4
N_LAYERS_SSD = DEPTH // 4
N_MOD = 6
EPS = 1e-6
NEG_INF = -1e30

FNET_GROUPS = 8
FNET_GROUP_DIM = D_MODEL // FNET_GROUPS

NA_HEADS = 16
NA_HEAD_DIM = D_MODEL // NA_HEADS
NA_WIN_ROWS_MAX = 8
NA_WIN_COLS = 16
NA_COL_BLOCK = 16
NA_COL_BAND = NA_COL_BLOCK + NA_WIN_COLS
CTX_Q_BLOCK = 128

GMLP_CHUNK = 128
GMLP_DFF = 2 * D_MODEL
GMLP_GROUPS = 8
GMLP_GROUP_DIM = GMLP_DFF // GMLP_GROUPS

SSD_D_INNER = 2 * D_MODEL
SSD_HEAD_DIM = 64
SSD_HEADS = SSD_D_INNER // SSD_HEAD_DIM
SSD_GROUPS = 8
SSD_STATE = 128
SSD_CONV = 4
SSD_CHUNK = 128
SSD_CONV_DIM = SSD_D_INNER + 2 * SSD_GROUPS * SSD_STATE
SSD_PROJ = SSD_D_INNER + SSD_CONV_DIM + 2 * SSD_HEADS

MOE_GROUPS = 4
MOE_EXPERTS_PER_GROUP = 4
MOE_EXPERTS = MOE_GROUPS * MOE_EXPERTS_PER_GROUP
MOE_TOP_K = 2
MOE_D_FF = 512

kernel_name = 'hybrid_dit_context_prefix_step'

def rmsnorm(x, g):
    x32 = x.astype(jnp.float32)
    y = x32 * lax.rsqrt(jnp.mean(x32 * x32, axis=-1, keepdims=True) + EPS)
    return (y * g.astype(jnp.float32)).astype(x.dtype)

def adaln(cond, w, b):
    return (jax.nn.silu(cond) @ w + b).reshape(cond.shape[0], N_MOD, D_MODEL)

def modulate(x, mod, i):
    return x * (1 + mod[:, i + 1][:, None, :]) + mod[:, i][:, None, :]

def fourier_mixer(h, w_o):
    b, s, _ = h.shape
    hg = h.astype(jnp.float32).reshape(b, s, FNET_GROUPS, FNET_GROUP_DIM)
    f = jnp.fft.fft2(hg, axes=(1, 3), norm='ortho').real
    return f.reshape(b, s, D_MODEL).astype(h.dtype) @ w_o

def _split_heads(h, w_qkv):
    b, s, _ = h.shape
    qkv = (h @ w_qkv).reshape(b, s, 3, NA_HEADS, NA_HEAD_DIM).transpose(2, 0, 3, 1, 4)
    return qkv[0] * (NA_HEAD_DIM ** -0.5), qkv[1], qkv[2]

def na_context(h, w_qkv, w_o):
    b, s, _ = h.shape
    q, k, v = _split_heads(h, w_qkv)
    nblk = s // CTX_Q_BLOCK
    q_blocks = q.reshape(b, NA_HEADS, nblk, CTX_Q_BLOCK, NA_HEAD_DIM).transpose(2, 0, 1, 3, 4)

    def block(q_i):
        sc = jnp.einsum('bhqd,bhkd->bhqk', q_i, k).astype(jnp.float32)
        p = jax.nn.softmax(sc, axis=-1).astype(v.dtype)
        return jnp.einsum('bhqk,bhkd->bhqd', p, v)

    o = lax.map(block, q_blocks)
    o = o.transpose(1, 0, 3, 2, 4).reshape(b, s, D_MODEL)
    return o @ w_o, k, v

def na_latent(h, k_ctx, v_ctx, w_qkv, w_o, rpb):
    b, s, _ = h.shape
    R = s // GRID_W
    kr = min(NA_WIN_ROWS_MAX, R)
    ncb = GRID_W // NA_COL_BLOCK
    q, k, v = _split_heads(h, w_qkv)
    q = q.reshape(b, NA_HEADS, R, GRID_W, NA_HEAD_DIM)
    k = k.reshape(b, NA_HEADS, R, GRID_W, NA_HEAD_DIM)
    v = v.reshape(b, NA_HEADS, R, GRID_W, NA_HEAD_DIM)
    cols = jnp.arange(GRID_W)
    win0 = jnp.clip(cols - NA_WIN_COLS // 2, 0, GRID_W - NA_WIN_COLS).reshape(ncb, NA_COL_BLOCK)
    band0 = jnp.clip(jnp.arange(ncb) * NA_COL_BLOCK - NA_WIN_COLS // 2, 0, GRID_W - NA_COL_BAND)
    band_cols = band0[:, None] + jnp.arange(NA_COL_BAND)[None, :]
    qcols = cols.reshape(ncb, NA_COL_BLOCK)
    kc = band_cols[:, None, :]
    col_ok = (kc >= win0[:, :, None]) & (kc < win0[:, :, None] + NA_WIN_COLS)
    dc_idx = jnp.clip(kc - qcols[:, :, None], 1 - NA_WIN_COLS, NA_WIN_COLS - 1) + NA_WIN_COLS - 1
    k_band = k[:, :, :, band_cols]
    v_band = v[:, :, :, band_cols]
    q_blk = q.reshape(b, NA_HEADS, R, ncb, NA_COL_BLOCK, NA_HEAD_DIM).transpose(2, 0, 1, 3, 4, 5)

    def row(args):
        r, q_r = args
        rs = jnp.clip(r - kr // 2, 0, R - kr)
        kb = lax.dynamic_slice_in_dim(k_band, rs, kr, axis=2)
        vb = lax.dynamic_slice_in_dim(v_band, rs, kr, axis=2)
        dr_idx = rs + jnp.arange(kr) - r + NA_WIN_ROWS_MAX - 1
        bias = rpb[:, dr_idx][:, :, dc_idx].transpose(0, 2, 3, 1, 4)
        s_loc = jnp.einsum('bhnqd,bhinkd->bhnqik', q_r, kb).astype(jnp.float32) + bias.astype(jnp.float32)[None]
        s_loc = jnp.where(col_ok[None, None, :, :, None, :], s_loc, NEG_INF)
        s_ctx = jnp.einsum('bhnqd,bhpd->bhnqp', q_r, k_ctx).astype(jnp.float32)
        sc = jnp.concatenate([s_loc.reshape(b, NA_HEADS, ncb, NA_COL_BLOCK, kr * NA_COL_BAND), s_ctx], axis=-1)
        p = jax.nn.softmax(sc, axis=-1).astype(v.dtype)
        p_loc = p[..., :kr * NA_COL_BAND].reshape(b, NA_HEADS, ncb, NA_COL_BLOCK, kr, NA_COL_BAND)
        p_ctx = p[..., kr * NA_COL_BAND:]
        return (jnp.einsum('bhnqik,bhinkd->bhnqd', p_loc, vb)
                + jnp.einsum('bhnqp,bhpd->bhnqd', p_ctx, v_ctx))

    o = lax.map(row, (jnp.arange(R), q_blk))
    o = o.transpose(1, 0, 3, 4, 2, 5).reshape(b, s, D_MODEL)
    return o @ w_o

def gmlp_mixer(h, w_in, g_v, w_s, b_s, w_out):
    b, s, _ = h.shape
    uv = jax.nn.gelu(h @ w_in)
    u, v = uv[..., :GMLP_DFF], uv[..., GMLP_DFF:]
    v = rmsnorm(v, g_v).reshape(b, s // GMLP_CHUNK, GMLP_CHUNK, GMLP_GROUPS, GMLP_GROUP_DIM)
    v = jnp.einsum('gpq,bnqgc->bnpgc', w_s, v) + b_s.T[:, :, None]
    return (u * v.reshape(b, s, GMLP_DFF)) @ w_out

def dwconv(x, w, bias):
    width = w.shape[0]
    left = width // 2
    y = lax.conv_general_dilated(x, w[:, None, :], window_strides=(1,),
                                 padding=[(left, width - 1 - left)],
                                 dimension_numbers=('NWC', 'WIO', 'NWC'),
                                 feature_group_count=x.shape[-1])
    return y + bias

def ssd_scan(x, dt, a, bm, cm, h0):
    b, s, _, _ = x.shape
    hpg = SSD_HEADS // SSD_GROUPS
    L = SSD_CHUNK
    nc = s // L
    f32 = jnp.float32
    x = x.astype(f32).reshape(b, nc, L, SSD_GROUPS, hpg, SSD_HEAD_DIM)
    dt = dt.reshape(b, nc, L, SSD_GROUPS, hpg)
    bm = bm.astype(f32).reshape(b, nc, L, SSD_GROUPS, SSD_STATE)
    cm = cm.astype(f32).reshape(b, nc, L, SSD_GROUPS, SSD_STATE)
    a_cs = jnp.cumsum(dt * a.reshape(SSD_GROUPS, hpg), axis=2)
    dtx = x * dt[..., None]
    lower = jnp.tril(jnp.ones((L, L), bool))[None, None, :, :, None, None]
    seg = a_cs[:, :, :, None] - a_cs[:, :, None, :]
    decay = jnp.exp(jnp.where(lower, seg, -jnp.inf))
    cb = jnp.einsum('bclgn,bcsgn->bclsg', cm, bm)
    y_diag = jnp.einsum('bclsg,bclsgh,bcsghp->bclghp', cb, decay, dtx)
    decay_to_end = jnp.exp(a_cs[:, :, -1:] - a_cs)
    chunk_states = jnp.einsum('bclgn,bclgh,bclghp->bcghpn', bm, decay_to_end, dtx)
    chunk_decay = jnp.exp(a_cs[:, :, -1])

    def step(state, inp):
        st, dec = inp
        return state * dec[..., None, None] + st, state

    h_init = h0.astype(f32).reshape(b, SSD_GROUPS, hpg, SSD_HEAD_DIM, SSD_STATE)
    h_last, h_prev = lax.scan(step, h_init, (jnp.moveaxis(chunk_states, 1, 0), jnp.moveaxis(chunk_decay, 1, 0)))
    h_prev = jnp.moveaxis(h_prev, 0, 1)
    y_off = jnp.einsum('bclgn,bcghpn,bclgh->bclghp', cm, h_prev, jnp.exp(a_cs))
    y = (y_diag + y_off).reshape(b, s, SSD_HEADS, SSD_HEAD_DIM)
    return y, h_last.reshape(b, SSD_HEADS, SSD_HEAD_DIM, SSD_STATE)

def _flip(t):
    return jnp.flip(t, axis=1)

def ssd_mixer(h, h0_f, h0_b, w_in, conv_w, conv_b, a_log, dt_bias, d_skip, g_norm, w_out):
    b, s, _ = h.shape
    proj = h @ w_in
    z = proj[..., :SSD_D_INNER]
    xbc = jax.nn.silu(dwconv(proj[..., SSD_D_INNER:SSD_D_INNER + SSD_CONV_DIM], conv_w, conv_b))
    dt_raw = proj[..., SSD_D_INNER + SSD_CONV_DIM:].astype(jnp.float32).reshape(b, s, 2, SSD_HEADS)
    gn = SSD_GROUPS * SSD_STATE
    x = xbc[..., :SSD_D_INNER].reshape(b, s, SSD_HEADS, SSD_HEAD_DIM)
    bm = xbc[..., SSD_D_INNER:SSD_D_INNER + gn].reshape(b, s, SSD_GROUPS, SSD_STATE)
    cm = xbc[..., SSD_D_INNER + gn:].reshape(b, s, SSD_GROUPS, SSD_STATE)
    dt = jax.nn.softplus(dt_raw + dt_bias.astype(jnp.float32))
    a = -jnp.exp(a_log.astype(jnp.float32))
    y_f, hf = ssd_scan(x, dt[:, :, 0], a[0], bm, cm, h0_f)
    y_b, hb = ssd_scan(_flip(x), _flip(dt[:, :, 1]), a[1], _flip(bm), _flip(cm), h0_b)
    y = y_f + _flip(y_b) + d_skip.astype(jnp.float32)[:, None] * x.astype(jnp.float32)
    y = y.reshape(b, s, SSD_D_INNER) * jax.nn.silu(z.astype(jnp.float32))
    y = rmsnorm(y, g_norm).astype(h.dtype)
    return y @ w_out, hf, hb

def hier_moe(h, w_gr, b_gr, w_er, b_er, w_gate, w_up, w_down):
    t = h.reshape(-1, D_MODEL)
    g_prob = jax.nn.softmax((t @ w_gr).astype(jnp.float32) + b_gr.astype(jnp.float32), axis=-1)
    g_p, g_idx = lax.top_k(g_prob, 1)
    e_logits = ((t @ w_er).astype(jnp.float32) + b_er.astype(jnp.float32)).reshape(-1, MOE_GROUPS, MOE_EXPERTS_PER_GROUP)
    e_logits = jnp.take_along_axis(e_logits, g_idx[:, :, None], axis=1)[:, 0]
    e_p, e_idx = lax.top_k(jax.nn.softmax(e_logits, axis=-1), MOE_TOP_K)
    w = g_p * e_p / jnp.sum(e_p, axis=-1, keepdims=True)
    sel = jax.nn.one_hot(g_idx * MOE_EXPERTS_PER_GROUP + e_idx, MOE_EXPERTS, dtype=jnp.float32)
    combine = jnp.einsum('tk,tke->te', w, sel)
    hg = jnp.einsum('td,edf->tef', t, w_gate)
    hu = jnp.einsum('td,edf->tef', t, w_up)
    act = jax.nn.silu(hg) * hu * combine[:, :, None].astype(t.dtype)
    return jnp.einsum('tef,efd->td', act, w_down).reshape(h.shape)

def setup_inputs(seed: int = 0) -> dict:
    key = jax.random.key(seed)
    k = jax.random.split(key, 40)
    f32 = jnp.float32

    def nrm(i, shape, scale):
        return jax.random.normal(k[i], shape, f32) * scale

    dt0 = jnp.exp(jax.random.uniform(k[26], (N_LAYERS_SSD, 2, SSD_HEADS), f32, math.log(1e-3), math.log(1e-1)))
    return {
        'x_prompt': nrm(0, (BATCH, SEQ, D_MODEL), 1.0),
        'x_sample': nrm(1, (DEC_BATCH, DEC_SEQ, D_MODEL), 1.0),
        'cache_k': nrm(2, (DEC_BATCH, N_LAYERS_NA, NA_HEADS, PAST_LEN, NA_HEAD_DIM), 1.0),
        'cache_v': nrm(3, (DEC_BATCH, N_LAYERS_NA, NA_HEADS, PAST_LEN, NA_HEAD_DIM), 1.0),
        'state_ssm_fwd': nrm(4, (DEC_BATCH, N_LAYERS_SSD, SSD_HEADS, SSD_HEAD_DIM, SSD_STATE), 0.1),
        'state_ssm_bwd': nrm(5, (DEC_BATCH, N_LAYERS_SSD, SSD_HEADS, SSD_HEAD_DIM, SSD_STATE), 0.1),
        'c': nrm(6, (DEC_BATCH, D_MODEL), 1.0),
        'c_ctx': nrm(7, (D_MODEL,), 1.0),
        'ada_w': nrm(8, (DEPTH, D_MODEL, N_MOD * D_MODEL), 0.5 * D_MODEL ** -0.5),
        'ada_b': nrm(9, (DEPTH, N_MOD * D_MODEL), 0.02),
        'norm1_g': 1.0 + nrm(10, (DEPTH, D_MODEL), 0.02),
        'norm2_g': 1.0 + nrm(11, (DEPTH, D_MODEL), 0.02),
        'final_g': 1.0 + nrm(12, (D_MODEL,), 0.02),
        'fnet_w_o': nrm(13, (N_LAYERS_FOURIER, D_MODEL, D_MODEL), D_MODEL ** -0.5),
        'na_w_qkv': nrm(14, (N_LAYERS_NA, D_MODEL, 3 * D_MODEL), D_MODEL ** -0.5),
        'na_w_o': nrm(15, (N_LAYERS_NA, D_MODEL, D_MODEL), D_MODEL ** -0.5),
        'na_rpb': nrm(16, (N_LAYERS_NA, NA_HEADS, 2 * NA_WIN_ROWS_MAX - 1, 2 * NA_WIN_COLS - 1), 0.1),
        'gmlp_w_in': nrm(17, (N_LAYERS_GMLP, D_MODEL, 2 * GMLP_DFF), D_MODEL ** -0.5),
        'gmlp_g_v': 1.0 + nrm(18, (N_LAYERS_GMLP, GMLP_DFF), 0.02),
        'gmlp_w_s': nrm(19, (N_LAYERS_GMLP, GMLP_GROUPS, GMLP_CHUNK, GMLP_CHUNK), GMLP_CHUNK ** -0.5),
        'gmlp_b_s': 1.0 + nrm(20, (N_LAYERS_GMLP, GMLP_GROUPS, GMLP_CHUNK), 0.1),
        'gmlp_w_out': nrm(21, (N_LAYERS_GMLP, GMLP_DFF, D_MODEL), GMLP_DFF ** -0.5),
        'ssd_w_in': nrm(22, (N_LAYERS_SSD, D_MODEL, SSD_PROJ), D_MODEL ** -0.5),
        'ssd_conv_w': nrm(23, (N_LAYERS_SSD, SSD_CONV, SSD_CONV_DIM), SSD_CONV ** -0.5),
        'ssd_conv_b': nrm(24, (N_LAYERS_SSD, SSD_CONV_DIM), 0.02),
        'ssd_a_log': jnp.log(jax.random.uniform(k[25], (N_LAYERS_SSD, 2, SSD_HEADS), f32, 1.0, 16.0)),
        'ssd_dt_bias': dt0 + jnp.log(-jnp.expm1(-dt0)),
        'ssd_d_skip': 1.0 + nrm(27, (N_LAYERS_SSD, SSD_HEADS), 0.02),
        'ssd_g_norm': 1.0 + nrm(28, (N_LAYERS_SSD, SSD_D_INNER), 0.02),
        'ssd_w_out': nrm(29, (N_LAYERS_SSD, SSD_D_INNER, D_MODEL), SSD_D_INNER ** -0.5),
        'moe_w_gr': nrm(30, (DEPTH, D_MODEL, MOE_GROUPS), D_MODEL ** -0.5),
        'moe_b_gr': nrm(31, (DEPTH, MOE_GROUPS), 0.01),
        'moe_w_er': nrm(32, (DEPTH, D_MODEL, MOE_EXPERTS), D_MODEL ** -0.5),
        'moe_b_er': nrm(33, (DEPTH, MOE_EXPERTS), 0.01),
        'moe_w_gate': nrm(34, (DEPTH, MOE_EXPERTS, D_MODEL, MOE_D_FF), D_MODEL ** -0.5),
        'moe_w_up': nrm(35, (DEPTH, MOE_EXPERTS, D_MODEL, MOE_D_FF), D_MODEL ** -0.5),
        'moe_w_down': nrm(36, (DEPTH, MOE_EXPERTS, MOE_D_FF, D_MODEL), MOE_D_FF ** -0.5),
    }

def reference(x_prompt, x_sample, cache_k, cache_v, state_ssm_fwd, state_ssm_bwd, c, c_ctx,
              ada_w, ada_b, norm1_g, norm2_g, final_g, fnet_w_o,
              na_w_qkv, na_w_o, na_rpb,
              gmlp_w_in, gmlp_g_v, gmlp_w_s, gmlp_b_s, gmlp_w_out,
              ssd_w_in, ssd_conv_w, ssd_conv_b, ssd_a_log, ssd_dt_bias, ssd_d_skip, ssd_g_norm, ssd_w_out,
              moe_w_gr, moe_b_gr, moe_w_er, moe_b_er, moe_w_gate, moe_w_up, moe_w_down):
    hp, hs = x_prompt, x_sample
    bsz = x_prompt.shape[0]
    new_k, new_v, new_sf, new_sb = [], [], [], []
    for l in range(DEPTH):
        kind, j = l % N_MIXERS, l // N_MIXERS
        mp = adaln(c_ctx[None, :], ada_w[l], ada_b[l])
        ms = adaln(c, ada_w[l], ada_b[l])
        ap = modulate(rmsnorm(hp, norm1_g[l]), mp, 0)
        a_s = modulate(rmsnorm(hs, norm1_g[l]), ms, 0)
        if kind == 0:
            op = fourier_mixer(ap, fnet_w_o[j])
            os_ = fourier_mixer(a_s, fnet_w_o[j])
        elif kind == 1:
            op, kp, vp = na_context(ap, na_w_qkv[j], na_w_o[j])
            os_ = na_latent(a_s, cache_k[:, j], cache_v[:, j], na_w_qkv[j], na_w_o[j], na_rpb[j])
            new_k.append(kp)
            new_v.append(vp)
        elif kind == 2:
            op = gmlp_mixer(ap, gmlp_w_in[j], gmlp_g_v[j], gmlp_w_s[j], gmlp_b_s[j], gmlp_w_out[j])
            os_ = gmlp_mixer(a_s, gmlp_w_in[j], gmlp_g_v[j], gmlp_w_s[j], gmlp_b_s[j], gmlp_w_out[j])
        else:
            zero = jnp.zeros((bsz, SSD_HEADS, SSD_HEAD_DIM, SSD_STATE), jnp.float32)
            op, sf, sb = ssd_mixer(ap, zero, zero, ssd_w_in[j], ssd_conv_w[j], ssd_conv_b[j], ssd_a_log[j],
                                   ssd_dt_bias[j], ssd_d_skip[j], ssd_g_norm[j], ssd_w_out[j])
            os_ = ssd_mixer(a_s, state_ssm_fwd[:, j], state_ssm_bwd[:, j], ssd_w_in[j], ssd_conv_w[j], ssd_conv_b[j],
                            ssd_a_log[j], ssd_dt_bias[j], ssd_d_skip[j], ssd_g_norm[j], ssd_w_out[j])[0]
            new_sf.append(sf)
            new_sb.append(sb)
        hp = hp + mp[:, 2][:, None, :] * op
        hs = hs + ms[:, 2][:, None, :] * os_
        hp = hp + mp[:, 5][:, None, :] * hier_moe(modulate(rmsnorm(hp, norm2_g[l]), mp, 3), moe_w_gr[l], moe_b_gr[l],
                                                  moe_w_er[l], moe_b_er[l], moe_w_gate[l], moe_w_up[l], moe_w_down[l])
        hs = hs + ms[:, 5][:, None, :] * hier_moe(modulate(rmsnorm(hs, norm2_g[l]), ms, 3), moe_w_gr[l], moe_b_gr[l],
                                                  moe_w_er[l], moe_b_er[l], moe_w_gate[l], moe_w_up[l], moe_w_down[l])
    y_prompt = rmsnorm(hp, final_g)
    y_sample = rmsnorm(hs, final_g)
    new_cache_k = jnp.stack(new_k, axis=1)
    new_cache_v = jnp.stack(new_v, axis=1)
    new_state_ssm_fwd = jnp.stack(new_sf, axis=1)
    new_state_ssm_bwd = jnp.stack(new_sb, axis=1)
    return (y_prompt, y_sample, new_cache_k, new_cache_v, new_state_ssm_fwd, new_state_ssm_bwd)


_drawn_inputs = setup_inputs


def setup_inputs(seed=0):
    import zlib

    import numpy as np

    out = dict(_drawn_inputs(seed))
    spreads = {}
    factors = {'final_g': 2.882,
     'na_rpb': 8.0,
     'gmlp_g_v': 8.0,
     'ssd_d_skip': 8.0,
     'ssd_g_norm': 8.0,
     'moe_b_gr': 4.176,
     'moe_b_er': 4.556}
    for name, (base, spread) in spreads.items():
        noise = np.random.default_rng([zlib.crc32(name.encode()), seed]).standard_normal(out[name].shape)
        drawn = base * np.exp(spread * noise) if base else spread * noise
        out[name] = jnp.asarray(drawn.astype(out[name].dtype))
    for name, factor in factors.items():
        out[name] = (out[name] * factor).astype(out[name].dtype)
    return out
```

```python
import numpy as np
import concourse.bass as bass
from concourse import mybir
from contextlib import ExitStack

FP32 = mybir.dt.float32
ALU = mybir.AluOpType
ACT = mybir.ActivationFunctionType
AX = mybir.AxisListType

P = 128
D = 1024
DC = D // P
S = 2
T = S * P
DEPTH = 4
EPS = 1e-6
RING = 4
SLOT_COLS = 512
NMOD = 6
HEADS = 16
HD = 64
E = 16
EG = 4
FF = 512
NR = EG + E
GDFF = 2048
SG = 8
HPG = 4
SH = 32
XBC = 4096
ARENA = 15616
LAYERS = (0, 1, 2, 3)

XU = 4
ADA_LOADS = NMOD * D // SLOT_COLS
MIX_LOADS = {0: 2, 1: 8, 2: 12, 3: 17}
MOE_LOADS = 3 * E

VECS = [("g1", DEPTH * DC), ("g2", DEPTH * DC), ("ada_b", DEPTH * NMOD * DC), ("cond", DC * S),
        ("gv", GDFF // P), ("gn", 2 * D // P), ("conv_w", 4 * XBC // P), ("conv_b", XBC // P)]
VEC_AT, _n = {}, 0
for _name, _w in VECS:
    VEC_AT[_name] = (_n, _w)
    _n += _w
VEC_COLS = _n
MATS = ["ident", "ones", "t_le", "t_ge", "t_gt", "t_lt", "dft_c", "dft_s", "seq_c", "seq_ns", "na_mask"]
MAT_AT = {m: i for i, m in enumerate(MATS)}


def build(nc, a, o):
    ctx = ExitStack()
    with ctx:
        def sb(name, shape):
            return ctx.enter_context(nc.sbuf_tensor(name, shape, FP32))

        def sem(name):
            return ctx.enter_context(nc.semaphore(name))

        ring = sb("ring", [P, RING, DC * SLOT_COLS])
        hid = sb("hid", [P, S, D])
        xn = sb("xn", [P, S, D])
        at = sb("at", [P, DC, T])
        gate = sb("gate", [P, 2, S, D])
        acc = sb("acc", [P, S, D])
        mats = sb("mats", [P, len(MATS), P])
        vecs = sb("vecs", [P, VEC_COLS])
        cond = sb("condT", [P, DC, S])
        modt = sb("modt", [P, NMOD * DC, S])
        gsc = sb("gsc", [P, 2, DC, S])
        wr = sb("wr", [P, DEPTH, DC, NR])
        rbias = sb("rbias", [P, DEPTH, NR])
        first = sb("first", [P, EG])
        finalg = sb("finalg", [P, D])
        stat = sb("stat", [P, 32])
        outtmp = sb("outtmp", [P, 2, SLOT_COLS])
        rt = sb("rt", [P, 24, S, EG])
        rlog = sb("rlog", [P, S, NR])
        rsel = sb("rsel", [P, S, EG, EG])
        comb = sb("comb", [P, S, E])
        arena = sb("arena", [P, ARENA])

        def carve(at0, *shape):
            n = int(np.prod(shape))
            assert at0 + n <= ARENA, (at0, n)
            v = arena[:, at0:at0 + n]
            if len(shape) == 2:
                v = v.rearrange("p (a b) -> p a b", a=shape[0])
            elif len(shape) == 3:
                v = v.rearrange("p (a b c) -> p a b c", a=shape[0], b=shape[1])
            return v

        actT = carve(0, 4, T)
        sgl = carve(1024, 4, T)
        f1 = carve(0, 2, 512)
        ft = carve(1024, DC, T)
        qT = carve(0, DC, T)
        kT = carve(2048, DC, T)
        vtok = carve(4096, S, D)
        kcT = carve(6144, DC, P)
        vctx = carve(7168, 1, D)
        rpb = carve(8192, HEADS, P)
        oT = carve(10240, DC, T)
        prob = carve(12288, 2, 512)
        probT = carve(13312, 2, 512)
        nmax = carve(14336, 16, 2)
        esum = carve(14368, 16, 2)
        rsum = carve(14400, 16, 2)
        uT = carve(0, 16, T)
        vg = carve(4096, S, GDFF)
        wsT = carve(8192, SG, P)
        bs = carve(9216, SG, P)
        gt = carve(10240, 2, T)
        xbcT = carve(0, 32, T)
        zs = carve(8192, S, 2 * D)
        segs = carve(12288, 2, 512)
        ttri = carve(13312, 2, 512)
        yfix = carve(14336, 1, 256)
        xtok = acc[:, 0, 0:512]
        cbm = sb("cbm", [P, 2, P])
        dtx = acc[:, 0, 512:1024].rearrange("p (d n) -> p d n", d=2)
        dtxw = acc[:, 1, 0:512].rearrange("p (d n) -> p d n", d=2)
        stout = carve(14592, 1, 512)
        offs = carve(15104, 1, 512)
        h0 = acc[:, 1:2, 512:1024]
        dtw = sb("dtw", [P, 8, S * 64])
        adt = sb("adt", [P, S, 64])
        nadt = sb("nadt", [P, S, 64])
        edec = sb("edec", [P, 2, 64])
        dtb = sb("dtb", [P, 3, 64])

        psum = ctx.enter_context(nc.psum_tensor("psum", [P, 8, 512], FP32))
        ps = [psum[:, i, :] for i in range(8)]

        def bank(i, *shape):
            v = ps[i][:, :int(np.prod(shape))]
            if len(shape) == 2:
                v = v.rearrange("p (a b) -> p a b", a=shape[0])
            elif len(shape) == 3:
                v = v.rearrange("p (a b c) -> p a b c", a=shape[0], b=shape[1])
            return v

        def vec(name):
            n, w = VEC_AT[name]
            return vecs[:, n:n + w]

        def mat(name):
            return mats[:, MAT_AT[name], :]

        def slot(k):
            return ring[:, k % RING, :].rearrange("p (c n) -> p c n", c=DC)

        def slot_down(k):
            return ring[:, k % RING, :].rearrange("p (c n) -> p c n", c=FF // P)

        full = [sem(f"ring_full{i}") for i in range(RING)]
        slot_done = sem("slot_done")
        consts_in = sem("consts_in")
        small_in = {i: sem(f"small_in{i}") for i in (1, 2, 3)}
        cond_ready = sem("cond_ready")
        ada_ev = sem("ada_ev")
        gsc_ready = sem("gsc_ready")
        gate_mm, gate_ev = sem("gate_mm"), sem("gate_ev")
        sq_done, var_ready, rstd_ready, xn_ready = sem("sq_done"), sem("var_ready"), sem("rstd_ready"), sem("xn_ready")
        tr_mm, at_act, at_dve = sem("tr_mm"), sem("at_act"), sem("at_dve")
        o_mm, h_ready = sem("o_mm"), sem("h_ready")
        route_mm = sem("route_mm")
        rexp = sem("router_exp_ready")
        rexp_in = sem("router_exp_in")
        g_mm, sg_ready, act_ready = sem("g_mm"), sem("sg_ready"), sem("act_ready")
        y_mm, y_ev = sem("y_mm"), sem("y_ev")
        dve_chain, pool_chain = sem("dve_chain"), sem("pool_chain")
        f1_mm, f1_ev, f2_mm, ft_ready = sem("f1_mm"), sem("f1_ev"), sem("f2_mm"), sem("ft_ready")
        qk_mm, qk_ev, v_mm, v_ev = sem("qk_mm"), sem("qk_ev"), sem("v_mm"), sem("v_ev")
        kt_mm, kt_ev = sem("ktok_mm"), sem("ktok_ev")
        s_mm, nm_ready, e_ready, p_ready = sem("scores_mm"), sem("nmax_ready"), sem("exp_ready"), sem("prob_ready")
        t_mm, pt_ready, av_mm, ot_ready = sem("probT_mm"), sem("probT_ready"), sem("av_mm"), sem("oT_ready")
        m_mm, m_ev = sem("gmlp_mm"), sem("gmlp_ev")
        vsq, vvar, vrstd, vn_ready = sem("v_sq"), sem("v_var"), sem("v_rstd"), sem("vn_ready")
        sp_mm, sp_ev = sem("spatial_mm"), sem("gated_ready")
        x_mm, x_b, x_cv, x_act = sem("xbc_mm"), sem("xbc_tap"), sem("xbc_conv"), sem("xbc_ready")
        dt_exp, dt_ln = sem("dt_exp"), sem("dt_ln")
        dt_abs, a_exp = sem("dt_abs"), sem("a_exp")
        adt_ready, cum_mm, edec_ready = sem("adt_ready"), sem("cum_mm"), sem("edec_ready")
        z_mm, z_ev = sem("z_mm"), sem("z_ev")
        xt_mm, xt_ev, tt_ready = sem("xtok_mm"), sem("xtok_ev"), sem("tri_dt_ready")
        seg_mm, seg_ready, dec_ready, m_ready = sem("seg_mm"), sem("seg_ready"), sem("decay_ready"), sem("mix_ready")
        dtx_ready, yg_mm, y_done = sem("dtx_ready"), sem("yg_mm"), sem("y_done")
        off_ev, h0_in, st_out = sem("off_ev"), sem("h0_in"), sem("st_out")
        ysq, yvar, yrstd, yn_ready, yt_mm, yt_ev = (sem("y_sq"), sem("y_var"), sem("y_rstd"), sem("yn_ready"),
                                                     sem("yT_mm"), sem("yT_ready"))
        kv_out, fin_ready, fin_out = sem("kv_out"), sem("fin_ready"), sem("fin_out")

        def ada_base(n):
            return sum(ADA_LOADS + MIX_LOADS[x] + MOE_LOADS for x in LAYERS[:n])

        def mix_base(n):
            return ada_base(n) + ADA_LOADS

        def moe_base(n):
            return mix_base(n) + MIX_LOADS[LAYERS[n]]

        def block_of(w, rows0, cols):
            return w[rows0:rows0 + D, cols].rearrange("(c p) n -> p c n", p=P)

        ctx.enter_context(nc.allow_non_contiguous_dma("small constants, weight blocks by rows"))
        block = ctx.enter_context(nc.Block())

        @block.sync
        def _(sp):
            def load(k, dst, src, i=None, per=0):
                if i is not None:
                    sp.wait_ge(slot_done, i * per + (k - RING + 1))
                elif k >= RING:
                    sp.wait_ge(slot_done, k - RING + 1)
                sp.dma_start(dst, src).then_inc(full[k % RING], 16)

            for n, l in enumerate(LAYERS):
                k = ada_base(n)
                if n == 0:
                    for j in range(ADA_LOADS):
                        load(k + j, slot(k + j), block_of(a["ada_w"][l], 0, slice(j * SLOT_COLS, (j + 1) * SLOT_COLS)))
                else:
                    with sp.Fori(0, ADA_LOADS // RING) as i:
                        for j in range(RING):
                            load(k + j, slot(k + j), block_of(
                                a["ada_w"][l], 0, bass.ds(i * (RING * SLOT_COLS) + j * SLOT_COLS, SLOT_COLS)), i, RING)
                k = mix_base(n)
                if l == 0:
                    todo = [(a["fnet_w_o"][0], 0, j) for j in range(2)]
                elif l == 1:
                    todo = [(a["na_w_qkv"][0], 0, j) for j in range(6)] + [(a["na_w_o"][0], 0, j) for j in range(2)]
                elif l == 2:
                    todo = [(a["gmlp_w_in"][0], 0, j) for j in range(8)]
                    todo += [(a["gmlp_w_out"][0], kk * D, j) for j in range(2) for kk in range(2)]
                else:
                    todo = [(a["ssd_w_in"][0], 0, 4 + j) for j in range(8)] + [None]
                    todo += [(a["ssd_w_in"][0], 0, j) for j in range(4)]
                    todo += [(a["ssd_w_out"][0], kk * D, j) for j in range(2) for kk in range(2)]
                for q, it in enumerate(todo):
                    if it is None:
                        load(k + q, slot(k + q)[:, :, 0:64], block_of(a["ssd_w_in"][0], 0, slice(2 * D + XBC, 2 * D + XBC + 64)))
                    else:
                        w, r0, j = it
                        load(k + q, slot(k + q), block_of(w, r0, slice(j * SLOT_COLS, (j + 1) * SLOT_COLS)))
                assert len(todo) == MIX_LOADS[l]
                k = moe_base(n)
                with sp.Fori(0, E // XU) as i:
                    for x in range(XU):
                        for q, w in enumerate(("moe_w_gate", "moe_w_up", "moe_w_down")):
                            kk = k + 3 * x + q
                            rows = a[w][l].rearrange("e (c p) n -> e p c n", p=P)
                            src = rows[bass.ds(i * XU + x, 1)].rearrange("o p c n -> p (o c) n")
                            load(kk, slot_down(kk) if q == 2 else slot(kk), src, i, 3 * XU)

        @block.gpsimd
        def _(pool):
            pool.dma_start(vecs[:, :], a["vecs"]).then_inc(consts_in, 16)
            pool.dma_start(mats[:, :, :], a["mats"]).then_inc(consts_in, 16)
            pool.dma_start(hid[:, 0, :], a["x_prompt"][0]).then_inc(consts_in, 16)
            pool.dma_start(hid[:, 1, :], a["x_sample"][0]).then_inc(consts_in, 16)
            pool.dma_start(wr[:, :, :, 0:EG], a["wgr"]).then_inc(consts_in, 16)
            pool.dma_start(wr[:, :, :, EG:NR], a["wer"]).then_inc(consts_in, 16)
            pool.dma_start(rbias[:, :, 0:EG], a["moe_b_gr"].partition_broadcast(P)).then_inc(consts_in, 16)
            pool.dma_start(rbias[:, :, EG:NR], a["moe_b_er"].partition_broadcast(P)).then_inc(consts_in, 16)
            pool.dma_start(finalg[:, :], a["final_g"].partition_broadcast(P)).then_inc(consts_in, 16)
            for j in range(EG):
                pool.memset(first[:, j:j + 1], float(EG - j)).then_inc(pool_chain, 1)
            for n, l in enumerate(LAYERS):
                if l in small_in:
                    if n:
                        pool.wait_ge(h_ready, 8 * n)
                if l == 1:
                    pool.dma_start(rpb, a["rpb_band"]).then_inc(small_in[1], 16)
                    pool.dma_start(kcT, a["cache_kT"]).then_inc(small_in[1], 16)
                    pool.dma_start(vctx[:, 0, :].rearrange("p (h d) -> p h d", h=HEADS),
                                   a["cache_v"][0, 0].rearrange("h t d -> t h d")).then_inc(small_in[1], 16)
                    pool.wait_ge(v_ev, S)
                    pool.wait_ge(v_ev, S * 2)
                    pool.dma_start(o["new_cache_v"][0, 0].rearrange("h t d -> t h d"),
                                   vtok[:, 0, :].rearrange("p (h d) -> p h d", h=HEADS)).then_inc(kv_out, 16)
                    pool.wait_ge(kt_ev, 2)
                    pool.dma_start(o["new_cache_k"][0, 0].rearrange("h t d -> t h d"),
                                   xn[:, 0, :].rearrange("p (h d) -> p h d", h=HEADS)).then_inc(kv_out, 16)
                if l == 2:
                    pool.dma_start(wsT, a["wsT"]).then_inc(small_in[2], 16)
                    pool.dma_start(bs, a["gmlp_b_s"][0].partition_broadcast(P)).then_inc(small_in[2], 16)
                if l == 3:
                    pool.dma_start(dtb[:, 0, :], a["ssd_dt_bias"][0].rearrange("a b -> (a b)").partition_broadcast(P)).then_inc(small_in[3], 16)
                    pool.dma_start(dtb[:, 1, :], a["ssd_a_log"][0].rearrange("a b -> (a b)").partition_broadcast(P)).then_inc(small_in[3], 16)
                    pool.dma_start(dtb[:, 2, 0:SH], a["ssd_d_skip"][0].partition_broadcast(P)).then_inc(small_in[3], 16)
                    pool.wait_ge(adt_ready, 1)
                    tri = [mat("t_le"), mat("t_ge")]
                    for u in range(S * SG):
                        s, g = divmod(u, SG)
                        if u:
                            pool.wait_ge(seg_mm, 2 * u)
                        for d in range(2):
                            pool.tensor_tensor(
                                ttri[:, d, :].rearrange("p (h l) -> p h l", h=HPG),
                                tri[d].unsqueeze(1).to_broadcast([P, HPG, P]),
                                adt[:, s, d * SH + g * HPG:d * SH + (g + 1) * HPG].unsqueeze(2).to_broadcast([P, HPG, P]),
                                ALU.mult).then_inc(tt_ready, 1)
                        if s == 1:
                            if g:
                                pool.wait_ge(yg_mm, u)
                            pool.dma_start(h0[:, 0, :].rearrange("p (d n) -> p d n", d=2),
                                           a["h0T"][:, :, g * 256:(g + 1) * 256]).then_inc(h0_in, 16)
                        else:
                            pool.wait_ge(off_ev, u + 1)
                            for d, name in enumerate(("new_state_ssm_fwd", "new_state_ssm_bwd")):
                                pool.dma_start(
                                    o[name][0, 0, g * HPG:(g + 1) * HPG].rearrange("(a b) p n -> (b p) a n", a=2),
                                    stout[:, 0, d * 256:(d + 1) * 256].rearrange("p (a n) -> p a n", a=2)).then_inc(st_out, 16)
            for s in range(S):
                pool.wait_ge(fin_ready, s + 1)
                pool.dma_start(o["y_prompt" if s == 0 else "y_sample"][0], xn[:, s, :]).then_inc(fin_out, 16)
            pool.wait_ge(fin_out, 16 * S)
            if 1 in LAYERS:
                pool.wait_ge(kv_out, 32)
            if 3 in LAYERS:
                pool.wait_ge(st_out, 32 * SG)

        @block.tensor
        def _(pe):
            def arrive(k, i=None, per=0):
                if i is None:
                    pe.wait_ge(full[k % RING], 16 * (k // RING + 1))
                else:
                    pe.wait_ge(full[k % RING], i * (16 * per // RING) + 16 * (k // RING + 1))

            def dense_chan(k, m, dst, src=at, nk=DC):
                for c in range(nk):
                    last = nc.tensor.matmul(dst, slot(k)[:, c, m * P:(m + 1) * P], src[:, c, :],
                                            start=(c == 0), stop=(c == nk - 1))
                return last

            def dense_tok(k, s, dst, src=at, c0=0, nk=DC, start=True, stop=True, cols=SLOT_COLS):
                for c in range(nk):
                    last = nc.tensor.matmul(dst, src[:, c0 + c, s * P:(s + 1) * P], slot(k)[:, c, 0:cols],
                                            start=(start and c == 0), stop=(stop and c == nk - 1))
                return last

            def out_proj(n, k, src, halves):
                for j in range(2):
                    for kk in range(halves):
                        arrive(k)
                        for s in range(S):
                            last = dense_tok(k, s, ps[4 + 2 * j + s][:, :], src, kk * DC, DC, kk == 0, kk == halves - 1)
                            if kk == halves - 1 and s == 0:
                                last.then_inc(o_mm, 1)
                        last.then_inc(slot_done, 1)
                        k += 1

            def norm_transposes(n, which):
                t = 2 * n + which
                for s in range(S):
                    pe.wait_ge(xn_ready, S * t + s + 1)
                    for h in range(2):
                        for c in range(4):
                            last = nc.tensor.transpose(bank(2 * s + h, 4, P)[:, c, :],
                                                       xn[:, s, (4 * h + c) * P:(4 * h + c + 1) * P], mat("ident"))
                        last.then_inc(tr_mm, 1)

            pe.wait_ge(consts_in, 16 * 9)
            pe.wait_ge(cond_ready, 1)
            for n, l in enumerate(LAYERS):
                k0 = ada_base(n)

                def ada_slot(j, i=None):
                    arrive(k0 + j, i, RING)
                    dst = bank(j % 2, 4, S)
                    for m in range(4):
                        for c in range(DC):
                            last = nc.tensor.matmul(dst[:, m, :], slot(k0 + j)[:, c, m * P:(m + 1) * P], cond[:, c, :],
                                                    start=(c == 0), stop=(c == DC - 1))
                    last.then_inc(slot_done, 1)
                if n:
                    pe.wait_ge(h_ready, 8 * n)
                with pe.Fori(0, ADA_LOADS // RING) as i:
                    for j in range(RING):
                        pe.wait_ge(ada_ev, i * RING + (ADA_LOADS * n + j + 1))
                        ada_slot(j, i)
                pe.wait_ge(ada_ev, ADA_LOADS * (n + 1) + 2)
                for q in range(8):
                    w, s, h = q // 4, (q // 2) % 2, q % 2
                    if q >= 2:
                        pe.wait_ge(gate_ev, 8 * n + q - 1)
                    for c in range(4):
                        col = (3 * w + 2) * DC + 4 * h + c
                        last = nc.tensor.matmul(bank(q % 2, 4, P)[:, c, :], modt[:, col, s:s + 1].to_broadcast([P, P]),
                                                mat("ident"), start=True, stop=True)
                    last.then_inc(gate_mm, 1)
                pe.wait_ge(gate_ev, 8 * (n + 1))
                norm_transposes(n, 0)
                pe.wait_ge(at_act, S * (2 * n + 1))
                pe.wait_ge(at_dve, S * (2 * n + 1))
                k = mix_base(n)
                if l == 0:
                    def fourier_rows(u):
                        s, gp = divmod(u, 4)
                        if u >= 2:
                            pe.wait_ge(f1_ev, u - 1)
                        for gi in range(2):
                            last = nc.tensor.matmul(bank(u % 2, 2, 256)[:, gi, :], at[:, 2 * gp + gi, s * P:(s + 1) * P],
                                                    mats[:, MAT_AT["dft_c"]:MAT_AT["dft_c"] + 2, :].rearrange("p a b -> p (a b)"),
                                                    start=True, stop=True)
                        last.then_inc(f1_mm, 1)

                    def fourier_cols(u):
                        pe.wait_ge(f1_ev, u + 1)
                        if u >= 2:
                            pe.wait_ge(ft_ready, u - 1)
                        for gi in range(2):
                            dst = bank(2 + u % 2, 2, P)[:, gi, :]
                            src = f1[:, u % 2, :].rearrange("p (g x c) -> p g x c", g=2, x=2)
                            nc.tensor.matmul(dst, src[:, gi, 0, :], mat("seq_c"), start=True, stop=False)
                            last = nc.tensor.matmul(dst, src[:, gi, 1, :], mat("seq_ns"), start=False, stop=True)
                        last.then_inc(f2_mm, 1)
                    for u in range(9):
                        if u < 8:
                            fourier_rows(u)
                        if u >= 1:
                            fourier_cols(u - 1)
                    pe.wait_ge(ft_ready, 8)
                    out_proj(n, k, ft, 1)
                elif l == 1:
                    for j in range(4):
                        arrive(k)
                        for mh in range(2):
                            u = 2 * j + mh
                            if u >= 4:
                                pe.wait_ge(qk_ev, u - 3)
                            for m in range(2):
                                last = dense_chan(k, 2 * mh + m, bank(u % 4, 2, T)[:, m, :])
                            last.then_inc(slot_done if mh else qk_mm, 1)
                        k += 1
                    for j in range(2):
                        arrive(k)
                        for s in range(S):
                            b = 2 * j + s
                            pe.wait_ge(qk_ev, 5 + b)
                            last = dense_tok(k, s, ps[b][:, :])
                            last.then_inc(slot_done if s else v_mm, 1)
                        k += 1
                    for h in range(2):
                        for c in range(4):
                            last = nc.tensor.transpose(bank(4 + h, 4, P)[:, c, :], kT[:, 4 * h + c, 0:P], mat("ident"))
                        last.then_inc(kt_mm, 1)
                    pe.wait_ge(small_in[1], 48)
                    pe.wait_ge(kt_ev, 2)
                    pe.wait_ge(v_ev, 4)

                    def scores(u):
                        s, j = divmod(u, DC)
                        if u >= 2:
                            pe.wait_ge(e_ready, u - 1)
                        dst = psum[:, 2 * (u % 2):2 * (u % 2) + 2, :]
                        for hh in range(2):
                            r = slice(HD * hh, HD * (hh + 1))
                            last = nc.tensor.matmul(dst[:, hh, 0:P], qT[r, j, s * P:(s + 1) * P], kT[r, j, s * P:(s + 1) * P],
                                                    start=True, stop=True)
                            if s:
                                last = nc.tensor.matmul(dst[:, hh, P:2 * P], qT[r, j, P:2 * P], kcT[r, j, :], start=True, stop=True)
                        last.then_inc(s_mm, 1)

                    def prob_transposes(u):
                        s, j = divmod(u, DC)
                        pe.wait_ge(p_ready, u + 1)
                        if u >= 2:
                            pe.wait_ge(pt_ready, u - 1)
                        for b in range(2 * (1 + s)):
                            last = nc.tensor.transpose(bank(4 + u % 2, 4, P)[:, b, :],
                                                       prob[:, u % 2, b * P:(b + 1) * P], mat("ident"))
                        last.then_inc(t_mm, 1)

                    def weighted_values(u):
                        s, j = divmod(u, DC)
                        pe.wait_ge(pt_ready, u + 1)
                        if u >= 2:
                            pe.wait_ge(ot_ready, u - 1)
                        pT = probT[:, u % 2, :].rearrange("p (b q) -> p b q", b=4)
                        for hh in range(2):
                            cols = slice((2 * j + hh) * HD, (2 * j + hh + 1) * HD)
                            dst = ps[6 + u % 2][HD * hh:HD * (hh + 1), 0:P]
                            last = nc.tensor.matmul(dst, vtok[:, s, cols], pT[:, hh * (1 + s), :], start=True, stop=(s == 0))
                            if s:
                                last = nc.tensor.matmul(dst, vctx[:, 0, cols], pT[:, 2 * hh + 1, :], start=False, stop=True)
                        last.then_inc(av_mm, 1)
                    U = S * DC
                    for i in range(U + 2):
                        if i < U:
                            scores(i)
                        if 1 <= i <= U:
                            prob_transposes(i - 1)
                        if i >= 2:
                            weighted_values(i - 2)
                    pe.wait_ge(ot_ready, U)
                    out_proj(n, k, oT, 1)
                elif l == 2:
                    for j in range(8):
                        arrive(k)
                        for x in range(2):
                            u = 2 * j + x
                            if u >= 4:
                                pe.wait_ge(m_ev, u - 3)
                            if j < 4:
                                for m in range(2):
                                    last = dense_chan(k, 2 * x + m, bank(u % 4, 2, T)[:, m, :])
                            else:
                                last = dense_tok(k, x, ps[u % 4][:, :])
                            last.then_inc(slot_done if x else m_mm, 1)
                        k += 1
                    pe.wait_ge(small_in[2], 32)
                    pe.wait_ge(vn_ready, S)
                    for g in range(SG):
                        if g >= 4:
                            pe.wait_ge(sp_ev, g - 3)
                        for ci in range(2):
                            for s in range(S):
                                c = 2 * g + ci
                                last = nc.tensor.matmul(bank(g % 4, 2, T)[:, ci, s * P:(s + 1) * P],
                                                        vg[:, s, c * P:(c + 1) * P], wsT[:, g, :], start=True, stop=True)
                        last.then_inc(sp_mm, 1)
                    pe.wait_ge(sp_ev, SG)
                    out_proj(n, k, uT, 2)
                else:
                    for j in range(8):
                        arrive(k)
                        for x in range(2):
                            u = 2 * j + x
                            if u >= 4:
                                pe.wait_ge(x_cv, u - 3)
                            for m in range(2):
                                last = dense_chan(k, 2 * x + m, bank(u % 4, 2, T)[:, m, :])
                            last.then_inc(slot_done if x else x_mm, 1)
                        k += 1
                    arrive(k)
                    for s in range(S):
                        last = dense_tok(k, s, ps[4][:, s * 64:(s + 1) * 64], cols=64)
                    last.then_inc(slot_done, 1)
                    k += 1
                    for j in range(4):
                        arrive(k)
                        for s in range(S):
                            u = 2 * j + s
                            if u < 4:
                                pe.wait_ge(x_cv, 13 + u)
                            else:
                                pe.wait_ge(z_ev, u - 3)
                            last = dense_tok(k, s, ps[u % 4][:, :])
                            last.then_inc(slot_done if s else z_mm, 1)
                        k += 1
                    pe.wait_ge(adt_ready, 1)
                    cums = [(0, 0, "t_gt"), (0, 1, "t_lt"), (1, 0, "t_le"), (1, 1, "t_ge")]
                    for s, d, m in cums:
                        last = nc.tensor.matmul(ps[5][:, s * 64 + d * SH:s * 64 + (d + 1) * SH], mat(m),
                                                adt[:, s, d * SH:(d + 1) * SH], start=True, stop=True)
                    last.then_inc(cum_mm, 1)
                    pe.wait_ge(x_act, 16)
                    pe.wait_ge(z_ev, 8)
                    pe.wait_ge(edec_ready, 1)
                    tri = [mat("t_le"), mat("t_ge")]
                    for u in range(S * SG):
                        s, g = divmod(u, SG)
                        tok = slice(s * P, (s + 1) * P)
                        if u:
                            pe.wait_ge(xt_ev, u)
                        nc.tensor.transpose(ps[0][:, 0:P], xbcT[:, 2 * g, tok], mat("ident"))
                        nc.tensor.transpose(ps[0][:, P:2 * P], xbcT[:, 2 * g + 1, tok], mat("ident"))
                        nc.tensor.transpose(ps[0][:, 2 * P:3 * P], xbcT[:, 16 + g, tok], mat("ident"))
                        nc.tensor.matmul(ps[0][:, 3 * P:4 * P], xbcT[:, 16 + g, tok], xbcT[:, 24 + g, tok],
                                         start=True, stop=True).then_inc(xt_mm, 1)
                        for d in range(2):
                            pe.wait_ge(tt_ready, 2 * u + d + 1)
                            if u:
                                pe.wait_ge(seg_ready, 2 * (u - 1) + d + 1)
                            nc.tensor.matmul(ps[1 + d][:, :], mat("ones"), ttri[:, d, :], start=True, stop=False)
                            nc.tensor.matmul(bank(1 + d, HPG, P), tri[d],
                                             nadt[:, s, d * SH + g * HPG:d * SH + (g + 1) * HPG].unsqueeze(2).to_broadcast([P, HPG, P]),
                                             start=False, stop=True).then_inc(seg_mm, 1)
                        pe.wait_ge(m_ready, 2 * u + 2)
                        pe.wait_ge(dtx_ready, u + 1)
                        if u:
                            pe.wait_ge(y_done, u)
                        for h in range(HPG):
                            for d in range(2):
                                last = nc.tensor.matmul(ps[3][:, h * HD:(h + 1) * HD], segs[:, d, h * P:(h + 1) * P],
                                                        dtx[:, d, h * HD:(h + 1) * HD], start=(d == 0), stop=(d == 1))
                        if u:
                            pe.wait_ge(off_ev, min(u, SG))
                        if s == 0:
                            for d in range(2):
                                for hp in range(2):
                                    last = nc.tensor.matmul(bank(4, 4, P)[:, 2 * d + hp, :], dtxw[:, d, hp * P:(hp + 1) * P],
                                                            xtok[:, 2 * P:3 * P], start=True, stop=True)
                        else:
                            pe.wait_ge(h0_in, 16 * (g + 1))
                            last = nc.tensor.matmul(ps[4][:, :], xbcT[:, 24 + g, tok], h0[:, 0, :], start=True, stop=True)
                        last.then_inc(yg_mm, 1)
                    pe.wait_ge(y_done, S * SG)
                    for s in range(S):
                        pe.wait_ge(yn_ready, s + 1)
                        for q in range(4):
                            u = 4 * s + q
                            if u >= 4:
                                pe.wait_ge(yt_ev, u - 3)
                            for c in range(4):
                                last = nc.tensor.transpose(bank(u % 4, 4, P)[:, c, :], zs[:, s, (4 * q + c) * P:(4 * q + c + 1) * P],
                                                           mat("ident"))
                            last.then_inc(yt_mm, 1)
                    pe.wait_ge(yt_ev, 8)
                    out_proj(n, k, xbcT, 2)
                norm_transposes(n, 1)
                pe.wait_ge(at_act, S * (2 * n + 2))
                pe.wait_ge(at_dve, S * (2 * n + 2))
                for s in range(S):
                    for c in range(DC):
                        last = nc.tensor.matmul(bank(4, S, NR)[:, s, :], at[:, c, s * P:(s + 1) * P], wr[:, l, c, :],
                                                start=(c == 0), stop=(c == DC - 1))
                last.then_inc(route_mm, 1)
                k = moe_base(n)
                with pe.Fori(0, E // XU) as i:
                    for x in range(XU):
                        x0 = E * n + x
                        for w in range(2):
                            kk = k + 3 * x + w
                            arrive(kk, i, 3 * XU)
                            for h in range(2):
                                pe.wait_ge(act_ready, i * (2 * XU) + (2 * x0 + h + 1))
                                for m in range(2):
                                    last = dense_chan(kk, 2 * h + m, bank(2 * w + h, 2, T)[:, m, :])
                                last.then_inc(slot_done if h else g_mm, 1)
                        kk = k + 3 * x + 2
                        arrive(kk, i, 3 * XU)
                        pe.wait_ge(act_ready, i * (2 * XU) + (2 * x0 + 4))
                        for s in range(S):
                            for j in range(2):
                                b = 2 * s + j
                                pe.wait_ge(y_ev, i * (4 * XU) + (4 * x0 + b + 1))
                                for c in range(FF // P):
                                    last = nc.tensor.matmul(ps[4 + b][:, :], actT[:, c, s * P:(s + 1) * P],
                                                            slot_down(kk)[:, c, j * SLOT_COLS:(j + 1) * SLOT_COLS],
                                                            start=(c == 0), stop=(c == FF // P - 1))
                                last.then_inc(slot_done if b == 3 else y_mm, 1)

        @block.scalar
        def _(act):
            A = nc.scalar.activation
            act.wait_ge(consts_in, 16 * 9)
            A(cond[:, :, :], vec("cond").rearrange("p (c s) -> p c s", s=S), ACT.Silu).then_inc(cond_ready, 1)

            def norm(n, which):
                t = 2 * n + which
                if t:
                    act.wait_ge(h_ready, 4 * t)
                for s in range(S):
                    A(acc[:, s, :], hid[:, s, :], ACT.Square, accum_out=stat[:, s:s + 1]).then_inc(sq_done, 1)
                for s in range(S):
                    act.wait_ge(var_ready, S * t + s + 1)
                    A(stat[:, 4 + s:5 + s], stat[:, 2 + s:3 + s], ACT.Sqrt).then_inc(rstd_ready, 1)
                if n == len(LAYERS):
                    return
                act.wait_ge(gsc_ready, n + 1)
                for s in range(S):
                    act.wait_ge(tr_mm, 4 * t + 2 * s + 1)
                    for c in range(4):
                        last = A(at[:, c, s * P:(s + 1) * P], bank(2 * s, 4, P)[:, c, :], ACT.Identity,
                                 scale=gsc[:, which, c, s:s + 1], bias=modt[:, 3 * which * DC + c, s:s + 1])
                    last.then_inc(at_act, 1)

            for n, l in enumerate(LAYERS):
                for q in range(8):
                    w, s, h = q // 4, (q // 2) % 2, q % 2
                    act.wait_ge(gate_mm, 8 * n + q + 1)
                    A(gate[:, w, s, h * 512:(h + 1) * 512], ps[q % 2][:, :], ACT.Copy).then_inc(gate_ev, 1)
                norm(n, 0)
                k = mix_base(n)
                if l == 0:
                    for u in range(8):
                        act.wait_ge(f1_mm, u + 1)
                        if u >= 2:
                            act.wait_ge(f2_mm, u - 1)
                        A(f1[:, u % 2, :], ps[u % 2][:, :], ACT.Copy).then_inc(f1_ev, 1)
                elif l == 1:
                    for u in range(8):
                        j, mh = divmod(u, 2)
                        if mh:
                            act.wait_ge(slot_done, k + j + 1)
                        else:
                            act.wait_ge(qk_mm, j + 1)
                        if u < 4:
                            A(qT[:, 2 * u:2 * u + 2, :], bank(u % 4, 2, T), ACT.Copy, scale=HD ** -0.5).then_inc(qk_ev, 1)
                        else:
                            A(kT[:, 2 * u - 8:2 * u - 6, :], bank(u % 4, 2, T), ACT.Copy).then_inc(qk_ev, 1)
                    U = S * DC
                    for i in range(U + 1):
                        if i < U:
                            w = P * (1 + i // DC)
                            act.wait_ge(nm_ready, i + 1)
                            if i >= 2:
                                act.wait_ge(t_mm, i - 1)
                            for hh in range(2):
                                last = A(prob[:, i % 2, hh * w:(hh + 1) * w], ps[2 * (i % 2) + hh][:, 0:w], ACT.Exp,
                                         bias=nmax[:, i, hh:hh + 1], accum_out=esum[:, i, hh:hh + 1])
                            last.then_inc(e_ready, 1)
                        if i >= 1:
                            v = i - 1
                            act.wait_ge(t_mm, v + 1)
                            if v >= 2:
                                act.wait_ge(av_mm, v - 1)
                            w = 2 * P * (1 + v // DC)
                            A(probT[:, v % 2, 0:w], ps[4 + v % 2][:, 0:w], ACT.Copy).then_inc(pt_ready, 1)
                elif l == 2:
                    for u in range(16):
                        j, x = divmod(u, 2)
                        if x:
                            act.wait_ge(slot_done, k + j + 1)
                        else:
                            act.wait_ge(m_mm, j + 1)
                        if j < 4:
                            A(uT[:, 2 * u:2 * u + 2, :], bank(u % 4, 2, T), ACT.Gelu_apprx_tanh).then_inc(m_ev, 1)
                        else:
                            A(vg[:, x, (j - 4) * 512:(j - 3) * 512], ps[u % 4][:, :], ACT.Gelu_apprx_tanh).then_inc(m_ev, 1)
                    act.wait_ge(m_ev, 16)
                    for s in range(S):
                        A(acc[:, :, :].rearrange("p a b -> p (a b)"), vg[:, s, :], ACT.Square,
                          accum_out=stat[:, 6 + s:7 + s]).then_inc(vsq, 1)
                        act.wait_ge(vsq, s + 1)
                    for s in range(S):
                        act.wait_ge(vvar, s + 1)
                        A(stat[:, 10 + s:11 + s], stat[:, 8 + s:9 + s], ACT.Sqrt).then_inc(vrstd, 1)
                else:
                    cw, cb = vec("conv_w"), vec("conv_b")
                    for u in range(17):
                        if u < 16:
                            j, x = divmod(u, 2)
                            if x:
                                act.wait_ge(slot_done, k + j + 1)
                            else:
                                act.wait_ge(x_mm, j + 1)
                            for m in range(2):
                                c = 2 * u + m
                                last = A(xbcT[:, c, :], bank(u % 4, 2, T)[:, m, :], ACT.Identity,
                                         scale=cw[:, 64 + c:65 + c], bias=cb[:, c:c + 1])
                            last.then_inc(x_b, 1)
                        if u:
                            act.wait_ge(x_cv, u)
                            A(xbcT[:, 2 * u - 2:2 * u, :], xbcT[:, 2 * u - 2:2 * u, :], ACT.Silu).then_inc(x_act, 1)
                    act.wait_ge(small_in[3], 48)
                    A(dtb[:, 1, :], dtb[:, 1, :], ACT.Exp).then_inc(a_exp, 1)
                    act.wait_ge(dt_abs, 1)
                    A(dtw[:, 2, :], dtw[:, 1, :], ACT.Exp).then_inc(dt_exp, 1)
                    act.wait_ge(dt_abs, 2)
                    A(dtw[:, 4, :], dtw[:, 3, :], ACT.Ln).then_inc(dt_ln, 1)
                    for u in range(8):
                        j, s = divmod(u, 2)
                        if s:
                            act.wait_ge(slot_done, k + 9 + j + 1)
                        else:
                            act.wait_ge(z_mm, j + 1)
                        A(zs[:, s, j * 512:(j + 1) * 512], ps[u % 4][:, :], ACT.Silu).then_inc(z_ev, 1)
                    act.wait_ge(cum_mm, 1)
                    A(edec[:, :, :], bank(5, 2, 64), ACT.Exp).then_inc(edec_ready, 1)
                    for u in range(S * SG):
                        for d in range(2):
                            act.wait_ge(seg_ready, 2 * u + d + 1)
                            A(segs[:, d, :], segs[:, d, :], ACT.Exp).then_inc(dec_ready, 1)
                        if u < SG:
                            act.wait_ge(yg_mm, u + 1)
                            if u:
                                act.wait_ge(st_out, 32 * u)
                            A(stout[:, 0, :], ps[4][:, :], ACT.Copy).then_inc(off_ev, 1)
                    for s in range(S):
                        act.wait_ge(y_done, SG * (s + 1))
                        if s:
                            act.wait_ge(ysq, 1)
                        A(xn[:, :, :].rearrange("p a b -> p (a b)"), zs[:, s, :], ACT.Square,
                          accum_out=stat[:, 12 + s:13 + s]).then_inc(ysq, 1)
                    for s in range(S):
                        act.wait_ge(yvar, s + 1)
                        A(stat[:, 16 + s:17 + s], stat[:, 14 + s:15 + s], ACT.Sqrt).then_inc(yrstd, 1)
                    gn = vec("gn")
                    for u in range(8):
                        s, q = divmod(u, 4)
                        act.wait_ge(yt_mm, u + 1)
                        for c in range(4):
                            last = A(xbcT[:, 4 * q + c, s * P:(s + 1) * P], bank(u % 4, 4, P)[:, c, :], ACT.Identity,
                                     scale=gn[:, 4 * q + c:4 * q + c + 1])
                        last.then_inc(yt_ev, 1)
                norm(n, 1)
                for r in range(2):
                    act.wait_ge(rexp_in, 2 * n + r + 1)
                    A(rt[:, 2 + 5 * r, :, :], rt[:, 1 + 5 * r, :, :], ACT.Exp).then_inc(rexp, 1)
                k = moe_base(n)
                with act.Fori(0, E // XU) as i:
                    for x in range(XU):
                        x0 = E * n + x
                        for h in range(2):
                            if h:
                                act.wait_ge(slot_done, i * (3 * XU) + (k + 3 * x + 1))
                            else:
                                act.wait_ge(g_mm, i * (2 * XU) + (2 * x0 + 1))
                            act.wait_ge(act_ready, i * (2 * XU) + (2 * x0 + h + 1))
                            A(sgl[:, 2 * h:2 * h + 2, :], bank(h, 2, T), ACT.Silu).then_inc(sg_ready, 1)
            norm(len(LAYERS), 0)

        @block.vector
        def _(dve):
            V = nc.vector
            count = [0]

            def link(ins):
                count[0] += 1
                ins.then_inc(dve_chain, 1)
                dve.wait_ge(dve_chain, count[0])

            V.memset(stat[:, 24:25], 0.0).then_inc(ada_ev, 2)
            V.memset(stat[:, 25:26], 0.0).then_inc(act_ready, 2)
            V.memset(stat[:, 26:27], 0.0).then_inc(y_ev, 4)
            dve.wait_ge(consts_in, 16 * 9)
            dve.wait_ge(pool_chain, EG)

            def root_input(col_in, col_out, width, signal):
                link(V.tensor_scalar(stat[:, col_out:col_out + 1], stat[:, col_in:col_in + 1], 1.0 / width, EPS, ALU.mult, ALU.add))
                V.reciprocal(stat[:, col_out:col_out + 1], stat[:, col_out:col_out + 1]).then_inc(signal, 1)

            def norm(n, which):
                t = 2 * n + which
                for s in range(S):
                    dve.wait_ge(sq_done, S * t + s + 1)
                    root_input(s, 2 + s, D, var_ready)
                if t:
                    dve.wait_ge(h_ready, 4 * t)
                for s in range(S):
                    dve.wait_ge(rstd_ready, S * t + s + 1)
                    if n == len(LAYERS):
                        link(V.tensor_scalar(xn[:, s, :], hid[:, s, :], stat[:, 4 + s:5 + s], None, ALU.mult))
                        V.tensor_tensor(xn[:, s, :], xn[:, s, :], finalg[:, :], ALU.mult).then_inc(fin_ready, 1)
                    else:
                        V.tensor_scalar(xn[:, s, :], hid[:, s, :], stat[:, 4 + s:5 + s], None, ALU.mult).then_inc(xn_ready, 1)
                if n == len(LAYERS):
                    return
                for s in range(S):
                    dve.wait_ge(tr_mm, 4 * t + 2 * s + 2)
                    for c in range(4, DC):
                        last = V.tensor_scalar(at[:, c, s * P:(s + 1) * P], bank(2 * s + 1, 4, P)[:, c - 4, :],
                                               gsc[:, which, c, s:s + 1], modt[:, 3 * which * DC + c, s:s + 1], ALU.mult, ALU.add)
                    last.then_inc(at_dve, 1)

            def add_mixer(n, k_last):
                for j in range(2):
                    for s in range(S):
                        if s:
                            dve.wait_ge(slot_done, k_last[j] + 1)
                        else:
                            dve.wait_ge(o_mm, 2 * n + j + 1)
                        cols = slice(j * 512, (j + 1) * 512)
                        link(V.tensor_tensor(outtmp[:, s, :], ps[4 + 2 * j + s][:, :], gate[:, 0, s, cols], ALU.mult))
                        V.tensor_tensor(hid[:, s, cols], hid[:, s, cols], outtmp[:, s, :], ALU.add).then_inc(h_ready, 1)

            def first_of_max(vals, m, tmp, onehot):
                link(V.tensor_tensor(tmp, vals, m.to_broadcast([P, S, EG]), ALU.is_equal))
                link(V.tensor_tensor(tmp, tmp, first[:, :].unsqueeze(1).to_broadcast([P, S, EG]), ALU.mult))
                link(V.tensor_reduce(m, tmp, AX.X, ALU.max))
                link(V.tensor_tensor(onehot, tmp, m.to_broadcast([P, S, EG]), ALU.is_equal))

            def route(n, l):
                R = lambda q: rt[:, q, :, :]
                one = lambda q: rt[:, 16 + q, :, 0:1]
                dve.wait_ge(route_mm, n + 1)
                link(V.tensor_tensor(rlog[:, :, :], bank(4, S, NR), rbias[:, l, :].unsqueeze(1).to_broadcast([P, S, NR]), ALU.add))
                gl = rlog[:, :, 0:EG]
                link(V.tensor_reduce(one(0), gl, AX.X, ALU.max))
                V.tensor_tensor(R(1), gl, one(0).to_broadcast([P, S, EG]), ALU.subtract).then_inc(rexp_in, 1)
                first_of_max(gl, one(0), R(3), R(4))
                dve.wait_ge(rexp, 2 * n + 1)
                link(V.tensor_reduce(one(1), R(2), AX.X, ALU.add))
                link(V.reciprocal(one(1), one(1)))
                link(V.tensor_tensor(rsel[:, :, :, :], rlog[:, :, EG:NR].rearrange("p s (g e) -> p s g e", g=EG),
                                     R(4).unsqueeze(3).to_broadcast([P, S, EG, EG]), ALU.mult))
                link(V.tensor_reduce(R(5), rsel[:, :, :, :].rearrange("p s g e -> p s e g"), AX.X, ALU.add))
                link(V.tensor_reduce(one(2), R(5), AX.X, ALU.max))
                V.tensor_tensor(R(6), R(5), one(2).to_broadcast([P, S, EG]), ALU.subtract).then_inc(rexp_in, 1)
                dve.wait_ge(rexp, 2 * n + 2)
                link(V.tensor_reduce(one(3), R(7), AX.X, ALU.max))
                first_of_max(R(7), one(3), R(8), R(9))
                link(V.scalar_tensor_tensor(R(10), R(9), -4.0, R(7), ALU.mult, ALU.add))
                link(V.tensor_reduce(one(4), R(10), AX.X, ALU.max))
                first_of_max(R(10), one(4), R(8), R(11))
                link(V.tensor_tensor(R(12), R(9), R(11), ALU.add))
                link(V.tensor_tensor(R(12), R(12), R(7), ALU.mult))
                link(V.tensor_reduce(one(5), R(12), AX.X, ALU.add))
                link(V.reciprocal(one(5), one(5)))
                link(V.tensor_tensor(one(5), one(5), one(1), ALU.mult))
                link(V.tensor_tensor(R(12), R(12), one(5).to_broadcast([P, S, EG]), ALU.mult))
                link(V.tensor_tensor(comb[:, :, :].rearrange("p s (g e) -> p s g e", g=EG),
                                     R(4).unsqueeze(3).to_broadcast([P, S, EG, EG]),
                                     R(12).unsqueeze(2).to_broadcast([P, S, EG, EG]), ALU.mult))

            for n, l in enumerate(LAYERS):
                k0 = ada_base(n)
                ab = vec("ada_b")
                with dve.Fori(0, ADA_LOADS // RING) as i:
                    for j in range(RING):
                        dve.wait_ge(slot_done, i * RING + (k0 + j + 1))
                        V.tensor_tensor(
                            modt[:, bass.ds(i * (RING * 4) + 4 * j, 4), :], bank(j % 2, 4, S),
                            ab[:, bass.ds(i * (RING * 4) + (l * NMOD * DC + 4 * j), 4)].unsqueeze(2).to_broadcast([P, 4, S]),
                            ALU.add).then_inc(ada_ev, 1)
                dve.wait_ge(ada_ev, ADA_LOADS * (n + 1) + 2)
                for w in range(2):
                    g = vec("g1" if w == 0 else "g2")[:, l * DC:(l + 1) * DC]
                    last = V.scalar_tensor_tensor(gsc[:, w, :, :], modt[:, (3 * w + 1) * DC:(3 * w + 2) * DC, :], 1.0,
                                                  g.unsqueeze(2).to_broadcast([P, DC, S]), ALU.add, ALU.mult)
                last.then_inc(gsc_ready, 1)
                dve.wait_ge(gsc_ready, n + 1)
                norm(n, 0)
                k = mix_base(n)
                if l == 0:
                    for u in range(8):
                        s, gp = divmod(u, 4)
                        dve.wait_ge(f2_mm, u + 1)
                        V.tensor_copy(ft[:, 2 * gp:2 * gp + 2, s * P:(s + 1) * P], bank(2 + u % 2, 2, P)).then_inc(ft_ready, 1)
                    add_mixer(n, [k, k + 1])
                elif l == 1:
                    dve.wait_ge(small_in[1], 48)
                    link(V.tensor_tensor(rpb, rpb, mat("na_mask").unsqueeze(1).to_broadcast([P, HEADS, P]), ALU.add))
                    for j in range(2):
                        for s in range(S):
                            if s:
                                dve.wait_ge(slot_done, k + 4 + j + 1)
                            else:
                                dve.wait_ge(v_mm, j + 1)
                            V.tensor_copy(vtok[:, s, j * 512:(j + 1) * 512], ps[2 * j + s][:, :]).then_inc(v_ev, 1)
                    for h in range(2):
                        dve.wait_ge(kt_mm, h + 1)
                        V.tensor_copy(xn[:, 0, h * 512:(h + 1) * 512], ps[4 + h][:, :]).then_inc(kt_ev, 1)
                    U = S * DC
                    for i in range(U + 2):
                        if i < U:
                            s, j = divmod(i, DC)
                            dve.wait_ge(s_mm, i + 1)
                            sc = psum[:, 2 * (i % 2):2 * (i % 2) + 2, 0:P * (1 + s)]
                            if s:
                                link(V.tensor_tensor(sc[:, :, 0:P], sc[:, :, 0:P], rpb[:, 2 * j:2 * j + 2, :], ALU.add))
                            V.tensor_reduce(nmax[:, i, :], sc, AX.X, ALU.max, negate=True).then_inc(nm_ready, 1)
                        if 1 <= i <= U:
                            v = i - 1
                            w = P * (1 + v // DC)
                            dve.wait_ge(e_ready, v + 1)
                            link(V.reciprocal(rsum[:, v, :], esum[:, v, :]))
                            pr = prob[:, v % 2, 0:2 * w].rearrange("p (h k) -> p h k", h=2)
                            V.tensor_tensor(pr, pr, rsum[:, v, :].unsqueeze(2).to_broadcast([P, 2, w]), ALU.mult).then_inc(p_ready, 1)
                        if i >= 2:
                            v = i - 2
                            s, j = divmod(v, DC)
                            dve.wait_ge(av_mm, v + 1)
                            V.tensor_copy(oT[:, j, s * P:(s + 1) * P], ps[6 + v % 2][:, 0:P]).then_inc(ot_ready, 1)
                    add_mixer(n, [k + 6, k + 7])
                    dve.wait_ge(kv_out, 32)
                elif l == 2:
                    for s in range(S):
                        dve.wait_ge(vsq, s + 1)
                        root_input(6 + s, 8 + s, GDFF, vvar)
                    for s in range(S):
                        dve.wait_ge(vrstd, s + 1)
                        V.tensor_scalar(vg[:, s, :], vg[:, s, :], stat[:, 10 + s:11 + s], None, ALU.mult).then_inc(vn_ready, 1)
                    dve.wait_ge(small_in[2], 32)
                    gv = vec("gv")
                    for g in range(SG):
                        dve.wait_ge(sp_mm, g + 1)
                        for ci in range(2):
                            c = 2 * g + ci
                            link(V.scalar_tensor_tensor(
                                gt[:, ci, :].rearrange("p (s t) -> p s t", s=S),
                                bank(g % 4, 2, T)[:, ci, :].rearrange("p (s t) -> p s t", s=S), gv[:, c:c + 1],
                                bs[:, g, :].unsqueeze(1).to_broadcast([P, S, P]), ALU.mult, ALU.add))
                            last = V.tensor_tensor(uT[:, c, :], uT[:, c, :], gt[:, ci, :], ALU.mult)
                        last.then_inc(sp_ev, 1)
                    add_mixer(n, [k + 9, k + 11])
                else:
                    cw = vec("conv_w")
                    for u in range(16):
                        dve.wait_ge(x_b, u + 1)
                        for tap, (o0, i0, w) in ((0, (2, 0, P - 2)), (1, (1, 0, P - 1)), (3, (0, 1, P - 1))):
                            for m in range(2):
                                c = 2 * u + m
                                x = xbcT[:, c, :].rearrange("p (s t) -> p s t", s=S)
                                src = bank(u % 4, 2, T)[:, m, :].rearrange("p (s t) -> p s t", s=S)
                                last = V.scalar_tensor_tensor(x[:, :, o0:o0 + w], src[:, :, i0:i0 + w], cw[:, tap * 32 + c:tap * 32 + c + 1],
                                                              x[:, :, o0:o0 + w], ALU.mult, ALU.add)
                                if tap < 3:
                                    link(last)
                        last.then_inc(x_cv, 1)
                    dve.wait_ge(slot_done, k + 9)
                    dve.wait_ge(small_in[3], 48)
                    W = lambda q: dtw[:, q, :]
                    W2 = lambda q: dtw[:, q, :].rearrange("p (s h) -> p s h", s=S)
                    both = lambda r: dtb[:, r, :].unsqueeze(1).to_broadcast([P, S, 64])
                    link(V.tensor_tensor(W2(0), bank(4, S, 64), both(0), ALU.add))
                    V.scalar_tensor_tensor(W(1), W(0), -1.0, W(0), ALU.mult, ALU.min).then_inc(dt_abs, 1)
                    dve.wait_ge(dt_exp, 1)
                    V.tensor_scalar(W(3), W(2), 1.0, None, ALU.add).then_inc(dt_abs, 1)
                    dve.wait_ge(dt_abs, 2)
                    link(V.tensor_scalar(W(5), W(3), -1.0, None, ALU.add))
                    link(V.tensor_scalar(W(6), W(5), 0.0, None, ALU.is_equal))
                    link(V.tensor_tensor(W(5), W(5), W(6), ALU.add))
                    link(V.reciprocal(W(5), W(5)))
                    dve.wait_ge(dt_ln, 1)
                    link(V.tensor_tensor(W(4), W(4), W(6), ALU.add))
                    link(V.tensor_tensor(W(4), W(4), W(5), ALU.mult))
                    link(V.tensor_tensor(W(4), W(4), W(2), ALU.mult))
                    link(V.scalar_tensor_tensor(W(7), W(0), 0.0, W(4), ALU.max, ALU.add))
                    dve.wait_ge(a_exp, 1)
                    link(V.tensor_tensor(nadt[:, :, :], W2(7), both(1), ALU.mult))
                    V.tensor_scalar(adt[:, :, :], nadt[:, :, :], -1.0, None, ALU.mult).then_inc(adt_ready, 1)
                    dve.wait_ge(z_ev, 8)
                    dve.wait_ge(edec_ready, 1)
                    tri = [mat("t_le"), mat("t_ge")]
                    heads = lambda x: x.rearrange("p (h e) -> p h e", h=HPG)
                    for u in range(S * SG):
                        s, g = divmod(u, SG)
                        hs = [slice(d * SH + g * HPG, d * SH + (g + 1) * HPG) for d in range(2)]
                        over = lambda x: x.unsqueeze(2).to_broadcast([P, HPG, HD])
                        dve.wait_ge(xt_mm, u + 1)
                        if u:
                            dve.wait_ge(yg_mm, u)
                        V.tensor_copy(xtok[:, :], ps[0][:, :]).then_inc(xt_ev, 1)
                        dve.wait_ge(xt_ev, u + 1)
                        for d in range(2):
                            V.tensor_tensor(cbm[:, d, :], xtok[:, 384:512], tri[d], ALU.mult)
                            last = V.tensor_tensor(heads(dtx[:, d, :]), heads(xtok[:, 0:256]), over(W2(7)[:, s, hs[d]]), ALU.mult)
                            if s == 0:
                                link(last)
                                last = V.tensor_tensor(heads(dtxw[:, d, :]), heads(dtx[:, d, :]), over(edec[:, 0, hs[d]]), ALU.mult)
                        last.then_inc(dtx_ready, 1)
                        for d in range(2):
                            dve.wait_ge(seg_mm, 2 * u + d + 1)
                            V.tensor_scalar(segs[:, d, :], ps[1 + d][:, :], 0.0, None, ALU.min).then_inc(seg_ready, 1)
                        dve.wait_ge(dtx_ready, u + 1)
                        link(V.tensor_tensor(heads(yfix[:, 0, :]), heads(xtok[:, 0:256]), over(dtb[:, 2, g * HPG:(g + 1) * HPG]), ALU.mult))
                        for d in range(2):
                            dve.wait_ge(dec_ready, 2 * u + d + 1)
                            V.tensor_tensor(heads(segs[:, d, :]), heads(segs[:, d, :]), cbm[:, d, :].unsqueeze(1).to_broadcast([P, HPG, P]),
                                            ALU.mult).then_inc(m_ready, 1)
                        dve.wait_ge(yg_mm, u + 1)
                        link(V.tensor_tensor(yfix[:, 0, :], yfix[:, 0, :], ps[3][:, 0:256], ALU.add))
                        if s == 1:
                            for d in range(2):
                                cols = slice(d * 256, (d + 1) * 256)
                                link(V.tensor_tensor(heads(offs[:, 0, cols]), heads(ps[4][:, cols]), over(edec[:, 1, hs[d]]), ALU.mult))
                                link(V.tensor_tensor(yfix[:, 0, :], yfix[:, 0, :], offs[:, 0, cols], ALU.add))
                        zg = zs[:, s, g * 256:(g + 1) * 256]
                        V.tensor_tensor(zg, zg, yfix[:, 0, :], ALU.mult).then_inc(y_done, 1)
                    for s in range(S):
                        dve.wait_ge(ysq, s + 1)
                        root_input(12 + s, 14 + s, 2 * D, yvar)
                    dve.wait_ge(y_done, S * SG)
                    for s in range(S):
                        dve.wait_ge(yrstd, s + 1)
                        V.tensor_scalar(zs[:, s, :], zs[:, s, :], stat[:, 16 + s:17 + s], None, ALU.mult).then_inc(yn_ready, 1)
                    add_mixer(n, [k + 14, k + 16])
                norm(n, 1)
                link(V.memset(acc[:, :, :], 0.0))
                route(n, l)
                k = moe_base(n)
                with dve.Fori(0, E // XU) as i:
                    for x in range(XU):
                        x0 = E * n + x
                        for h in range(2):
                            dve.wait_ge(sg_ready, i * (2 * XU) + (2 * x0 + h + 1))
                            if h:
                                dve.wait_ge(slot_done, i * (3 * XU) + (k + 3 * x + 2))
                            else:
                                dve.wait_ge(g_mm, i * (2 * XU) + (2 * x0 + 2))
                            V.tensor_tensor(actT[:, 2 * h:2 * h + 2, :], sgl[:, 2 * h:2 * h + 2, :], bank(2 + h, 2, T),
                                            ALU.mult).then_inc(act_ready, 1)
                        for b in range(4):
                            s, j = divmod(b, 2)
                            if b == 3:
                                dve.wait_ge(slot_done, i * (3 * XU) + (k + 3 * x + 3))
                            else:
                                dve.wait_ge(y_mm, i * (3 * XU) + (3 * x0 + b + 1))
                            dve.wait_ge(y_ev, i * (4 * XU) + (4 * x0 + b + 1))
                            part = acc[:, s, j * 512:(j + 1) * 512]
                            V.scalar_tensor_tensor(part, ps[4 + b][:, :], comb[:, s, bass.ds(i * XU + x, 1)], part,
                                                   ALU.mult, ALU.add).then_inc(y_ev, 1)
                dve.wait_ge(y_ev, 4 * E * (n + 1) + 4)
                for s in range(S):
                    for j in range(2):
                        cols = slice(j * 512, (j + 1) * 512)
                        link(V.tensor_tensor(outtmp[:, j, :], acc[:, s, cols], gate[:, 1, s, cols], ALU.mult))
                        V.tensor_tensor(hid[:, s, cols], hid[:, s, cols], outtmp[:, j, :], ALU.add).then_inc(h_ready, 1)
                dve.wait_ge(h_ready, 8 * (n + 1))
            norm(len(LAYERS), 0)


_AS_GIVEN = ["x_prompt", "x_sample", "cache_v", "ada_w", "final_g", "fnet_w_o", "na_w_qkv", "na_w_o",
             "gmlp_w_in", "gmlp_b_s", "gmlp_w_out", "ssd_w_in", "ssd_a_log", "ssd_dt_bias", "ssd_d_skip", "ssd_w_out",
             "moe_b_gr", "moe_b_er", "moe_w_gate", "moe_w_up", "moe_w_down"]
_OUTS = [("y_prompt", (1, P, D)), ("y_sample", (1, P, D)),
         ("new_cache_k", (1, 1, HEADS, P, HD)), ("new_cache_v", (1, 1, HEADS, P, HD)),
         ("new_state_ssm_fwd", (1, 1, SH, HD, P)), ("new_state_ssm_bwd", (1, 1, SH, HD, P))]


def constant_matrices():
    i = np.arange(P)
    r, c = i[:, None], i[None, :]
    angle = 2 * np.pi * ((r * c) % P) / P
    grid_w, win = 64, 16
    qc, kc = r % grid_w, c % grid_w
    w0 = np.clip(qc - win // 2, 0, grid_w - win)
    m = {"ident": r == c, "ones": r >= 0 * c, "t_le": r <= c, "t_ge": r >= c, "t_gt": r > c, "t_lt": r < c,
         "dft_c": np.cos(angle), "dft_s": np.sin(angle), "seq_c": np.cos(angle) / P, "seq_ns": -np.sin(angle) / P,
         "na_mask": np.where((kc >= w0) & (kc < w0 + win), 0.0, -1e30)}
    return np.ascontiguousarray(np.stack([np.broadcast_to(m[k], (P, P)).astype(np.float32) for k in MATS], 1))


def columns(x):
    return np.asarray(x).reshape(-1, P).T


def lay_out(x):
    x = {k: np.asarray(v) for k, v in x.items()}
    arrays = {k: np.ascontiguousarray(x[k]) for k in _AS_GIVEN}
    cond = np.stack([x["c_ctx"].reshape(DC, P), x["c"][0].reshape(DC, P)], 1)
    packed = {"g1": columns(x["norm1_g"]), "g2": columns(x["norm2_g"]), "ada_b": columns(x["ada_b"]),
              "cond": columns(cond), "gv": columns(x["gmlp_g_v"]), "gn": columns(x["ssd_g_norm"]),
              "conv_w": columns(x["ssd_conv_w"]), "conv_b": columns(x["ssd_conv_b"])}
    arrays["vecs"] = np.ascontiguousarray(np.concatenate([packed[k] for k, _ in VECS], 1))
    arrays["mats"] = constant_matrices()
    arrays["wgr"] = np.ascontiguousarray(x["moe_w_gr"].reshape(DEPTH, DC, P, EG).transpose(2, 0, 1, 3))
    arrays["wer"] = np.ascontiguousarray(x["moe_w_er"].reshape(DEPTH, DC, P, E).transpose(2, 0, 1, 3))
    i = np.arange(P)
    rr = (i[None, :] // 64) - (i[:, None] // 64) + 7
    cc = np.clip((i[None, :] % 64) - (i[:, None] % 64), -15, 15) + 15
    arrays["rpb_band"] = np.ascontiguousarray(x["na_rpb"][0][:, rr, cc].transpose(1, 0, 2))
    arrays["cache_kT"] = np.ascontiguousarray(x["cache_k"][0, 0].reshape(DC, 2, P, HD).transpose(1, 3, 0, 2).reshape(P, DC, P))
    arrays["wsT"] = np.ascontiguousarray(x["gmlp_w_s"][0].transpose(2, 0, 1))
    arrays["h0T"] = np.ascontiguousarray(
        np.stack([x["state_ssm_fwd"][0, 0].reshape(2 * D, P).T, x["state_ssm_bwd"][0, 0].reshape(2 * D, P).T], 1))
    return arrays


def kernel(**inputs):
    import concourse.bacc as _bacc
    from concourse.bass_utils import run_bass_kernel_spmd as _run

    nc = _bacc.Bacc("TRN2", target_bir_lowering=False, num_devices=1)
    given = lay_out(inputs)
    arrays = {f"in_{k}": v for k, v in given.items()}
    a = {k: nc.dram_tensor(f"in_{k}", v.shape, mybir.dt.from_np(v.dtype), kind="ExternalInput").ap() for k, v in given.items()}
    o = {k: nc.dram_tensor(f"out_{k}", shape, FP32, kind="ExternalOutput").ap() for k, shape in _OUTS}
    build(nc, a, o)
    r = _run(nc, [arrays], core_ids=[0])
    return tuple(r.results[0][f"out_{k}"] for k, _ in _OUTS)
```

```python
import numpy as np
import concourse.bass as bass
from concourse import mybir
from contextlib import ExitStack

FP32 = mybir.dt.float32
ALU = mybir.AluOpType
ACT = mybir.ActivationFunctionType
AX = mybir.AxisListType

P = 128
D = 1024
DC = D // P
S = 2
T = S * P
DEPTH = 4
EPS = 1e-6
RING = 4
SLOT_COLS = 512
NMOD = 6
HEADS = 16
HD = 64
E = 16
EG = 4
FF = 512
NR = EG + E
GDFF = 2048
SG = 8
HPG = 4
SH = 32
XBC = 4096
ARENA = 15616
LAYERS = (0, 1, 2, 3)

XG = E // EG
ADA_LOADS = NMOD * D // SLOT_COLS
MIX_LOADS = {0: 2, 1: 8, 2: 12, 3: 17}
MOE_LOADS = 3 * E
PLAIN = ["G0", "U0", "G1", "U1", "D0", "G2", "U2", "D1", "G3", "U3", "D2", "D3"]
MIXED = ["G0", "U0", "G1", "U1", "A0", "D0", "G2", "U2", "A1", "D1", "G3", "U3", "A2", "D2", "A3", "D3"]

VECS = [("g1", DEPTH * DC), ("g2", DEPTH * DC), ("ada_b", DEPTH * NMOD * DC), ("cond", DC * S),
        ("gv", GDFF // P), ("gn", 2 * D // P), ("conv_w", 4 * XBC // P), ("conv_b", XBC // P)]
VEC_AT, _n = {}, 0
for _name, _w in VECS:
    VEC_AT[_name] = (_n, _w)
    _n += _w
VEC_COLS = _n
MATS = ["ident", "ones", "t_le", "t_ge", "t_gt", "t_lt", "dft_c", "dft_s", "seq_c", "seq_ns", "na_mask", "iota"]
MAT_AT = {m: i for i, m in enumerate(MATS)}


def build(nc, a, o):
    ctx = ExitStack()
    with ctx:
        def sb(name, shape):
            return ctx.enter_context(nc.sbuf_tensor(name, shape, FP32))

        def sem(name):
            return ctx.enter_context(nc.semaphore(name))

        ring = sb("ring", [P, RING, DC * SLOT_COLS])
        hid = sb("hid", [P, S, D])
        xn = sb("xn", [P, S, D])
        at = sb("at", [P, DC, T])
        gate = sb("gate", [P, 2, S, D])
        acc = sb("acc", [P, S, D])
        mats = sb("mats", [P, len(MATS), P])
        vecs = sb("vecs", [P, VEC_COLS])
        cond = sb("condT", [P, DC, S])
        modt = sb("modt", [P, NMOD * DC, S])
        gsc = sb("gsc", [P, 2, DC, S])
        wr = sb("wr", [P, DEPTH, DC, NR])
        rbias = sb("rbias", [P, DEPTH, NR])
        first = sb("first", [P, EG])
        finalg = sb("finalg", [P, D])
        stat = sb("stat", [P, 32])
        outtmp = sb("outtmp", [P, 2, SLOT_COLS])
        adacc = outtmp
        rt = sb("rt", [P, 24, S, EG])
        rlog = sb("rlog", [P, S, NR])
        rsel = sb("rsel", [P, S, EG, EG])
        posr = sb("posr", [P, S + 1, EG])
        ovi = ctx.enter_context(nc.sbuf_tensor("ovi", [P, 2], mybir.dt.int32))
        ovs = sb("ovs", [P, 8, EG])
        arena = sb("arena", [P, ARENA])

        def carve(at0, *shape):
            n = int(np.prod(shape))
            assert at0 + n <= ARENA, (at0, n)
            v = arena[:, at0:at0 + n]
            if len(shape) == 2:
                v = v.rearrange("p (a b) -> p a b", a=shape[0])
            elif len(shape) == 3:
                v = v.rearrange("p (a b c) -> p a b c", a=shape[0], b=shape[1])
            return v

        xg = carve(0, DC, P)
        onehot = carve(1024, S, P)
        ghT = carve(1280, EG + 1, T)
        ysb = carve(2560, EG + 1, D)
        sgl = carve(7680, 1, FF)
        actv = carve(8192, 1, FF)
        actT = carve(8704, FF // P, P)
        wsl = carve(9216, EG + 1, XG)
        wov = carve(9280, DC, SLOT_COLS)
        f1 = carve(0, 2, 512)
        ft = carve(1024, DC, T)
        qT = carve(0, DC, T)
        kT = carve(2048, DC, T)
        vtok = carve(4096, S, D)
        kcT = carve(6144, DC, P)
        vctx = carve(7168, 1, D)
        rpb = carve(8192, HEADS, P)
        oT = carve(10240, DC, T)
        prob = carve(12288, 2, 512)
        probT = carve(13312, 2, 512)
        nmax = carve(14336, 16, 2)
        esum = carve(14368, 16, 2)
        rsum = carve(14400, 16, 2)
        uT = carve(0, 16, T)
        vg = carve(4096, S, GDFF)
        wsT = carve(8192, SG, P)
        bs = carve(9216, SG, P)
        gt = carve(10240, 2, T)
        xbcT = carve(0, 32, T)
        zs = carve(8192, S, 2 * D)
        segs = carve(12288, 4, 512)
        ttri = carve(14336, 2, 512)
        yfix = carve(15360, 1, 256)
        xtok = acc[:, 0, :].rearrange("p (u n) -> p u n", u=2)
        cbm = at[:, 2:4, :].rearrange("p c n -> p (c n)").rearrange("p (u n) -> p u n", u=4)
        dtx = acc[:, 1, :].rearrange("p (u n) -> p u n", u=4)
        dtxw = xn[:, 0, :].rearrange("p (u n) -> p u n", u=4)
        stout = at[:, 0:2, :].rearrange("p c n -> p (c n)").unsqueeze(1)
        offs = stout
        h0 = xn[:, 1, :].rearrange("p (u n) -> p u n", u=2)
        dtw = sb("dtw", [P, 8, S * 64])
        adt = sb("adt", [P, S, 64])
        nadt = sb("nadt", [P, S, 64])
        edec = sb("edec", [P, 2, 64])
        dtb = sb("dtb", [P, 3, 64])

        psum = ctx.enter_context(nc.psum_tensor("psum", [P, 8, 512], FP32))
        ps = [psum[:, i, :] for i in range(8)]

        def bank(i, *shape):
            v = ps[i][:, :int(np.prod(shape))]
            if len(shape) == 2:
                v = v.rearrange("p (a b) -> p a b", a=shape[0])
            elif len(shape) == 3:
                v = v.rearrange("p (a b c) -> p a b c", a=shape[0], b=shape[1])
            return v

        def vec(name):
            n, w = VEC_AT[name]
            return vecs[:, n:n + w]

        def mat(name):
            return mats[:, MAT_AT[name], :]

        def slot(k):
            return ring[:, k % RING, :].rearrange("p (c n) -> p c n", c=DC)

        def slot_down(k):
            return ring[:, k % RING, :].rearrange("p (c n) -> p c n", c=FF // P)

        full = [sem(f"ring_full{i}") for i in range(RING)]
        slot_done = sem("slot_done")
        consts_in = sem("consts_in")
        small_in = {i: sem(f"small_in{i}") for i in (1, 2, 3)}
        cond_ready = sem("cond_ready")
        ada_step, ada_ev = sem("ada_step"), sem("ada_ev")
        gsc_ready = sem("gsc_ready")
        gate_mm, gate_ev = sem("gate_mm"), sem("gate_ev")
        sq_done, var_ready, rstd_ready, xn_ready = sem("sq_done"), sem("var_ready"), sem("rstd_ready"), sem("xn_ready")
        tr_mm, at_act, at_dve = sem("tr_mm"), sem("at_act"), sem("at_dve")
        o_mm, h_ready = sem("o_mm"), sem("h_ready")
        route_mm = sem("route_mm")
        rexp = sem("router_exp_ready")
        rexp_in = sem("router_exp_in")
        tok_mm, tok_ev = sem("tok_mm"), sem("tok_ev")
        pos_mm, oh_ready, ov_known = sem("pos_mm"), sem("group_onehot_ready"), sem("ov_known")
        onehot_ready, gt_mm, gt_ev = sem("onehot_ready"), sem("gt_mm"), sem("gt_ev")
        xg_mm, xg_ready = sem("xg_mm"), sem("xg_ready")
        sg_ready, act_ready, actT_mm, actT_ev = sem("sg_ready"), sem("act_ready"), sem("actT_mm"), sem("actT_ev")
        y_ev, out_mm = sem("y_ev"), sem("out_mm")
        v_oh, v_gt, v_gt_ev, v_xg, v_xg_ev = sem("v_oh"), sem("v_gt"), sem("v_gt_ev"), sem("v_xg"), sem("v_xg_ev")
        v_w, v_done, v_sg, v_act, v_t, v_t_ev = sem("v_w"), sem("v_done"), sem("v_sg"), sem("v_act"), sem("v_t"), sem("v_t_ev")
        v_chain = sem("v_chain")
        v_y_ev, v_out, v_added = sem("v_y_ev"), sem("v_out"), sem("v_added")
        dve_chain, pool_chain = sem("dve_chain"), sem("pool_chain")
        f1_mm, f1_ev, f2_mm, ft_ready = sem("f1_mm"), sem("f1_ev"), sem("f2_mm"), sem("ft_ready")
        qk_mm, qk_ev, v_mm, v_ev = sem("qk_mm"), sem("qk_ev"), sem("v_mm"), sem("v_ev")
        kt_mm, kt_ev = sem("ktok_mm"), sem("ktok_ev")
        s_mm, nm_ready, e_ready, p_ready = sem("scores_mm"), sem("nmax_ready"), sem("exp_ready"), sem("prob_ready")
        t_mm, pt_ready, av_mm, ot_ready = sem("probT_mm"), sem("probT_ready"), sem("av_mm"), sem("oT_ready")
        m_mm, m_ev = sem("gmlp_mm"), sem("gmlp_ev")
        vsq, vvar, vrstd, vn_ready = sem("v_sq"), sem("v_var"), sem("v_rstd"), sem("vn_ready")
        sp_mm, sp_ev = sem("spatial_mm"), sem("gated_ready")
        x_mm, x_b, x_cv, x_act = sem("xbc_mm"), sem("xbc_tap"), sem("xbc_conv"), sem("xbc_ready")
        dt_exp, dt_ln = sem("dt_exp"), sem("dt_ln")
        dt_abs, a_exp = sem("dt_abs"), sem("a_exp")
        adt_ready, cum_mm, edec_ready = sem("adt_ready"), sem("cum_mm"), sem("edec_ready")
        z_mm, z_ev = sem("z_mm"), sem("z_ev")
        xt_mm, xt_ev, tt_ready = sem("xtok_mm"), sem("xtok_ev"), sem("tri_dt_ready")
        seg_mm, seg_ready, dec_ready, m_ready = sem("seg_mm"), sem("seg_ready"), sem("decay_ready"), sem("mix_ready")
        dtx_step, cbm_step = sem("dtx_step"), sem("cbm_step")
        dtx_ready, yg_mm, y_done = sem("dtx_ready"), sem("yg_mm"), sem("y_done")
        off_ev, st_out = sem("off_ev"), sem("st_out")
        h0_in = [sem("h0_in_even"), sem("h0_in_odd")]
        ysq, yvar, yrstd, yn_ready, yt_mm, yt_ev = (sem("y_sq"), sem("y_var"), sem("y_rstd"), sem("yn_ready"),
                                                     sem("yT_mm"), sem("yT_ready"))
        kv_out, fin_ready, fin_out = sem("kv_out"), sem("fin_ready"), sem("fin_out")

 
        def moe_loads(n):
            return MOE_LOADS + (ADA_LOADS if n + 1 < len(LAYERS) else 0)

        def mix_base(n):
            return ADA_LOADS + sum(MIX_LOADS[x] + moe_loads(i) for i, x in enumerate(LAYERS[:n]))

        def moe_base(n):
            return mix_base(n) + MIX_LOADS[LAYERS[n]]

        def order(n, last):
            return PLAIN if last or n + 1 == len(LAYERS) else MIXED

        def dve_blocks(n):
            return ADA_LOADS // 2 + ADA_LOADS * n

        def block_of(w, rows0, cols):
            return w[rows0:rows0 + D, cols].rearrange("(c p) n -> p c n", p=P)

        ctx.enter_context(nc.allow_non_contiguous_dma("small constants, weight blocks by rows"))
        block = ctx.enter_context(nc.Block())

        @block.sync
        def _(sp):
            def load(k, dst, src, i=None, per=0):
                if i is not None:
                    sp.wait_ge(slot_done, i * per + (k - RING + 1))
                elif k >= RING:
                    sp.wait_ge(slot_done, k - RING + 1)
                sp.dma_start(dst, src).then_inc(full[k % RING], 16)

            for n, l in enumerate(LAYERS):
                if n == 0:
                    for j in range(ADA_LOADS):
                        load(j, slot(j), block_of(a["ada_w"][l], 0, slice(j * SLOT_COLS, (j + 1) * SLOT_COLS)))
                k = mix_base(n)
                if l == 0:
                    todo = [(a["fnet_w_o"][0], 0, j) for j in range(2)]
                elif l == 1:
                    todo = [(a["na_w_qkv"][0], 0, j) for j in range(6)] + [(a["na_w_o"][0], 0, j) for j in range(2)]
                elif l == 2:
                    todo = [(a["gmlp_w_in"][0], 0, j) for j in range(8)]
                    todo += [(a["gmlp_w_out"][0], kk * D, j) for j in range(2) for kk in range(2)]
                else:
                    todo = [(a["ssd_w_in"][0], 0, 4 + j) for j in range(8)] + [None]
                    todo += [(a["ssd_w_in"][0], 0, j) for j in range(4)]
                    todo += [(a["ssd_w_out"][0], kk * D, j) for j in range(2) for kk in range(2)]
                for q, it in enumerate(todo):
                    if it is None:
                        load(k + q, slot(k + q)[:, :, 0:64], block_of(a["ssd_w_in"][0], 0, slice(2 * D + XBC, 2 * D + XBC + 64)))
                    else:
                        w, r0, j = it
                        load(k + q, slot(k + q), block_of(w, r0, slice(j * SLOT_COLS, (j + 1) * SLOT_COLS)))
                assert len(todo) == MIX_LOADS[l]
                k = moe_base(n)

                def group_loads(k, i, last):
                    seq = order(n, last)
                    for q, (what, x) in enumerate(seq):
                        x = int(x)
                        if what == "A":
                            cols = bass.ds(i * (XG * SLOT_COLS) + x * SLOT_COLS, SLOT_COLS)
                            src, dst = block_of(a["ada_w"][LAYERS[n + 1]], 0, cols), slot(k + q)
                        else:
                            w = a[{"G": "moe_w_gate", "U": "moe_w_up", "D": "moe_w_down"}[what]][l]
                            rows = w.rearrange("e (c p) n -> e p c n", p=P)
                            src = rows[bass.ds(i * XG + x, 1)].rearrange("o p c n -> p (o c) n")
                            dst = slot_down(k + q) if what == "D" else slot(k + q)
                        if last:
                            load(k + q, dst, src)
                        else:
                            load(k + q, dst, src, i, len(seq))
                with sp.Fori(0, EG - 1) as i:
                    group_loads(k, i, False)
                group_loads(k + (EG - 1) * len(order(n, False)), EG - 1, True)
                sp.wait_ge(ov_known, n + 1)
                flag = sp.value_load(ovi[0:1, 0:1], min_val=0, max_val=1)
                base = sp.value_load(ovi[0:1, 1:2], min_val=0, max_val=E - XG)
                with sp.If(flag > 0):
                    sp.wait_ge(v_oh, n + 1)
                    for x in range(XG):
                        for q, w in enumerate(("moe_w_gate", "moe_w_up", "moe_w_down")):
                            if n or x or q:
                                sp.wait_ge(v_done, 3 * (XG * n + x) + q)
                            rows = a[w][l].rearrange("e (c p) n -> e p c n", p=P)[bass.ds(base + x, 1)]
                            dst = wov if q < 2 else wov.rearrange("p c n -> p (c n)").rearrange("p (c n) -> p c n", c=FF // P)
                            sp.dma_start(dst, rows.rearrange("o p c n -> p (o c) n")).then_inc(v_w, 16)
                with sp.Else():
                    sp.sem_inc(v_w, 16 * 3 * XG)

        @block.gpsimd
        def _(pool):
            pool.dma_start(vecs[:, :], a["vecs"]).then_inc(consts_in, 16)
            pool.dma_start(mats[:, :, :], a["mats"]).then_inc(consts_in, 16)
            pool.dma_start(hid[:, 0, :], a["x_prompt"][0]).then_inc(consts_in, 16)
            pool.dma_start(hid[:, 1, :], a["x_sample"][0]).then_inc(consts_in, 16)
            pool.dma_start(wr[:, :, :, 0:EG], a["wgr"]).then_inc(consts_in, 16)
            pool.dma_start(wr[:, :, :, EG:NR], a["wer"]).then_inc(consts_in, 16)
            pool.dma_start(rbias[:, :, 0:EG], a["moe_b_gr"].partition_broadcast(P)).then_inc(consts_in, 16)
            pool.dma_start(rbias[:, :, EG:NR], a["moe_b_er"].partition_broadcast(P)).then_inc(consts_in, 16)
            pool.dma_start(finalg[:, :], a["final_g"].partition_broadcast(P)).then_inc(consts_in, 16)
            for j in range(EG):
                pool.memset(first[:, j:j + 1], float(EG - j)).then_inc(pool_chain, 1)
            for n, l in enumerate(LAYERS):
                if l in small_in:
                    if n:
                        pool.wait_ge(h_ready, 8 * n)
                if l == 1:
                    pool.dma_start(rpb, a["rpb_band"]).then_inc(small_in[1], 16)
                    pool.dma_start(kcT, a["cache_kT"]).then_inc(small_in[1], 16)
                    pool.dma_start(vctx[:, 0, :].rearrange("p (h d) -> p h d", h=HEADS),
                                   a["cache_v"][0, 0].rearrange("h t d -> t h d")).then_inc(small_in[1], 16)
                    pool.wait_ge(v_ev, S)
                    pool.wait_ge(v_ev, S * 2)
                    pool.dma_start(o["new_cache_v"][0, 0].rearrange("h t d -> t h d"),
                                   vtok[:, 0, :].rearrange("p (h d) -> p h d", h=HEADS)).then_inc(kv_out, 16)
                    pool.wait_ge(kt_ev, 2)
                    pool.dma_start(o["new_cache_k"][0, 0].rearrange("h t d -> t h d"),
                                   xn[:, 0, :].rearrange("p (h d) -> p h d", h=HEADS)).then_inc(kv_out, 16)
                if l == 2:
                    pool.dma_start(wsT, a["wsT"]).then_inc(small_in[2], 16)
                    pool.dma_start(bs, a["gmlp_b_s"][0].partition_broadcast(P)).then_inc(small_in[2], 16)
                if l == 3:
                    pool.dma_start(dtb[:, 0, :], a["ssd_dt_bias"][0].rearrange("a b -> (a b)").partition_broadcast(P)).then_inc(small_in[3], 16)
                    pool.dma_start(dtb[:, 1, :], a["ssd_a_log"][0].rearrange("a b -> (a b)").partition_broadcast(P)).then_inc(small_in[3], 16)
                    pool.dma_start(dtb[:, 2, 0:SH], a["ssd_d_skip"][0].partition_broadcast(P)).then_inc(small_in[3], 16)
                    pool.wait_ge(adt_ready, 1)
                    tri = [mat("t_le"), mat("t_ge")]
                    for u in range(S * SG):
                        s, g = divmod(u, SG)
                        if u:
                            pool.wait_ge(seg_mm, 2 * u)
                        for d in range(2):
                            pool.tensor_tensor(
                                ttri[:, d, :].rearrange("p (h l) -> p h l", h=HPG),
                                tri[d].unsqueeze(1).to_broadcast([P, HPG, P]),
                                adt[:, s, d * SH + g * HPG:d * SH + (g + 1) * HPG].unsqueeze(2).to_broadcast([P, HPG, P]),
                                ALU.mult).then_inc(tt_ready, 1)
                        if s == 1:
                            if g >= 2:
                                pool.wait_ge(yg_mm, u - 1)
                            pool.dma_start(h0[:, g % 2, :].rearrange("p (d n) -> p d n", d=2),
                                           a["h0T"][:, :, g * 256:(g + 1) * 256]).then_inc(h0_in[g % 2], 16)
                        if 1 <= u <= SG:
                            pool.wait_ge(off_ev, u)
                            for d, name in enumerate(("new_state_ssm_fwd", "new_state_ssm_bwd")):
                                pool.dma_start(
                                    o[name][0, 0, (u - 1) * HPG:u * HPG].rearrange("(a b) p n -> (b p) a n", a=2),
                                    stout[:, 0, d * 256:(d + 1) * 256].rearrange("p (a n) -> p a n", a=2)).then_inc(st_out, 16)
            for s in range(S):
                pool.wait_ge(fin_ready, s + 1)
                pool.dma_start(o["y_prompt" if s == 0 else "y_sample"][0], xn[:, s, :]).then_inc(fin_out, 16)
            pool.wait_ge(fin_out, 16 * S)
            if 1 in LAYERS:
                pool.wait_ge(kv_out, 32)
            if 3 in LAYERS:
                pool.wait_ge(st_out, 32 * SG)

        @block.tensor
        def _(pe):
            def arrive(k, i=None, per=0):
                if i is None:
                    pe.wait_ge(full[k % RING], 16 * (k // RING + 1))
                else:
                    pe.wait_ge(full[k % RING], i * (16 * per // RING) + 16 * (k // RING + 1))

            def dense_chan(k, m, dst, src=at, nk=DC):
                for c in range(nk):
                    last = nc.tensor.matmul(dst, slot(k)[:, c, m * P:(m + 1) * P], src[:, c, :],
                                            start=(c == 0), stop=(c == nk - 1))
                return last

            def dense_tok(k, s, dst, src=at, c0=0, nk=DC, start=True, stop=True, cols=SLOT_COLS):
                for c in range(nk):
                    last = nc.tensor.matmul(dst, src[:, c0 + c, s * P:(s + 1) * P], slot(k)[:, c, 0:cols],
                                            start=(start and c == 0), stop=(stop and c == nk - 1))
                return last

            def out_proj(n, k, src, halves):
                for j in range(2):
                    for kk in range(halves):
                        arrive(k)
                        for s in range(S):
                            last = dense_tok(k, s, ps[4 + 2 * j + s][:, :], src, kk * DC, DC, kk == 0, kk == halves - 1)
                            if kk == halves - 1 and s == 0:
                                last.then_inc(o_mm, 1)
                        last.then_inc(slot_done, 1)
                        k += 1

            def ada_block(k, dst):
                for m in range(4):
                    for c in range(DC):
                        last = nc.tensor.matmul(dst[:, m * S:(m + 1) * S], slot(k)[:, c, m * P:(m + 1) * P], cond[:, c, :],
                                                start=(c == 0), stop=(c == DC - 1))
                last.then_inc(slot_done, 1)

            def ada_sums(dst):
                for m in range(4):
                    for q in range(S):
                        last = nc.tensor.matmul(dst[:, m * S + q:m * S + q + 1], adacc[:, q, m * P:(m + 1) * P],
                                                mats[:, MAT_AT["ones"], 0:1], start=True, stop=True)
                last.then_inc(slot_done, 1)

            def norm_transposes(n, which):
                t = 2 * n + which
                for s in range(S):
                    pe.wait_ge(xn_ready, S * t + s + 1)
                    for h in range(2):
                        for c in range(4):
                            last = nc.tensor.transpose(bank(2 * s + h, 4, P)[:, c, :],
                                                       xn[:, s, (4 * h + c) * P:(4 * h + c + 1) * P], mat("ident"))
                        last.then_inc(tr_mm, 1)

            pe.wait_ge(consts_in, 16 * 9)
            pe.wait_ge(cond_ready, 1)
            for n, l in enumerate(LAYERS):
                if n == 0:
                    for j in range(ADA_LOADS):
                        if j % 2:
                            pe.wait_ge(ada_step, 16 * (j // 2 + 1))
                            ada_sums(bank(3, ADA_LOADS, 4 * S)[:, j, :])
                        else:
                            arrive(j)
                            ada_block(j, bank(3, ADA_LOADS, 4 * S)[:, j, :])
                pe.wait_ge(ada_ev, n + 1)
                for q in range(8):
                    w, s, h = q // 4, (q // 2) % 2, q % 2
                    if q >= 2:
                        pe.wait_ge(gate_ev, 8 * n + q - 1)
                    for c in range(4):
                        col = (3 * w + 2) * DC + 4 * h + c
                        last = nc.tensor.matmul(bank(q % 2, 4, P)[:, c, :], modt[:, col, s:s + 1].to_broadcast([P, P]),
                                                mat("ident"), start=True, stop=True)
                    last.then_inc(gate_mm, 1)
                pe.wait_ge(gate_ev, 8 * (n + 1))
                norm_transposes(n, 0)
                pe.wait_ge(at_act, S * (2 * n + 1))
                pe.wait_ge(at_dve, S * (2 * n + 1))
                k = mix_base(n)
                if l == 0:
                    def fourier_rows(u):
                        s, gp = divmod(u, 4)
                        if u >= 2:
                            pe.wait_ge(f1_ev, u - 1)
                        for gi in range(2):
                            last = nc.tensor.matmul(bank(u % 2, 2, 256)[:, gi, :], at[:, 2 * gp + gi, s * P:(s + 1) * P],
                                                    mats[:, MAT_AT["dft_c"]:MAT_AT["dft_c"] + 2, :].rearrange("p a b -> p (a b)"),
                                                    start=True, stop=True)
                        last.then_inc(f1_mm, 1)

                    def fourier_cols(u):
                        pe.wait_ge(f1_ev, u + 1)
                        if u >= 2:
                            pe.wait_ge(ft_ready, u - 1)
                        for gi in range(2):
                            dst = bank(2 + u % 2, 2, P)[:, gi, :]
                            src = f1[:, u % 2, :].rearrange("p (g x c) -> p g x c", g=2, x=2)
                            nc.tensor.matmul(dst, src[:, gi, 0, :], mat("seq_c"), start=True, stop=False)
                            last = nc.tensor.matmul(dst, src[:, gi, 1, :], mat("seq_ns"), start=False, stop=True)
                        last.then_inc(f2_mm, 1)
                    for u in range(9):
                        if u < 8:
                            fourier_rows(u)
                        if u >= 1:
                            fourier_cols(u - 1)
                    pe.wait_ge(ft_ready, 8)
                    out_proj(n, k, ft, 1)
                elif l == 1:
                    for j in range(4):
                        arrive(k)
                        for mh in range(2):
                            u = 2 * j + mh
                            if u >= 4:
                                pe.wait_ge(qk_ev, u - 3)
                            for m in range(2):
                                last = dense_chan(k, 2 * mh + m, bank(u % 4, 2, T)[:, m, :])
                            last.then_inc(slot_done if mh else qk_mm, 1)
                        k += 1
                    for j in range(2):
                        arrive(k)
                        for s in range(S):
                            b = 2 * j + s
                            pe.wait_ge(qk_ev, 5 + b)
                            last = dense_tok(k, s, ps[b][:, :])
                            last.then_inc(slot_done if s else v_mm, 1)
                        k += 1
                    for h in range(2):
                        for c in range(4):
                            last = nc.tensor.transpose(bank(4 + h, 4, P)[:, c, :], kT[:, 4 * h + c, 0:P], mat("ident"))
                        last.then_inc(kt_mm, 1)
                    pe.wait_ge(small_in[1], 48)
                    pe.wait_ge(kt_ev, 2)
                    pe.wait_ge(v_ev, 4)

                    def scores(u):
                        s, j = divmod(u, DC)
                        if u >= 2:
                            pe.wait_ge(e_ready, u - 1)
                        dst = psum[:, 2 * (u % 2):2 * (u % 2) + 2, :]
                        for hh in range(2):
                            r = slice(HD * hh, HD * (hh + 1))
                            last = nc.tensor.matmul(dst[:, hh, 0:P], qT[r, j, s * P:(s + 1) * P], kT[r, j, s * P:(s + 1) * P],
                                                    start=True, stop=True)
                            if s:
                                last = nc.tensor.matmul(dst[:, hh, P:2 * P], qT[r, j, P:2 * P], kcT[r, j, :], start=True, stop=True)
                        last.then_inc(s_mm, 1)

                    def prob_transposes(u):
                        s, j = divmod(u, DC)
                        pe.wait_ge(p_ready, u + 1)
                        if u >= 2:
                            pe.wait_ge(pt_ready, u - 1)
                        for b in range(2 * (1 + s)):
                            last = nc.tensor.transpose(bank(4 + u % 2, 4, P)[:, b, :],
                                                       prob[:, u % 2, b * P:(b + 1) * P], mat("ident"))
                        last.then_inc(t_mm, 1)

                    def weighted_values(u):
                        s, j = divmod(u, DC)
                        pe.wait_ge(pt_ready, u + 1)
                        if u >= 2:
                            pe.wait_ge(ot_ready, u - 1)
                        pT = probT[:, u % 2, :].rearrange("p (b q) -> p b q", b=4)
                        for hh in range(2):
                            cols = slice((2 * j + hh) * HD, (2 * j + hh + 1) * HD)
                            dst = ps[6 + u % 2][HD * hh:HD * (hh + 1), 0:P]
                            last = nc.tensor.matmul(dst, vtok[:, s, cols], pT[:, hh * (1 + s), :], start=True, stop=(s == 0))
                            if s:
                                last = nc.tensor.matmul(dst, vctx[:, 0, cols], pT[:, 2 * hh + 1, :], start=False, stop=True)
                        last.then_inc(av_mm, 1)
                    U = S * DC
                    for i in range(U + 2):
                        if i < U:
                            scores(i)
                        if 1 <= i <= U:
                            prob_transposes(i - 1)
                        if i >= 2:
                            weighted_values(i - 2)
                    pe.wait_ge(ot_ready, U)
                    out_proj(n, k, oT, 1)
                elif l == 2:
                    for j in range(8):
                        arrive(k)
                        for x in range(2):
                            u = 2 * j + x
                            if u >= 4:
                                pe.wait_ge(m_ev, u - 3)
                            if j < 4:
                                for m in range(2):
                                    last = dense_chan(k, 2 * x + m, bank(u % 4, 2, T)[:, m, :])
                            else:
                                last = dense_tok(k, x, ps[u % 4][:, :])
                            last.then_inc(slot_done if x else m_mm, 1)
                        k += 1
                    pe.wait_ge(small_in[2], 32)
                    pe.wait_ge(vn_ready, S)
                    for g in range(SG):
                        if g >= 4:
                            pe.wait_ge(sp_ev, g - 3)
                        for ci in range(2):
                            for s in range(S):
                                c = 2 * g + ci
                                last = nc.tensor.matmul(bank(g % 4, 2, T)[:, ci, s * P:(s + 1) * P],
                                                        vg[:, s, c * P:(c + 1) * P], wsT[:, g, :], start=True, stop=True)
                        last.then_inc(sp_mm, 1)
                    pe.wait_ge(sp_ev, SG)
                    out_proj(n, k, uT, 2)
                else:
                    for j in range(8):
                        arrive(k)
                        for x in range(2):
                            u = 2 * j + x
                            if u >= 4:
                                pe.wait_ge(x_cv, u - 3)
                            for m in range(2):
                                last = dense_chan(k, 2 * x + m, bank(u % 4, 2, T)[:, m, :])
                            last.then_inc(slot_done if x else x_mm, 1)
                        k += 1
                    arrive(k)
                    for s in range(S):
                        last = dense_tok(k, s, ps[4][:, s * 64:(s + 1) * 64], cols=64)
                    last.then_inc(slot_done, 1)
                    k += 1
                    for j in range(4):
                        arrive(k)
                        for s in range(S):
                            u = 2 * j + s
                            if u < 4:
                                pe.wait_ge(x_cv, 13 + u)
                            else:
                                pe.wait_ge(z_ev, u - 3)
                            last = dense_tok(k, s, ps[u % 4][:, :])
                            last.then_inc(slot_done if s else z_mm, 1)
                        k += 1
                    pe.wait_ge(adt_ready, 1)
                    cums = [(0, 0, "t_gt"), (0, 1, "t_lt"), (1, 0, "t_le"), (1, 1, "t_ge")]
                    for s, d, m in cums:
                        last = nc.tensor.matmul(ps[5][:, s * 64 + d * SH:s * 64 + (d + 1) * SH], mat(m),
                                                adt[:, s, d * SH:(d + 1) * SH], start=True, stop=True)
                    last.then_inc(cum_mm, 1)
                    pe.wait_ge(x_act, 16)
                    pe.wait_ge(z_ev, 8)
                    pe.wait_ge(edec_ready, 1)
                    tri = [mat("t_le"), mat("t_ge")]

                    def group_inputs(u):
                        s, g = divmod(u, SG)
                        tok = slice(s * P, (s + 1) * P)
                        if u:
                            pe.wait_ge(xt_ev, u)
                        nc.tensor.transpose(ps[0][:, 0:P], xbcT[:, 2 * g, tok], mat("ident"))
                        nc.tensor.transpose(ps[0][:, P:2 * P], xbcT[:, 2 * g + 1, tok], mat("ident"))
                        nc.tensor.transpose(ps[0][:, 2 * P:3 * P], xbcT[:, 16 + g, tok], mat("ident"))
                        nc.tensor.matmul(ps[0][:, 3 * P:4 * P], xbcT[:, 16 + g, tok], xbcT[:, 24 + g, tok],
                                         start=True, stop=True).then_inc(xt_mm, 1)
                        for d in range(2):
                            pe.wait_ge(tt_ready, 2 * u + d + 1)
                            if u:
                                pe.wait_ge(seg_ready, 2 * (u - 1) + d + 1)
                            nc.tensor.matmul(ps[1 + d][:, :], mat("ones"), ttri[:, d, :], start=True, stop=False)
                            nc.tensor.matmul(bank(1 + d, HPG, P), tri[d],
                                             nadt[:, s, d * SH + g * HPG:d * SH + (g + 1) * HPG].unsqueeze(2).to_broadcast([P, HPG, P]),
                                             start=False, stop=True).then_inc(seg_mm, 1)

                    def group_outputs(u):
                        s, g = divmod(u, SG)
                        t = 2 * (u % 2)
                        tok = slice(s * P, (s + 1) * P)
                        pe.wait_ge(m_ready, 2 * u + 2)
                        pe.wait_ge(dtx_ready, u + 1)
                        if u:
                            pe.wait_ge(y_done, u)
                            pe.wait_ge(off_ev, min(u, SG))
                        for h in range(HPG):
                            for d in range(2):
                                last = nc.tensor.matmul(ps[3][:, h * HD:(h + 1) * HD], segs[:, t + d, h * P:(h + 1) * P],
                                                        dtx[:, t + d, h * HD:(h + 1) * HD], start=(d == 0), stop=(d == 1))
                        if s == 0:
                            for d in range(2):
                                for hp in range(2):
                                    last = nc.tensor.matmul(bank(4, 4, P)[:, 2 * d + hp, :], dtxw[:, t + d, hp * P:(hp + 1) * P],
                                                            xtok[:, u % 2, 2 * P:3 * P], start=True, stop=True)
                        else:
                            pe.wait_ge(h0_in[g % 2], 16 * (g // 2 + 1))
                            last = nc.tensor.matmul(ps[4][:, :], xbcT[:, 24 + g, tok], h0[:, g % 2, :], start=True, stop=True)
                        last.then_inc(yg_mm, 1)
                    for i in range(S * SG + 1):
                        if i < S * SG:
                            group_inputs(i)
                        if i:
                            group_outputs(i - 1)
                    pe.wait_ge(y_done, S * SG)
                    for s in range(S):
                        pe.wait_ge(yn_ready, s + 1)
                        for q in range(4):
                            u = 4 * s + q
                            if u >= 4:
                                pe.wait_ge(yt_ev, u - 3)
                            for c in range(4):
                                last = nc.tensor.transpose(bank(u % 4, 4, P)[:, c, :], zs[:, s, (4 * q + c) * P:(4 * q + c + 1) * P],
                                                           mat("ident"))
                            last.then_inc(yt_mm, 1)
                    pe.wait_ge(yt_ev, 8)
                    out_proj(n, k, xbcT, 2)
                norm_transposes(n, 1)
                pe.wait_ge(at_act, S * (2 * n + 2))
                pe.wait_ge(at_dve, S * (2 * n + 2))
                for s in range(S):
                    for c in range(DC):
                        last = nc.tensor.matmul(bank(4, S, NR)[:, s, :], at[:, c, s * P:(s + 1) * P], wr[:, l, c, :],
                                                start=(c == 0), stop=(c == DC - 1))
                last.then_inc(route_mm, 1)
                for s in range(S):
                    for h in range(2):
                        for c in range(4):
                            last = nc.tensor.transpose(bank(2 * s + h, 4, P)[:, c, :], at[:, 4 * h + c, s * P:(s + 1) * P], mat("ident"))
                        last.then_inc(tok_mm, 1)
                pe.wait_ge(oh_ready, n + 1)
                oh = [rt[:, 4, s, :] for s in range(S)]
                nc.tensor.matmul(ps[5][:, 0:EG], mat("t_lt"), oh[0], start=True, stop=True)
                nc.tensor.matmul(ps[5][:, EG:2 * EG], mat("t_lt"), oh[1], start=True, stop=False)
                nc.tensor.matmul(ps[5][:, EG:2 * EG], mat("ones"), oh[0], start=False, stop=True)
                nc.tensor.matmul(ps[5][:, 2 * EG:3 * EG], mat("ones"), oh[0], start=True, stop=False)
                nc.tensor.matmul(ps[5][:, 2 * EG:3 * EG], mat("ones"), oh[1], start=False, stop=True).then_inc(pos_mm, 1)

                def gather_rows(rows_done, places_done):
                    for s in range(S):
                        nc.tensor.transpose(ps[2][:, s * P:(s + 1) * P], onehot[:, s, :], mat("ident"))
                    for s in range(S):
                        last = nc.tensor.matmul(ps[2][:, T:T + XG], onehot[:, s, :], rt[:, 12, s, :], start=(s == 0), stop=(s == 1))
                    last.then_inc(places_done, 1)
                    for c in range(DC):
                        for s in range(S):
                            last = nc.tensor.matmul(bank(4 + c // 4, 4, P)[:, c % 4, :], xn[:, s, c * P:(c + 1) * P], onehot[:, s, :],
                                                    start=(s == 0), stop=(s == 1))
                        if c % 4 == 3:
                            last.then_inc(rows_done, 1)

                def gather(i):
                    pe.wait_ge(onehot_ready, i + (EG * n + 1))
                    pe.wait_ge(gt_ev, i + EG * n)
                    if not (isinstance(i, int) and i == 0):
                        pe.wait_ge(actT_ev, i * XG + (E * n - 1))
                    gather_rows(xg_mm, gt_mm)

                def rows_times(dst, blk, cols=slice(0, SLOT_COLS)):
                    for c in range(DC):
                        last = nc.tensor.matmul(dst, xg[:, c, :], blk[:, c, cols], start=(c == 0), stop=(c == DC - 1))
                    return last

                def act_transposes():
                    for c in range(FF // P):
                        last = nc.tensor.transpose(bank(2, 4, P)[:, c, :], actv[:, 0, c * P:(c + 1) * P], mat("ident"))
                    return last

                def down(blk, start, stop):
                    for j in range(2):
                        for c in range(FF // P):
                            last = nc.tensor.matmul(ps[6 + j][:, :], actT[:, c, :], blk[:, c, j * SLOT_COLS:(j + 1) * SLOT_COLS],
                                                    start=(start and c == 0), stop=(stop and c == FF // P - 1))
                    return last

                def group(k, i, last_group):
                    seq = order(n, last_group)
                    per = len(seq)
                    ks = {w: k + q for q, w in enumerate(seq)}

                    def at_hand(w):
                        if last_group:
                            arrive(ks[w])
                        else:
                            arrive(ks[w], i, per)

                    def turned(x):
                        return i * XG + (E * n + x)

                    def gate_product(x):
                        at_hand(f"G{x}")
                        pe.wait_ge(sg_ready, turned(x))
                        rows_times(ps[0][:, :], slot(ks[f"G{x}"])).then_inc(slot_done, 1)

                    def up_product(x):
                        at_hand(f"U{x}")
                        pe.wait_ge(act_ready, turned(x))
                        rows_times(ps[1][:, :], slot(ks[f"U{x}"])).then_inc(slot_done, 1)

                    def transposes(x):
                        pe.wait_ge(act_ready, turned(x + 1))
                        if x == XG - 1:
                            if not last_group:
                                pe.wait_ge(gt_ev, i + (EG * n + 2))
                            else:
                                pe.wait_ge(actT_ev, turned(x))
                        else:
                            pe.wait_ge(actT_ev, turned(x))
                            if x == 0:
                                pe.wait_ge(gt_ev, i + (EG * n + 1))
                        act_transposes().then_inc(actT_mm, 1)

                    def down_product(x):
                        at_hand(f"D{x}")
                        pe.wait_ge(actT_ev, turned(x + 1))
                        if x == 0:
                            pe.wait_ge(y_ev, i + EG * n)
                        down(slot_down(ks[f"D{x}"]), x == 0, x == XG - 1).then_inc(slot_done, 1)

                    def ada_product(x):
                        if f"A{x}" in ks:
                            pe.wait_ge(ada_step, i * (16 * XG) + 16 * (dve_blocks(n) + x + 1))
                            ada_sums(ps[3][:, bass.ds(i * (16 * S) + x * 4 * S, 4 * S)])
                    pe.wait_ge(xg_ready, i + (EG * n + 1))
                    gate_product(0)
                    up_product(0)
                    for x in range(1, XG):
                        gate_product(x)
                        transposes(x - 1)
                        up_product(x)
                        ada_product(x - 1)
                        down_product(x - 1)
                    if not last_group:
                        gather(i + 1)
                    transposes(XG - 1)
                    ada_product(XG - 1)
                    down_product(XG - 1)

                pe.wait_ge(tok_ev, 4 * (n + 1))
                gather(0)
                pe.wait_ge(ov_known, n + 1)
                flag = pe.value_load(ovi[0:1, 0:1], min_val=0, max_val=1)
                k = moe_base(n)
                with pe.Fori(0, EG - 1) as i:
                    group(k, i, False)
                group(k + (EG - 1) * len(order(n, False)), EG - 1, True)
                pe.wait_ge(y_ev, EG * (n + 1))

                def scatter(groups, out_sem):
                    for s in range(S):
                        for j in range(2):
                            for q, g in enumerate(groups):
                                last = nc.tensor.matmul(ps[4 + 2 * s + j][:, :], ghT[:, g, s * P:(s + 1) * P],
                                                        ysb[:, g, j * SLOT_COLS:(j + 1) * SLOT_COLS],
                                                        start=(q == 0), stop=(q == len(groups) - 1))
                            last.then_inc(out_sem, 1)
                with pe.If(flag > 0):
                    pe.wait_ge(v_oh, n + 1)
                    gather_rows(v_xg, v_gt)
                    pe.wait_ge(v_xg_ev, 2 * (n + 1))
                    with pe.Fori(0, XG) as x:
                        for q in range(2):
                            pe.wait_ge(v_w, x * 48 + (16 * 12 * n + 16 * (q + 1)))
                            rows_times(ps[q][:, :], wov).then_inc(v_done, 1)
                        pe.wait_ge(v_act, x + (XG * n + 1))
                        pe.wait_ge(v_gt_ev, n + 1)
                        act_transposes().then_inc(v_t, 1)
                        pe.wait_ge(v_t_ev, x + (XG * n + 1))
                        pe.wait_ge(v_w, x * 48 + (16 * 12 * n + 48))
                        if True:
                            pe.wait_ge(v_y_ev, x + XG * n)
                            down(wov.rearrange("p c n -> p (c n)").rearrange("p (c n) -> p c n", c=FF // P), True, True).then_inc(v_done, 1)
                    pe.wait_ge(v_y_ev, XG * (n + 1))
                    scatter([EG], v_out)
                    pe.wait_ge(v_added, 4 * (n + 1))
                with pe.Else():
                    pe.sem_inc(v_gt, 1)
                    pe.sem_inc(v_xg, 2)
                    pe.sem_inc(v_done, 3 * XG)
                    pe.sem_inc(v_t, XG)
                    pe.sem_inc(v_out, 4)
                scatter(range(EG), out_mm)

        @block.scalar
        def _(act):
            A = nc.scalar.activation
            act.wait_ge(consts_in, 16 * 9)
            A(cond[:, :, :], vec("cond").rearrange("p (c s) -> p c s", s=S), ACT.Silu).then_inc(cond_ready, 1)

            def norm(n, which):
                t = 2 * n + which
                if t:
                    act.wait_ge(h_ready, 4 * t)
                for s in range(S):
                    A(acc[:, s, :], hid[:, s, :], ACT.Square, accum_out=stat[:, s:s + 1]).then_inc(sq_done, 1)
                for s in range(S):
                    act.wait_ge(var_ready, S * t + s + 1)
                    A(stat[:, 4 + s:5 + s], stat[:, 2 + s:3 + s], ACT.Sqrt).then_inc(rstd_ready, 1)
                if n == len(LAYERS):
                    return
                act.wait_ge(gsc_ready, n + 1)
                for s in range(S):
                    act.wait_ge(tr_mm, 4 * t + 2 * s + 1)
                    for c in range(4):
                        last = A(at[:, c, s * P:(s + 1) * P], bank(2 * s, 4, P)[:, c, :], ACT.Identity,
                                 scale=gsc[:, which, c, s:s + 1], bias=modt[:, 3 * which * DC + c, s:s + 1])
                    last.then_inc(at_act, 1)

            for n, l in enumerate(LAYERS):
                for q in range(8):
                    w, s, h = q // 4, (q // 2) % 2, q % 2
                    act.wait_ge(gate_mm, 8 * n + q + 1)
                    A(gate[:, w, s, h * 512:(h + 1) * 512], ps[q % 2][:, :], ACT.Copy).then_inc(gate_ev, 1)
                norm(n, 0)
                k = mix_base(n)
                if l == 0:
                    for u in range(8):
                        act.wait_ge(f1_mm, u + 1)
                        if u >= 2:
                            act.wait_ge(f2_mm, u - 1)
                        A(f1[:, u % 2, :], ps[u % 2][:, :], ACT.Copy).then_inc(f1_ev, 1)
                elif l == 1:
                    for u in range(8):
                        j, mh = divmod(u, 2)
                        if mh:
                            act.wait_ge(slot_done, k + j + 1)
                        else:
                            act.wait_ge(qk_mm, j + 1)
                        if u < 4:
                            A(qT[:, 2 * u:2 * u + 2, :], bank(u % 4, 2, T), ACT.Copy, scale=HD ** -0.5).then_inc(qk_ev, 1)
                        else:
                            A(kT[:, 2 * u - 8:2 * u - 6, :], bank(u % 4, 2, T), ACT.Copy).then_inc(qk_ev, 1)
                    U = S * DC
                    for i in range(U + 1):
                        if i < U:
                            w = P * (1 + i // DC)
                            act.wait_ge(nm_ready, i + 1)
                            if i >= 2:
                                act.wait_ge(t_mm, i - 1)
                            for hh in range(2):
                                last = A(prob[:, i % 2, hh * w:(hh + 1) * w], ps[2 * (i % 2) + hh][:, 0:w], ACT.Exp,
                                         bias=nmax[:, i, hh:hh + 1], accum_out=esum[:, i, hh:hh + 1])
                            last.then_inc(e_ready, 1)
                        if i >= 1:
                            v = i - 1
                            act.wait_ge(t_mm, v + 1)
                            if v >= 2:
                                act.wait_ge(av_mm, v - 1)
                            w = 2 * P * (1 + v // DC)
                            A(probT[:, v % 2, 0:w], ps[4 + v % 2][:, 0:w], ACT.Copy).then_inc(pt_ready, 1)
                elif l == 2:
                    for u in range(16):
                        j, x = divmod(u, 2)
                        if x:
                            act.wait_ge(slot_done, k + j + 1)
                        else:
                            act.wait_ge(m_mm, j + 1)
                        if j < 4:
                            A(uT[:, 2 * u:2 * u + 2, :], bank(u % 4, 2, T), ACT.Gelu_apprx_tanh).then_inc(m_ev, 1)
                        else:
                            A(vg[:, x, (j - 4) * 512:(j - 3) * 512], ps[u % 4][:, :], ACT.Gelu_apprx_tanh).then_inc(m_ev, 1)
                    act.wait_ge(m_ev, 16)
                    for s in range(S):
                        A(acc[:, :, :].rearrange("p a b -> p (a b)"), vg[:, s, :], ACT.Square,
                          accum_out=stat[:, 6 + s:7 + s]).then_inc(vsq, 1)
                        act.wait_ge(vsq, s + 1)
                    for s in range(S):
                        act.wait_ge(vvar, s + 1)
                        A(stat[:, 10 + s:11 + s], stat[:, 8 + s:9 + s], ACT.Sqrt).then_inc(vrstd, 1)
                else:
                    cw, cb = vec("conv_w"), vec("conv_b")
                    for u in range(17):
                        if u < 16:
                            j, x = divmod(u, 2)
                            if x:
                                act.wait_ge(slot_done, k + j + 1)
                            else:
                                act.wait_ge(x_mm, j + 1)
                            for m in range(2):
                                c = 2 * u + m
                                last = A(xbcT[:, c, :], bank(u % 4, 2, T)[:, m, :], ACT.Identity,
                                         scale=cw[:, 64 + c:65 + c], bias=cb[:, c:c + 1])
                            last.then_inc(x_b, 1)
                        if u:
                            act.wait_ge(x_cv, u)
                            A(xbcT[:, 2 * u - 2:2 * u, :], xbcT[:, 2 * u - 2:2 * u, :], ACT.Silu).then_inc(x_act, 1)
                    act.wait_ge(small_in[3], 48)
                    A(dtb[:, 1, :], dtb[:, 1, :], ACT.Exp).then_inc(a_exp, 1)
                    act.wait_ge(dt_abs, 1)
                    A(dtw[:, 2, :], dtw[:, 1, :], ACT.Exp).then_inc(dt_exp, 1)
                    act.wait_ge(dt_abs, 2)
                    A(dtw[:, 4, :], dtw[:, 3, :], ACT.Ln).then_inc(dt_ln, 1)
                    for u in range(8):
                        j, s = divmod(u, 2)
                        if s:
                            act.wait_ge(slot_done, k + 9 + j + 1)
                        else:
                            act.wait_ge(z_mm, j + 1)
                        A(zs[:, s, j * 512:(j + 1) * 512], ps[u % 4][:, :], ACT.Silu).then_inc(z_ev, 1)
                    act.wait_ge(cum_mm, 1)
                    A(edec[:, :, :], bank(5, 2, 64), ACT.Exp).then_inc(edec_ready, 1)
                    for i in range(S * SG + 1):
                        if i < S * SG:
                            act.wait_ge(xt_mm, i + 1)
                            if i >= 2:
                                act.wait_ge(yg_mm, i - 1)
                                act.wait_ge(y_done, i - 1)
                            A(xtok[:, i % 2, :], ps[0][:, :], ACT.Copy).then_inc(xt_ev, 1)
                            for d in range(2):
                                act.wait_ge(seg_ready, 2 * i + d + 1)
                                A(segs[:, 2 * (i % 2) + d, :], segs[:, 2 * (i % 2) + d, :], ACT.Exp).then_inc(dec_ready, 1)
                        if 1 <= i <= SG:
                            act.wait_ge(yg_mm, i)
                            if i > 1:
                                act.wait_ge(st_out, 32 * (i - 1))
                            A(stout[:, 0, :], ps[4][:, :], ACT.Copy).then_inc(off_ev, 1)
                    for s in range(S):
                        act.wait_ge(y_done, SG * S)
                        if s:
                            act.wait_ge(ysq, 1)
                        A(xn[:, :, :].rearrange("p a b -> p (a b)"), zs[:, s, :], ACT.Square,
                          accum_out=stat[:, 12 + s:13 + s]).then_inc(ysq, 1)
                    for s in range(S):
                        act.wait_ge(yvar, s + 1)
                        A(stat[:, 16 + s:17 + s], stat[:, 14 + s:15 + s], ACT.Sqrt).then_inc(yrstd, 1)
                    gn = vec("gn")
                    for u in range(8):
                        s, q = divmod(u, 4)
                        act.wait_ge(yt_mm, u + 1)
                        for c in range(4):
                            last = A(xbcT[:, 4 * q + c, s * P:(s + 1) * P], bank(u % 4, 4, P)[:, c, :], ACT.Identity,
                                     scale=gn[:, 4 * q + c:4 * q + c + 1])
                        last.then_inc(yt_ev, 1)
                norm(n, 1)
                for r in range(2):
                    act.wait_ge(rexp_in, 2 * n + r + 1)
                    A(rt[:, 2 + 5 * r, :, :], rt[:, 1 + 5 * r, :, :], ACT.Exp).then_inc(rexp, 1)
                def group(k, i, last_group):
                    seq = order(n, last_group)
                    ks = {w: k + q for q, w in enumerate(seq)}

                    def product(w):
                        if last_group:
                            act.wait_ge(slot_done, ks[w] + 1)
                        else:
                            act.wait_ge(slot_done, i * len(seq) + (ks[w] + 1))

                    def silu(x):
                        product(f"G{x}")
                        act.wait_ge(act_ready, i * XG + (E * n + x))
                        A(sgl[:, 0, :], ps[0][:, :], ACT.Silu).then_inc(sg_ready, 1)

                    def transposed(x):
                        act.wait_ge(actT_mm, i * XG + (E * n + x + 1))
                        A(actT[:, :, :], bank(2, 4, P), ACT.Copy).then_inc(actT_ev, 1)
                    silu(0)
                    for x in range(1, XG):
                        silu(x)
                        transposed(x - 1)
                    if not last_group:
                        gathered(i + 1)
                    transposed(XG - 1)
                    product("D3")
                    A(ysb[:, bass.ds(i, 1), :].rearrange("p o (j n) -> p (o j) n", j=2), psum[:, 6:8, :], ACT.Copy).then_inc(y_ev, 1)

                def gathered(i):
                    act.wait_ge(gt_mm, i + (EG * n + 1))
                    A(ghT[:, bass.ds(i, 1), :], ps[2][:, 0:T].unsqueeze(1), ACT.Copy)
                    A(wsl[:, bass.ds(i, 1), :], ps[2][:, T:T + XG].unsqueeze(1), ACT.Copy).then_inc(gt_ev, 1)
                    for h in range(2):
                        act.wait_ge(xg_mm, i * 2 + (2 * EG * n + h + 1))
                        last = A(xg[:, 4 * h:4 * h + 4, :], bank(4 + h, 4, P), ACT.Copy)
                    last.then_inc(xg_ready, 1)
                for s in range(S):
                    for h in range(2):
                        act.wait_ge(tok_mm, 4 * n + 2 * s + h + 1)
                        A(xn[:, s, h * 512:(h + 1) * 512], ps[2 * s + h][:, :], ACT.Copy).then_inc(tok_ev, 1)
                gathered(0)
                act.wait_ge(ov_known, n + 1)
                flag = act.value_load(ovi[0:1, 0:1], min_val=0, max_val=1)
                k = moe_base(n)
                with act.Fori(0, EG - 1) as i:
                    group(k, i, False)
                group(k + (EG - 1) * len(order(n, False)), EG - 1, True)
                with act.If(flag > 0):
                    act.wait_ge(v_gt, n + 1)
                    A(ghT[:, EG, :], ps[2][:, 0:T], ACT.Copy)
                    A(wsl[:, EG, :], ps[2][:, T:T + XG], ACT.Copy).then_inc(v_gt_ev, 1)
                    for h in range(2):
                        act.wait_ge(v_xg, 2 * n + h + 1)
                        A(xg[:, 4 * h:4 * h + 4, :], bank(4 + h, 4, P), ACT.Copy).then_inc(v_xg_ev, 1)
                    with act.Fori(0, XG) as x:
                        act.wait_ge(v_done, x * 3 + (3 * XG * n + 1))
                        act.wait_ge(v_act, x + XG * n)
                        A(sgl[:, 0, :], ps[0][:, :], ACT.Silu).then_inc(v_sg, 1)
                        act.wait_ge(v_t, x + (XG * n + 1))
                        A(actT[:, :, :], bank(2, 4, P), ACT.Copy).then_inc(v_t_ev, 1)
                with act.Else():
                    act.sem_inc(v_gt_ev, 1)
                    act.sem_inc(v_xg_ev, 2)
                    act.sem_inc(v_sg, XG)
                    act.sem_inc(v_t_ev, XG)
            norm(len(LAYERS), 0)

        @block.vector
        def _(dve):
            V = nc.vector
            count = [0]

            def link(ins):
                count[0] += 1
                ins.then_inc(dve_chain, 1)
                dve.wait_ge(dve_chain, count[0])

            dve.wait_ge(consts_in, 16 * 9)
            dve.wait_ge(pool_chain, EG)

            def sum_block(k, done, i=None, per=0):
                def step_wait(steps):
                    if i is None:
                        dve.wait_ge(ada_step, 16 * done + steps)
                    else:
                        dve.wait_ge(ada_step, i * (16 * XG) + (16 * done + steps))
                if i is None:
                    dve.wait_ge(full[k % RING], 16 * (k // RING + 1))
                else:
                    dve.wait_ge(full[k % RING], i * (16 * per // RING) + 16 * (k // RING + 1))
                for c in range(DC):
                    for q in range(S):
                        w = slot(k)[:, c, :]
                        if c == 0:
                            last = V.tensor_scalar(adacc[:, q, :], w, cond[:, c, q:q + 1], None, ALU.mult)
                        else:
                            step_wait(2 * c - 1 + q)
                            last = V.scalar_tensor_tensor(adacc[:, q, :], w, cond[:, c, q:q + 1], adacc[:, q, :], ALU.mult, ALU.add)
                        last.then_inc(ada_step, 1)

            dve.wait_ge(cond_ready, 1)
            for j in range(1, ADA_LOADS, 2):
                if j > 1:
                    dve.wait_ge(slot_done, j - 1)
                sum_block(j, j // 2)

            def root_input(col_in, col_out, width, signal):
                link(V.tensor_scalar(stat[:, col_out:col_out + 1], stat[:, col_in:col_in + 1], 1.0 / width, EPS, ALU.mult, ALU.add))
                V.reciprocal(stat[:, col_out:col_out + 1], stat[:, col_out:col_out + 1]).then_inc(signal, 1)

            def norm(n, which):
                t = 2 * n + which
                for s in range(S):
                    dve.wait_ge(sq_done, S * t + s + 1)
                    root_input(s, 2 + s, D, var_ready)
                if t:
                    dve.wait_ge(h_ready, 4 * t)
                for s in range(S):
                    dve.wait_ge(rstd_ready, S * t + s + 1)
                    if n == len(LAYERS):
                        link(V.tensor_scalar(xn[:, s, :], hid[:, s, :], stat[:, 4 + s:5 + s], None, ALU.mult))
                        V.tensor_tensor(xn[:, s, :], xn[:, s, :], finalg[:, :], ALU.mult).then_inc(fin_ready, 1)
                    else:
                        V.tensor_scalar(xn[:, s, :], hid[:, s, :], stat[:, 4 + s:5 + s], None, ALU.mult).then_inc(xn_ready, 1)
                if n == len(LAYERS):
                    return
                for s in range(S):
                    dve.wait_ge(tr_mm, 4 * t + 2 * s + 2)
                    for c in range(4, DC):
                        last = V.tensor_scalar(at[:, c, s * P:(s + 1) * P], bank(2 * s + 1, 4, P)[:, c - 4, :],
                                               gsc[:, which, c, s:s + 1], modt[:, 3 * which * DC + c, s:s + 1], ALU.mult, ALU.add)
                    last.then_inc(at_dve, 1)

            def add_mixer(n, k_last):
                for j in range(2):
                    for s in range(S):
                        if s:
                            dve.wait_ge(slot_done, k_last[j] + 1)
                        else:
                            dve.wait_ge(o_mm, 2 * n + j + 1)
                        cols = slice(j * 512, (j + 1) * 512)
                        link(V.tensor_tensor(outtmp[:, s, :], ps[4 + 2 * j + s][:, :], gate[:, 0, s, cols], ALU.mult))
                        V.tensor_tensor(hid[:, s, cols], hid[:, s, cols], outtmp[:, s, :], ALU.add).then_inc(h_ready, 1)

            def first_of_max(vals, m, tmp, onehot, signal=None):
                link(V.tensor_tensor(tmp, vals, m.to_broadcast([P, S, EG]), ALU.is_equal))
                link(V.tensor_tensor(tmp, tmp, first[:, :].unsqueeze(1).to_broadcast([P, S, EG]), ALU.mult))
                link(V.tensor_reduce(m, tmp, AX.X, ALU.max))
                last = V.tensor_tensor(onehot, tmp, m.to_broadcast([P, S, EG]), ALU.is_equal)
                if signal is None:
                    link(last)
                else:
                    last.then_inc(signal, 1)

            def route(n, l):
                R = lambda q: rt[:, q, :, :]
                one = lambda q: rt[:, 16 + q, :, 0:1]
                dve.wait_ge(route_mm, n + 1)
                link(V.tensor_tensor(rlog[:, :, :], bank(4, S, NR), rbias[:, l, :].unsqueeze(1).to_broadcast([P, S, NR]), ALU.add))
                gl = rlog[:, :, 0:EG]
                link(V.tensor_reduce(one(0), gl, AX.X, ALU.max))
                V.tensor_tensor(R(1), gl, one(0).to_broadcast([P, S, EG]), ALU.subtract).then_inc(rexp_in, 1)
                first_of_max(gl, one(0), R(3), R(4), oh_ready)
                dve.wait_ge(rexp, 2 * n + 1)
                link(V.tensor_reduce(one(1), R(2), AX.X, ALU.add))
                link(V.reciprocal(one(1), one(1)))
                dve.wait_ge(oh_ready, n + 1)
                link(V.tensor_tensor(rsel[:, :, :, :], rlog[:, :, EG:NR].rearrange("p s (g e) -> p s g e", g=EG),
                                     R(4).unsqueeze(3).to_broadcast([P, S, EG, EG]), ALU.mult))
                link(V.tensor_reduce(R(5), rsel[:, :, :, :].rearrange("p s g e -> p s e g"), AX.X, ALU.add))
                link(V.tensor_reduce(one(2), R(5), AX.X, ALU.max))
                V.tensor_tensor(R(6), R(5), one(2).to_broadcast([P, S, EG]), ALU.subtract).then_inc(rexp_in, 1)
                dve.wait_ge(rexp, 2 * n + 2)
                link(V.tensor_reduce(one(3), R(7), AX.X, ALU.max))
                first_of_max(R(7), one(3), R(8), R(9))
                link(V.scalar_tensor_tensor(R(10), R(9), -4.0, R(7), ALU.mult, ALU.add))
                link(V.tensor_reduce(one(4), R(10), AX.X, ALU.max))
                first_of_max(R(10), one(4), R(8), R(11))
                link(V.tensor_tensor(R(12), R(9), R(11), ALU.add))
                link(V.tensor_tensor(R(12), R(12), R(7), ALU.mult))
                link(V.tensor_reduce(one(5), R(12), AX.X, ALU.add))
                link(V.reciprocal(one(5), one(5)))
                link(V.tensor_tensor(one(5), one(5), one(1), ALU.mult))
                link(V.tensor_tensor(R(12), R(12), one(5).to_broadcast([P, S, EG]), ALU.mult))
                dve.wait_ge(pos_mm, n + 1)
                link(V.tensor_copy(posr[:, :, :], bank(5, S + 1, EG)))
                O = lambda q: ovs[:, q, :]
                link(V.tensor_scalar(O(0), posr[:, S, :], float(P), None, ALU.is_gt))
                link(V.tensor_tensor(O(1), O(0), first[:, :], ALU.mult))
                link(V.tensor_reduce(O(2)[:, 0:1], O(0), AX.X, ALU.max))
                link(V.tensor_reduce(O(2)[:, 1:2], O(1), AX.X, ALU.add))
                link(V.tensor_scalar(O(2)[:, 2:3], O(2)[:, 0:1], float(EG), None, ALU.mult))
                link(V.tensor_tensor(O(2)[:, 2:3], O(2)[:, 2:3], O(2)[:, 1:2], ALU.subtract))
                link(V.tensor_scalar(O(2)[:, 1:2], O(2)[:, 2:3], float(XG), None, ALU.mult))
                V.tensor_copy(ovi[:, :], O(2)[:, 0:2]).then_inc(ov_known, 1)

            def build_onehot(n, i):
                for s in range(S):
                    last = V.tensor_scalar(onehot[:, s, :], mat("iota"), posr[:, s, bass.ds(i, 1)], rt[:, 4, s, bass.ds(i, 1)],
                                           ALU.is_equal, ALU.mult)
                last.then_inc(onehot_ready, 1)

            for n, l in enumerate(LAYERS):
                if n == 0:
                    dve.wait_ge(slot_done, ADA_LOADS)
                V.tensor_tensor(modt[:, :, :], bank(3, NMOD * DC, S),
                                vec("ada_b")[:, l * NMOD * DC:(l + 1) * NMOD * DC].unsqueeze(2).to_broadcast([P, NMOD * DC, S]),
                                ALU.add).then_inc(ada_ev, 1)
                dve.wait_ge(ada_ev, n + 1)
                for w in range(2):
                    g = vec("g1" if w == 0 else "g2")[:, l * DC:(l + 1) * DC]
                    last = V.scalar_tensor_tensor(gsc[:, w, :, :], modt[:, (3 * w + 1) * DC:(3 * w + 2) * DC, :], 1.0,
                                                  g.unsqueeze(2).to_broadcast([P, DC, S]), ALU.add, ALU.mult)
                last.then_inc(gsc_ready, 1)
                dve.wait_ge(gsc_ready, n + 1)
                norm(n, 0)
                k = mix_base(n)
                if l == 0:
                    for u in range(8):
                        s, gp = divmod(u, 4)
                        dve.wait_ge(f2_mm, u + 1)
                        V.tensor_copy(ft[:, 2 * gp:2 * gp + 2, s * P:(s + 1) * P], bank(2 + u % 2, 2, P)).then_inc(ft_ready, 1)
                    add_mixer(n, [k, k + 1])
                elif l == 1:
                    dve.wait_ge(small_in[1], 48)
                    link(V.tensor_tensor(rpb, rpb, mat("na_mask").unsqueeze(1).to_broadcast([P, HEADS, P]), ALU.add))
                    for j in range(2):
                        for s in range(S):
                            if s:
                                dve.wait_ge(slot_done, k + 4 + j + 1)
                            else:
                                dve.wait_ge(v_mm, j + 1)
                            V.tensor_copy(vtok[:, s, j * 512:(j + 1) * 512], ps[2 * j + s][:, :]).then_inc(v_ev, 1)
                    for h in range(2):
                        dve.wait_ge(kt_mm, h + 1)
                        V.tensor_copy(xn[:, 0, h * 512:(h + 1) * 512], ps[4 + h][:, :]).then_inc(kt_ev, 1)
                    U = S * DC
                    for i in range(U + 2):
                        if i < U:
                            s, j = divmod(i, DC)
                            dve.wait_ge(s_mm, i + 1)
                            sc = psum[:, 2 * (i % 2):2 * (i % 2) + 2, 0:P * (1 + s)]
                            if s:
                                link(V.tensor_tensor(sc[:, :, 0:P], sc[:, :, 0:P], rpb[:, 2 * j:2 * j + 2, :], ALU.add))
                            V.tensor_reduce(nmax[:, i, :], sc, AX.X, ALU.max, negate=True).then_inc(nm_ready, 1)
                        if 1 <= i <= U:
                            v = i - 1
                            w = P * (1 + v // DC)
                            dve.wait_ge(e_ready, v + 1)
                            link(V.reciprocal(rsum[:, v, :], esum[:, v, :]))
                            pr = prob[:, v % 2, 0:2 * w].rearrange("p (h k) -> p h k", h=2)
                            V.tensor_tensor(pr, pr, rsum[:, v, :].unsqueeze(2).to_broadcast([P, 2, w]), ALU.mult).then_inc(p_ready, 1)
                        if i >= 2:
                            v = i - 2
                            s, j = divmod(v, DC)
                            dve.wait_ge(av_mm, v + 1)
                            V.tensor_copy(oT[:, j, s * P:(s + 1) * P], ps[6 + v % 2][:, 0:P]).then_inc(ot_ready, 1)
                    add_mixer(n, [k + 6, k + 7])
                    dve.wait_ge(kv_out, 32)
                elif l == 2:
                    for s in range(S):
                        dve.wait_ge(vsq, s + 1)
                        root_input(6 + s, 8 + s, GDFF, vvar)
                    for s in range(S):
                        dve.wait_ge(vrstd, s + 1)
                        V.tensor_scalar(vg[:, s, :], vg[:, s, :], stat[:, 10 + s:11 + s], None, ALU.mult).then_inc(vn_ready, 1)
                    dve.wait_ge(small_in[2], 32)
                    gv = vec("gv")
                    for g in range(SG):
                        dve.wait_ge(sp_mm, g + 1)
                        for ci in range(2):
                            c = 2 * g + ci
                            link(V.scalar_tensor_tensor(
                                gt[:, ci, :].rearrange("p (s t) -> p s t", s=S),
                                bank(g % 4, 2, T)[:, ci, :].rearrange("p (s t) -> p s t", s=S), gv[:, c:c + 1],
                                bs[:, g, :].unsqueeze(1).to_broadcast([P, S, P]), ALU.mult, ALU.add))
                            last = V.tensor_tensor(uT[:, c, :], uT[:, c, :], gt[:, ci, :], ALU.mult)
                        last.then_inc(sp_ev, 1)
                    add_mixer(n, [k + 9, k + 11])
                else:
                    cw = vec("conv_w")
                    for u in range(16):
                        dve.wait_ge(x_b, u + 1)
                        for tap, (o0, i0, w) in ((0, (2, 0, P - 2)), (1, (1, 0, P - 1)), (3, (0, 1, P - 1))):
                            for m in range(2):
                                c = 2 * u + m
                                x = xbcT[:, c, :].rearrange("p (s t) -> p s t", s=S)
                                src = bank(u % 4, 2, T)[:, m, :].rearrange("p (s t) -> p s t", s=S)
                                last = V.scalar_tensor_tensor(x[:, :, o0:o0 + w], src[:, :, i0:i0 + w], cw[:, tap * 32 + c:tap * 32 + c + 1],
                                                              x[:, :, o0:o0 + w], ALU.mult, ALU.add)
                                if tap < 3:
                                    link(last)
                        last.then_inc(x_cv, 1)
                    dve.wait_ge(slot_done, k + 9)
                    dve.wait_ge(small_in[3], 48)
                    W = lambda q: dtw[:, q, :]
                    W2 = lambda q: dtw[:, q, :].rearrange("p (s h) -> p s h", s=S)
                    both = lambda r: dtb[:, r, :].unsqueeze(1).to_broadcast([P, S, 64])
                    link(V.tensor_tensor(W2(0), bank(4, S, 64), both(0), ALU.add))
                    V.scalar_tensor_tensor(W(1), W(0), -1.0, W(0), ALU.mult, ALU.min).then_inc(dt_abs, 1)
                    dve.wait_ge(dt_exp, 1)
                    V.tensor_scalar(W(3), W(2), 1.0, None, ALU.add).then_inc(dt_abs, 1)
                    dve.wait_ge(dt_abs, 2)
                    link(V.tensor_scalar(W(5), W(3), -1.0, None, ALU.add))
                    link(V.tensor_scalar(W(6), W(5), 0.0, None, ALU.is_equal))
                    link(V.tensor_tensor(W(5), W(5), W(6), ALU.add))
                    link(V.reciprocal(W(5), W(5)))
                    dve.wait_ge(dt_ln, 1)
                    link(V.tensor_tensor(W(4), W(4), W(6), ALU.add))
                    link(V.tensor_tensor(W(4), W(4), W(5), ALU.mult))
                    link(V.tensor_tensor(W(4), W(4), W(2), ALU.mult))
                    link(V.scalar_tensor_tensor(W(7), W(0), 0.0, W(4), ALU.max, ALU.add))
                    dve.wait_ge(a_exp, 1)
                    link(V.tensor_tensor(nadt[:, :, :], W2(7), both(1), ALU.mult))
                    V.tensor_scalar(adt[:, :, :], nadt[:, :, :], -1.0, None, ALU.mult).then_inc(adt_ready, 1)
                    dve.wait_ge(z_ev, 8)
                    dve.wait_ge(edec_ready, 1)
                    tri = [mat("t_le"), mat("t_ge")]
                    heads = lambda x: x.rearrange("p (h e) -> p h e", h=HPG)
                    over = lambda x: x.unsqueeze(2).to_broadcast([P, HPG, HD])

                    def of_group(u):
                        s, g = divmod(u, SG)
                        return s, g, 2 * (u % 2), [slice(d * SH + g * HPG, d * SH + (g + 1) * HPG) for d in range(2)]

                    def group_operands(u):
                        s, g, t, hs = of_group(u)
                        if u >= 2:
                            dve.wait_ge(yg_mm, u - 1)
                        for d in range(2):
                            dve.wait_ge(seg_mm, 2 * u + d + 1)
                            V.tensor_scalar(segs[:, t + d, :], ps[1 + d][:, :], 0.0, None, ALU.min).then_inc(seg_ready, 1)
                        dve.wait_ge(xt_ev, u + 1)
                        x = heads(xtok[:, u % 2, 0:256])
                        for d in range(2):
                            last = V.tensor_tensor(heads(dtx[:, t + d, :]), x, over(W2(7)[:, s, hs[d]]), ALU.mult)
                            if d:
                                last.then_inc(dtx_step, 1)
                        for d in range(2):
                            V.tensor_tensor(cbm[:, t + d, :], xtok[:, u % 2, 384:512], tri[d], ALU.mult).then_inc(cbm_step, 1)
                        dve.wait_ge(dtx_step, u + 1)
                        if s == 0:
                            for d in range(2):
                                last = V.tensor_tensor(heads(dtxw[:, t + d, :]), heads(dtx[:, t + d, :]), over(edec[:, 0, hs[d]]), ALU.mult)
                            last.then_inc(dtx_ready, 1)
                        else:
                            V.memset(stat[:, 27:28], 0.0).then_inc(dtx_ready, 1)
                        for d in range(2):
                            dve.wait_ge(dec_ready, 2 * u + d + 1)
                            dve.wait_ge(cbm_step, 2 * u + d + 1)
                            V.tensor_tensor(heads(segs[:, t + d, :]), heads(segs[:, t + d, :]),
                                            cbm[:, t + d, :].unsqueeze(1).to_broadcast([P, HPG, P]), ALU.mult).then_inc(m_ready, 1)

                    def group_gated(u):
                        s, g, t, hs = of_group(u)
                        if u:
                            dve.wait_ge(y_done, u)
                        link(V.tensor_tensor(heads(yfix[:, 0, :]), heads(xtok[:, u % 2, 0:256]), over(dtb[:, 2, g * HPG:(g + 1) * HPG]), ALU.mult))
                        dve.wait_ge(yg_mm, u + 1)
                        link(V.tensor_tensor(yfix[:, 0, :], yfix[:, 0, :], ps[3][:, 0:256], ALU.add))
                        if s == 1:
                            if g == 0:
                                dve.wait_ge(st_out, 32 * SG)
                            for d in range(2):
                                cols = slice(d * 256, (d + 1) * 256)
                                last = V.tensor_tensor(heads(offs[:, 0, cols]), heads(ps[4][:, cols]), over(edec[:, 1, hs[d]]), ALU.mult)
                            link(last)
                            for d in range(2):
                                link(V.tensor_tensor(yfix[:, 0, :], yfix[:, 0, :], offs[:, 0, d * 256:(d + 1) * 256], ALU.add))
                        zg = zs[:, s, g * 256:(g + 1) * 256]
                        V.tensor_tensor(zg, zg, yfix[:, 0, :], ALU.mult).then_inc(y_done, 1)
                    for i in range(S * SG + 1):
                        if i < S * SG:
                            group_operands(i)
                        if i:
                            group_gated(i - 1)
                    for s in range(S):
                        dve.wait_ge(ysq, s + 1)
                        root_input(12 + s, 14 + s, 2 * D, yvar)
                    dve.wait_ge(y_done, S * SG)
                    for s in range(S):
                        dve.wait_ge(yrstd, s + 1)
                        V.tensor_scalar(zs[:, s, :], zs[:, s, :], stat[:, 16 + s:17 + s], None, ALU.mult).then_inc(yn_ready, 1)
                    add_mixer(n, [k + 14, k + 16])
                norm(n, 1)
                route(n, l)
                build_onehot(n, 0)
                dve.wait_ge(ov_known, n + 1)
                flag = dve.value_load(ovi[0:1, 0:1], min_val=0, max_val=1)
                k = moe_base(n)

                def group(k, i, last_group):
                    seq = order(n, last_group)
                    ks = {w: k + q for q, w in enumerate(seq)}
                    if not last_group:
                        dve.wait_ge(xg_ready, i + (EG * n + 1))
                        build_onehot(n, i + 1)
                    for x in range(XG):
                        dve.wait_ge(sg_ready, i * XG + (E * n + x + 1))
                        if last_group:
                            dve.wait_ge(slot_done, ks[f"U{x}"] + 1)
                        else:
                            dve.wait_ge(slot_done, i * len(seq) + (ks[f"U{x}"] + 1))
                        if x or n:
                            dve.wait_ge(actT_mm, i * XG + (E * n + x))
                        V.scalar_tensor_tensor(actv[:, 0, :], sgl[:, 0, :], weight(i, x), ps[1][:, :], ALU.mult, ALU.mult)\
                            .then_inc(act_ready, 1)
                        if f"A{x}" in ks:
                            per = len(seq)
                            if x:
                                dve.wait_ge(slot_done, i * per + (ks[f"A{x - 1}"] + 1))
                            else:
                                dve.wait_ge(slot_done, i * per + k)
                            sum_block(ks[f"A{x}"], dve_blocks(n) + x, i, per)

                def weight(i, x):
                    return wsl[:, bass.ds(i, 1), x:x + 1].rearrange("p o x -> p (o x)")
                with dve.Fori(0, EG - 1) as i:
                    group(k, i, False)
                group(k + (EG - 1) * len(order(n, False)), EG - 1, True)

                def add_moe(out_sem, base, signal, linked):
                    for s in range(S):
                        for j in range(2):
                            dve.wait_ge(out_sem, base + 2 * s + j + 1)
                            cols = slice(j * 512, (j + 1) * 512)
                            linked(V.tensor_tensor(outtmp[:, j, :], ps[4 + 2 * s + j][:, :], gate[:, 1, s, cols], ALU.mult))
                            V.tensor_tensor(hid[:, s, cols], hid[:, s, cols], outtmp[:, j, :], ALU.add).then_inc(signal, 1)
                with dve.If(flag > 0):
                    O = lambda q: ovs[:, q, :]
                    ch = [n * 64]

                    def vlink(ins):
                        ch[0] += 1
                        ins.then_inc(v_chain, 1)
                        dve.wait_ge(v_chain, ch[0])
                    vlink(V.tensor_tensor(ovs[:, 4:6, :], posr[:, 0:S, :], O(0).unsqueeze(1).to_broadcast([P, S, EG]), ALU.mult))
                    vlink(V.tensor_tensor(ovs[:, 6:8, :], rt[:, 4, :, :], O(0).unsqueeze(1).to_broadcast([P, S, EG]), ALU.mult))
                    vlink(V.tensor_reduce(O(3)[:, 0:2], ovs[:, 4:6, :], AX.X, ALU.add))
                    vlink(V.tensor_reduce(O(3)[:, 2:4], ovs[:, 6:8, :], AX.X, ALU.add))
                    vlink(V.tensor_scalar(O(3)[:, 0:2], O(3)[:, 0:2], -float(P), None, ALU.add))
                    vlink(V.memset(ysb[:, EG, :], 0.0))
                    dve.wait_ge(y_ev, EG * (n + 1))
                    for s in range(S):
                        last = V.tensor_scalar(onehot[:, s, :], mat("iota"), O(3)[:, s:s + 1], O(3)[:, 2 + s:3 + s],
                                               ALU.is_equal, ALU.mult)
                    last.then_inc(v_oh, 1)
                    with dve.Fori(0, XG) as x:
                        dve.wait_ge(v_sg, x + (XG * n + 1))
                        dve.wait_ge(v_gt_ev, n + 1)
                        dve.wait_ge(v_done, x * 3 + (3 * XG * n + 2))
                        dve.wait_ge(v_t, x + XG * n)
                        V.scalar_tensor_tensor(actv[:, 0, :], sgl[:, 0, :], wsl[:, EG, bass.ds(x, 1)], ps[1][:, :], ALU.mult, ALU.mult)\
                            .then_inc(v_act, 1)
                        dve.wait_ge(v_done, x * 3 + (3 * XG * n + 3))
                        dve.wait_ge(v_y_ev, x + XG * n)
                        ys = ysb[:, EG, :].rearrange("p (j n) -> p j n", j=2)
                        V.tensor_tensor(ys, ys, psum[:, 6:8, :], ALU.add).then_inc(v_y_ev, 1)
                    add_moe(v_out, 4 * n, v_added, vlink)
                    dve.wait_ge(v_added, 4 * (n + 1))
                    vlink(V.tensor_copy(O(3), O(0)))
                    V_LINKS = ch[0] - n * 64
                    V.nop().then_inc(v_chain, 64 - V_LINKS)
                with dve.Else():
                    dve.sem_inc(v_oh, 1)
                    dve.sem_inc(v_act, XG)
                    dve.sem_inc(v_y_ev, XG)
                    dve.sem_inc(v_added, 4)
                    dve.sem_inc(v_chain, 64)
                add_moe(out_mm, 4 * n, h_ready, link)
                dve.wait_ge(h_ready, 8 * (n + 1))
            norm(len(LAYERS), 0)


_AS_GIVEN = ["x_prompt", "x_sample", "cache_v", "ada_w", "final_g", "fnet_w_o", "na_w_qkv", "na_w_o",
             "gmlp_w_in", "gmlp_b_s", "gmlp_w_out", "ssd_w_in", "ssd_a_log", "ssd_dt_bias", "ssd_d_skip", "ssd_w_out",
             "moe_b_gr", "moe_b_er", "moe_w_gate", "moe_w_up", "moe_w_down"]
_OUTS = [("y_prompt", (1, P, D)), ("y_sample", (1, P, D)),
         ("new_cache_k", (1, 1, HEADS, P, HD)), ("new_cache_v", (1, 1, HEADS, P, HD)),
         ("new_state_ssm_fwd", (1, 1, SH, HD, P)), ("new_state_ssm_bwd", (1, 1, SH, HD, P))]


def constant_matrices():
    i = np.arange(P)
    r, c = i[:, None], i[None, :]
    angle = 2 * np.pi * ((r * c) % P) / P
    grid_w, win = 64, 16
    qc, kc = r % grid_w, c % grid_w
    w0 = np.clip(qc - win // 2, 0, grid_w - win)
    m = {"iota": c + 0 * r, "ident": r == c, "ones": r >= 0 * c, "t_le": r <= c, "t_ge": r >= c, "t_gt": r > c, "t_lt": r < c,
         "dft_c": np.cos(angle), "dft_s": np.sin(angle), "seq_c": np.cos(angle) / P, "seq_ns": -np.sin(angle) / P,
         "na_mask": np.where((kc >= w0) & (kc < w0 + win), 0.0, -1e30)}
    return np.ascontiguousarray(np.stack([np.broadcast_to(m[k], (P, P)).astype(np.float32) for k in MATS], 1))


def columns(x):
    return np.asarray(x).reshape(-1, P).T


def lay_out(x):
    x = {k: np.asarray(v) for k, v in x.items()}
    arrays = {k: np.ascontiguousarray(x[k]) for k in _AS_GIVEN}
    cond = np.stack([x["c_ctx"].reshape(DC, P), x["c"][0].reshape(DC, P)], 1)
    packed = {"g1": columns(x["norm1_g"]), "g2": columns(x["norm2_g"]), "ada_b": columns(x["ada_b"]),
              "cond": columns(cond), "gv": columns(x["gmlp_g_v"]), "gn": columns(x["ssd_g_norm"]),
              "conv_w": columns(x["ssd_conv_w"]), "conv_b": columns(x["ssd_conv_b"])}
    arrays["vecs"] = np.ascontiguousarray(np.concatenate([packed[k] for k, _ in VECS], 1))
    arrays["mats"] = constant_matrices()
    arrays["wgr"] = np.ascontiguousarray(x["moe_w_gr"].reshape(DEPTH, DC, P, EG).transpose(2, 0, 1, 3))
    arrays["wer"] = np.ascontiguousarray(x["moe_w_er"].reshape(DEPTH, DC, P, E).transpose(2, 0, 1, 3))
    i = np.arange(P)
    rr = (i[None, :] // 64) - (i[:, None] // 64) + 7
    cc = np.clip((i[None, :] % 64) - (i[:, None] % 64), -15, 15) + 15
    arrays["rpb_band"] = np.ascontiguousarray(x["na_rpb"][0][:, rr, cc].transpose(1, 0, 2))
    arrays["cache_kT"] = np.ascontiguousarray(x["cache_k"][0, 0].reshape(DC, 2, P, HD).transpose(1, 3, 0, 2).reshape(P, DC, P))
    arrays["wsT"] = np.ascontiguousarray(x["gmlp_w_s"][0].transpose(2, 0, 1))
    arrays["h0T"] = np.ascontiguousarray(
        np.stack([x["state_ssm_fwd"][0, 0].reshape(2 * D, P).T, x["state_ssm_bwd"][0, 0].reshape(2 * D, P).T], 1))
    return arrays


def kernel(**inputs):
    import concourse.bacc as _bacc
    from concourse.bass_utils import run_bass_kernel_spmd as _run

    nc = _bacc.Bacc("TRN2", target_bir_lowering=False, num_devices=1)
    given = lay_out(inputs)
    arrays = {f"in_{k}": v for k, v in given.items()}
    a = {k: nc.dram_tensor(f"in_{k}", v.shape, mybir.dt.from_np(v.dtype), kind="ExternalInput").ap() for k, v in given.items()}
    o = {k: nc.dram_tensor(f"out_{k}", shape, FP32, kind="ExternalOutput").ap() for k, shape in _OUTS}
    build(nc, a, o)
    r = _run(nc, [arrays], core_ids=[0])
    return tuple(r.results[0][f"out_{k}"] for k, _ in _OUTS)
```

```python
import numpy as np
import concourse.bass as bass
from concourse import mybir
from contextlib import ExitStack

FP32 = mybir.dt.float32
ALU = mybir.AluOpType
ACT = mybir.ActivationFunctionType
AX = mybir.AxisListType

P = 128
D = 1024
DC = D // P
S = 2
T = S * P
DEPTH = 4
EPS = 1e-6
RING = 4
SLOT_COLS = 512
NMOD = 6
HEADS = 16
HD = 64
E = 16
EG = 4
FF = 512
NR = EG + E
GDFF = 2048
SG = 8
HPG = 4
SH = 32
XBC = 4096
ARENA = 15616
LAYERS = (0, 1, 2, 3)
Y_BANKS = ((5, 6, 7, 5), (0, 1, 2, 3))

XG = E // EG
ADA_LOADS = NMOD * D // SLOT_COLS
MOE_LOADS = 3 * E
PLAIN = ["G0", "U0", "G1", "U1", "D0", "G2", "U2", "D1", "G3", "U3", "D2", "D3"]
MIXED = ["G0", "U0", "G1", "U1", "A0", "D0", "G2", "U2", "A1", "D1", "G3", "U3", "A2", "D2", "A3", "D3"]
GMLP_IN = [f"{w}{j}" for j in range(8) for w in "IA"]
GMLP_OUT = ["O0", "A8", "O1", "A9", "A10", "O2", "A11", "O3"]
GMLP_AT = {w: q for q, w in enumerate(GMLP_IN + GMLP_OUT)}
assert all(f"A{x}" in GMLP_AT for x in range(ADA_LOADS))
EARLY = {LAYERS.index(2)}
MIX_LOADS = {0: 2, 1: 8, 2: len(GMLP_AT), 3: 17}

VECS = [("g1", DEPTH * DC), ("g2", DEPTH * DC), ("ada_b", DEPTH * NMOD * DC), ("cond", DC * S),
        ("gv", GDFF // P), ("gn", 2 * D // P), ("conv_w", 4 * XBC // P), ("conv_b", XBC // P)]
VEC_AT, _n = {}, 0
for _name, _w in VECS:
    VEC_AT[_name] = (_n, _w)
    _n += _w
VEC_COLS = _n
MATS = ["ident", "ones", "t_le", "t_ge", "t_gt", "t_lt", "dft_c", "dft_s", "seq_c", "seq_ns", "na_mask", "iota"]
MAT_AT = {m: i for i, m in enumerate(MATS)}


def build(nc, a, o):
    ctx = ExitStack()
    with ctx:
        def sb(name, shape):
            return ctx.enter_context(nc.sbuf_tensor(name, shape, FP32))

        def sem(name):
            return ctx.enter_context(nc.semaphore(name))

        ring = sb("ring", [P, RING, DC * SLOT_COLS])
        hid = sb("hid", [P, S, D])
        xn = sb("xn", [P, S, D])
        at = sb("at", [P, DC, T])
        gate = sb("gate", [P, 2, S, D])
        acc = sb("acc", [P, S, D])
        mats = sb("mats", [P, len(MATS), P])
        vecs = sb("vecs", [P, VEC_COLS])
        cond = sb("condT", [P, DC, S])
        adkept = sb("adkept", [P, NMOD * DC, S])
        modt = sb("modt", [P, NMOD * DC, S])
        gsc = sb("gsc", [P, 2, DC, S])
        wr = sb("wr", [P, DEPTH, DC, NR])
        rbias = sb("rbias", [P, DEPTH, NR])
        first = sb("first", [P, EG])
        finalg = sb("finalg", [P, D])
        stat = sb("stat", [P, 32])
        outtmp = sb("outtmp", [P, 2, SLOT_COLS])
        adacc = outtmp
        rt = sb("rt", [P, 24, S, EG])
        rlog = sb("rlog", [P, S, NR])
        rsel = sb("rsel", [P, S, EG, EG])
        posr = sb("posr", [P, S + 1, EG])
        ovi = ctx.enter_context(nc.sbuf_tensor("ovi", [P, 2], mybir.dt.int32))
        ovs = sb("ovs", [P, 8, EG])
        arena = sb("arena", [P, ARENA])

        def carve(at0, *shape):
            n = int(np.prod(shape))
            assert at0 + n <= ARENA, (at0, n)
            v = arena[:, at0:at0 + n]
            if len(shape) == 2:
                v = v.rearrange("p (a b) -> p a b", a=shape[0])
            elif len(shape) == 3:
                v = v.rearrange("p (a b c) -> p a b c", a=shape[0], b=shape[1])
            return v

        xg = carve(0, DC, P)
        onehot = carve(1024, S, P)
        ghT = carve(1280, EG + 1, T)
        ysb = carve(2560, EG + 1, D)
        sgl = carve(7680, 1, FF)
        actv = carve(8192, 1, FF)
        actT = carve(8704, FF // P, P)
        wsl = carve(9216, EG + 1, XG)
        wov = carve(9280, DC, SLOT_COLS)
        adarow = carve(0, 1, SLOT_COLS)
        f1 = carve(0, 2, 512)
        ft = carve(1024, DC, T)
        qT = carve(0, DC, T)
        kT = carve(2048, DC, T)
        vtok = carve(4096, S, D)
        kcT = carve(6144, DC, P)
        vctx = carve(7168, 1, D)
        rpb = carve(8192, HEADS, P)
        oT = carve(10240, DC, T)
        prob = carve(12288, 3, 512)
        probT = carve(13824, 2, 512)
        nmax = carve(14848, 16, 2)
        esum = carve(14880, 16, 2)
        rsum = carve(14912, 16, 2)
        uT = carve(0, 16, T)
        vg = carve(4096, S, GDFF)
        wsT = carve(8192, SG, P)
        bs = carve(9216, SG, P)
        adacc2 = carve(11264, S, SLOT_COLS)
        gt = carve(10240, 2, T)
        xbcT = carve(0, 32, T)
        zs = carve(8192, S, 2 * D)
        segs = carve(12288, 4, 512)
        ttri = carve(14336, 2, 512)
        yfix = carve(15360, 1, 256)
        xtok = acc[:, 0, :].rearrange("p (u n) -> p u n", u=2)
        cbm = outtmp[:, 1, :].rearrange("p (u n) -> p u n", u=4)
        dtx = acc[:, 1, :].rearrange("p (u n) -> p u n", u=4)
        dtxw = xn[:, 0, :].rearrange("p (u n) -> p u n", u=4)
        stout = gate[:, 1, 0, :].rearrange("p (u n) -> p u n", u=2)
        ttri2 = gate[:, 1, 1, :].rearrange("p (d n) -> p d n", d=2)
        offs = outtmp[:, 0:1, :]
        h0 = xn[:, 1, :].rearrange("p (u n) -> p u n", u=2)
        dtw = sb("dtw", [P, 8, S * 64])
        adt = sb("adt", [P, S, 64])
        nadt = sb("nadt", [P, S, 64])
        edec = sb("edec", [P, 2, 64])
        dtb = sb("dtb", [P, 3, 64])

        psum = ctx.enter_context(nc.psum_tensor("psum", [P, 8, 512], FP32))
        ps = [psum[:, i, :] for i in range(8)]

        def bank(i, *shape):
            v = ps[i][:, :int(np.prod(shape))]
            if len(shape) == 2:
                v = v.rearrange("p (a b) -> p a b", a=shape[0])
            elif len(shape) == 3:
                v = v.rearrange("p (a b c) -> p a b c", a=shape[0], b=shape[1])
            return v

        def vec(name):
            n, w = VEC_AT[name]
            return vecs[:, n:n + w]

        def mat(name):
            return mats[:, MAT_AT[name], :]

        def slot(k):
            return ring[:, k % RING, :].rearrange("p (c n) -> p c n", c=DC)

        def slot_down(k):
            return ring[:, k % RING, :].rearrange("p (c n) -> p c n", c=FF // P)

        full = [sem(f"ring_full{i}") for i in range(RING)]
        slot_done = sem("slot_done")
        vecs_in, mats_in, consts_in = sem("vecs_in"), sem("mats_in"), sem("consts_in")
        small_in = {i: sem(f"small_in{i}") for i in (1, 2, 3)}
        cond_ready = sem("cond_ready")
        ada_step, ada_ev = sem("ada_step"), sem("ada_ev")
        ada_kept = sem("ada_kept")
        row_mm, row_ev = sem("ada_row_mm"), sem("ada_row_ev")
        gsc_ready = sem("gsc_ready")
        gate_mm, gate_ev = sem("gate_mm"), sem("gate_ev")
        sq_done, var_ready, rstd_ready, xn_ready = sem("sq_done"), sem("var_ready"), sem("rstd_ready"), sem("xn_ready")
        tr_mm, at_act, at_dve = sem("tr_mm"), sem("at_act"), sem("at_dve")
        o_mm, h_ready = sem("o_mm"), sem("h_ready")
        route_mm = sem("route_mm")
        rexp = sem("router_exp_ready")
        rexp_in = sem("router_exp_in")
        tok_mm, tok_ev = sem("tok_mm"), sem("tok_ev")
        pos_mm, oh_ready, ov_known = sem("pos_mm"), sem("group_onehot_ready"), sem("ov_known")
        onehot_ready, gt_mm, gt_ev = sem("onehot_ready"), sem("gt_mm"), sem("gt_ev")
        xg_mm, xg_ready = sem("xg_mm"), sem("xg_ready")
        sg_ready, act_ready, actT_mm, actT_ev = sem("sg_ready"), sem("act_ready"), sem("actT_mm"), sem("actT_ev")
        y_ev, out_mm = sem("y_ev"), sem("out_mm")
        v_oh, v_gt, v_gt_ev, v_xg, v_xg_ev = sem("v_oh"), sem("v_gt"), sem("v_gt_ev"), sem("v_xg"), sem("v_xg_ev")
        v_w, v_done, v_sg, v_act, v_t, v_t_ev = sem("v_w"), sem("v_done"), sem("v_sg"), sem("v_act"), sem("v_t"), sem("v_t_ev")
        v_chain = sem("v_chain")
        v_y_ev, v_out, v_added = sem("v_y_ev"), sem("v_out"), sem("v_added")
        dve_chain, pool_chain = sem("dve_chain"), sem("pool_chain")
        f1_mm, f1_ev, f2_mm, ft_ready = sem("f1_mm"), sem("f1_ev"), sem("f2_mm"), sem("ft_ready")
        qk_mm, qk_ev, v_mm, v_ev = sem("qk_mm"), sem("qk_ev"), sem("v_mm"), sem("v_ev")
        kt_mm, kt_ev = sem("ktok_mm"), sem("ktok_ev")
        s_mm, nm_ready, e_ready, p_ready = sem("scores_mm"), sem("nmax_ready"), sem("exp_ready"), sem("prob_ready")
        t_mm, pt_ready, av_mm, ot_ready = sem("probT_mm"), sem("probT_ready"), sem("av_mm"), sem("oT_ready")
        m_mm, m_ev = sem("gmlp_mm"), sem("gmlp_ev")
        vsq, vvar, vrstd, vn_ready = sem("v_sq"), sem("v_var"), sem("v_rstd"), sem("vn_ready")
        sp_mm, sp_ev = sem("spatial_mm"), sem("gated_ready")
        x_mm, x_b, x_cv, x_act = sem("xbc_mm"), sem("xbc_tap"), sem("xbc_conv"), sem("xbc_ready")
        dt_exp, dt_ln = sem("dt_exp"), sem("dt_ln")
        dt_abs, a_exp = sem("dt_abs"), sem("a_exp")
        adt_ready, cum_mm, edec_ready = sem("adt_ready"), sem("cum_mm"), sem("edec_ready")
        z_mm, z_ev = sem("z_mm"), sem("z_ev")
        xt_mm, xt_ev, tt_ready = sem("xtok_mm"), sem("xtok_ev"), sem("tri_dt_ready")
        seg_mm, seg_ready, dec_ready, m_ready = sem("seg_mm"), sem("seg_ready"), sem("decay_ready"), sem("mix_ready")
        dtx_step, cbm_step = sem("dtx_step"), sem("cbm_step")
        dtx_ready, yg_mm, y_done = sem("dtx_ready"), sem("yg_mm"), sem("y_done")
        off_ev = sem("off_ev")
        st_out = [sem("states_out_even"), sem("states_out_odd")]
        h0_in = [sem("h0_in_even"), sem("h0_in_odd")]
        yt_dve = sem("yT_dve_ready")
        ysq, yvar, yrstd, yn_ready, yt_mm, yt_ev = (sem("y_sq"), sem("y_var"), sem("y_rstd"), sem("yn_ready"),
                                                     sem("yT_mm"), sem("yT_ready"))
        kv_out, fin_ready, fin_out = sem("kv_out"), sem("fin_ready"), sem("fin_out")

        def moe_loads(n):
            return MOE_LOADS + (ADA_LOADS if n + 1 < len(LAYERS) and n not in EARLY else 0)

        def mix_base(n):
            return ADA_LOADS + sum(MIX_LOADS[x] + moe_loads(i) for i, x in enumerate(LAYERS[:n]))

        def moe_base(n):
            return mix_base(n) + MIX_LOADS[LAYERS[n]]

        def order(n, last):
            return PLAIN if last or n + 1 == len(LAYERS) or n in EARLY else MIXED

        def dve_blocks(n):
            return ADA_LOADS // 2 + ADA_LOADS * n

        def gate_bank(which, s, h):
            return 4 + 2 * h + s if which else 4 + 2 * s + h

        def block_of(w, rows0, cols):
            return w[rows0:rows0 + D, cols].rearrange("(c p) n -> p c n", p=P)

        ctx.enter_context(nc.allow_non_contiguous_dma("small constants, weight blocks by rows"))
        block = ctx.enter_context(nc.Block())

        @block.sync
        def _(sp):
            def load(k, dst, src, i=None, per=0):
                if i is not None:
                    sp.wait_ge(slot_done, i * per + (k - RING + 1))
                elif k >= RING:
                    sp.wait_ge(slot_done, k - RING + 1)
                sp.dma_start(dst, src).then_inc(full[k % RING], 16)

            for n, l in enumerate(LAYERS):
                if n == 0:
                    for j in range(ADA_LOADS):
                        load(j, slot(j), block_of(a["ada_w"][l], 0, slice(j * SLOT_COLS, (j + 1) * SLOT_COLS)))
                k = mix_base(n)
                if l == 0:
                    todo = [(a["fnet_w_o"][0], 0, j) for j in range(2)]
                elif l == 1:
                    todo = [(a["na_w_qkv"][0], 0, j) for j in range(6)] + [(a["na_w_o"][0], 0, j) for j in range(2)]
                elif l == 2:
                    mats_of = {"I": lambda j: (a["gmlp_w_in"][0], 0, j), "A": lambda j: (a["ada_w"][LAYERS[n + 1]], 0, j),
                               "O": lambda j: (a["gmlp_w_out"][0], j % 2 * D, j // 2)}
                    todo = [mats_of[w[0]](int(w[1:])) for w in GMLP_IN + GMLP_OUT]
                else:
                    todo = [(a["ssd_w_in"][0], 0, 4 + j) for j in range(8)] + [None]
                    todo += [(a["ssd_w_in"][0], 0, j) for j in range(4)]
                    todo += [(a["ssd_w_out"][0], kk * D, j) for j in range(2) for kk in range(2)]
                for q, it in enumerate(todo):
                    if it is None:
                        load(k + q, slot(k + q)[:, :, 0:64], block_of(a["ssd_w_in"][0], 0, slice(2 * D + XBC, 2 * D + XBC + 64)))
                    else:
                        w, r0, j = it
                        load(k + q, slot(k + q), block_of(w, r0, slice(j * SLOT_COLS, (j + 1) * SLOT_COLS)))
                assert len(todo) == MIX_LOADS[l]
                k = moe_base(n)

                def group_loads(k, i, last):
                    seq = order(n, last)
                    for q, (what, x) in enumerate(seq):
                        x = int(x)
                        if what == "A":
                            cols = bass.ds(i * (XG * SLOT_COLS) + x * SLOT_COLS, SLOT_COLS)
                            src, dst = block_of(a["ada_w"][LAYERS[n + 1]], 0, cols), slot(k + q)
                        else:
                            w = a[{"G": "moe_w_gate", "U": "moe_w_up", "D": "moe_w_down"}[what]][l]
                            rows = w.rearrange("e (c p) n -> e p c n", p=P)
                            src = rows[bass.ds(i * XG + x, 1)].rearrange("o p c n -> p (o c) n")
                            dst = slot_down(k + q) if what == "D" else slot(k + q)
                        if last:
                            load(k + q, dst, src)
                        else:
                            load(k + q, dst, src, i, len(seq))
                with sp.Fori(0, EG - 1) as i:
                    group_loads(k, i, False)
                group_loads(k + (EG - 1) * len(order(n, False)), EG - 1, True)
                sp.wait_ge(ov_known, n + 1)
                flag = sp.value_load(ovi[0:1, 0:1], min_val=0, max_val=1)
                base = sp.value_load(ovi[0:1, 1:2], min_val=0, max_val=E - XG)
                with sp.If(flag > 0):
                    sp.wait_ge(v_oh, n + 1)
                    for x in range(XG):
                        for q, w in enumerate(("moe_w_gate", "moe_w_up", "moe_w_down")):
                            if n or x or q:
                                sp.wait_ge(v_done, 3 * (XG * n + x) + q)
                            rows = a[w][l].rearrange("e (c p) n -> e p c n", p=P)[bass.ds(base + x, 1)]
                            dst = wov if q < 2 else wov.rearrange("p c n -> p (c n)").rearrange("p (c n) -> p c n", c=FF // P)
                            sp.dma_start(dst, rows.rearrange("o p c n -> p (o c) n")).then_inc(v_w, 16)
                with sp.Else():
                    sp.sem_inc(v_w, 16 * 3 * XG)

        @block.gpsimd
        def _(pool):
            pool.dma_start(vecs[:, :], a["vecs"]).then_inc(vecs_in, 16)
            pool.dma_start(mats[:, :, :], a["mats"]).then_inc(mats_in, 16)
            pool.dma_start(hid[:, 0, :], a["x_prompt"][0]).then_inc(consts_in, 16)
            pool.dma_start(hid[:, 1, :], a["x_sample"][0]).then_inc(consts_in, 16)
            pool.dma_start(wr[:, :, :, 0:EG], a["wgr"]).then_inc(consts_in, 16)
            pool.dma_start(wr[:, :, :, EG:NR], a["wer"]).then_inc(consts_in, 16)
            pool.dma_start(rbias[:, :, 0:EG], a["moe_b_gr"].partition_broadcast(P)).then_inc(consts_in, 16)
            pool.dma_start(rbias[:, :, EG:NR], a["moe_b_er"].partition_broadcast(P)).then_inc(consts_in, 16)
            pool.dma_start(finalg[:, :], a["final_g"].partition_broadcast(P)).then_inc(consts_in, 16)
            for j in range(EG):
                pool.memset(first[:, j:j + 1], float(EG - j)).then_inc(pool_chain, 1)
            for n, l in enumerate(LAYERS):
                if l in small_in:
                    if n:
                        pool.wait_ge(h_ready, 8 * n)
                if l == 1:
                    pool.dma_start(rpb, a["rpb_band"]).then_inc(small_in[1], 16)
                    pool.dma_start(kcT, a["cache_kT"]).then_inc(small_in[1], 16)
                    pool.dma_start(vctx[:, 0, :].rearrange("p (h d) -> p h d", h=HEADS),
                                   a["cache_v"][0, 0].rearrange("h t d -> t h d")).then_inc(small_in[1], 16)
                    pool.wait_ge(v_ev, S * 2)
                    pool.dma_start(o["new_cache_v"][0, 0].rearrange("h t d -> t h d"),
                                   vtok[:, 0, :].rearrange("p (h d) -> p h d", h=HEADS)).then_inc(kv_out, 16)
                    pool.wait_ge(kt_ev, 2)
                    pool.dma_start(o["new_cache_k"][0, 0].rearrange("h t d -> t h d"),
                                   xn[:, 0, :].rearrange("p (h d) -> p h d", h=HEADS)).then_inc(kv_out, 16)
                if l == 2:
                    pool.dma_start(wsT, a["wsT"]).then_inc(small_in[2], 16)
                    pool.dma_start(bs, a["gmlp_b_s"][0].partition_broadcast(P)).then_inc(small_in[2], 16)
                if l == 3:
                    pool.dma_start(dtb[:, 0, :], a["ssd_dt_bias"][0].rearrange("a b -> (a b)").partition_broadcast(P)).then_inc(small_in[3], 16)
                    pool.dma_start(dtb[:, 1, :], a["ssd_a_log"][0].rearrange("a b -> (a b)").partition_broadcast(P)).then_inc(small_in[3], 16)
                    pool.dma_start(dtb[:, 2, 0:SH], a["ssd_d_skip"][0].partition_broadcast(P)).then_inc(small_in[3], 16)
                    pool.wait_ge(adt_ready, 1)
                    tri = [mat("t_le"), mat("t_ge")]
                    for u in range(S * SG):
                        s, g = divmod(u, SG)
                        if u >= 2:
                            pool.wait_ge(seg_mm, 2 * (u - 1))
                        for d in range(2):
                            pool.tensor_tensor(
                                (ttri2 if u % 2 else ttri)[:, d, :].rearrange("p (h l) -> p h l", h=HPG),
                                tri[d].unsqueeze(1).to_broadcast([P, HPG, P]),
                                adt[:, s, d * SH + g * HPG:d * SH + (g + 1) * HPG].unsqueeze(2).to_broadcast([P, HPG, P]),
                                ALU.mult).then_inc(tt_ready, 1)
                        if s == 1:
                            if g >= 2:
                                pool.wait_ge(yg_mm, u - 1)
                            pool.dma_start(h0[:, g % 2, :].rearrange("p (d n) -> p d n", d=2),
                                           a["h0T"][:, :, g * 256:(g + 1) * 256]).then_inc(h0_in[g % 2], 16)
                        if 2 <= u <= SG + 1:
                            pool.wait_ge(off_ev, u - 1)
                            for d, name in enumerate(("new_state_ssm_fwd", "new_state_ssm_bwd")):
                                pool.dma_start(
                                    o[name][0, 0, (u - 2) * HPG:(u - 1) * HPG].rearrange("(a b) p n -> (b p) a n", a=2),
                                    stout[:, u % 2, d * 256:(d + 1) * 256].rearrange("p (a n) -> p a n", a=2)).then_inc(st_out[u % 2], 16)
            for s in range(S):
                pool.wait_ge(fin_ready, s + 1)
                pool.dma_start(o["y_prompt" if s == 0 else "y_sample"][0], xn[:, s, :]).then_inc(fin_out, 16)
            pool.wait_ge(fin_out, 16 * S)
            if 1 in LAYERS:
                pool.wait_ge(kv_out, 32)
            if 3 in LAYERS:
                for e in range(2):
                    pool.wait_ge(st_out[e], 32 * SG // 2)

        @block.tensor
        def _(pe):
            def arrive(k, i=None, per=0):
                if i is None:
                    pe.wait_ge(full[k % RING], 16 * (k // RING + 1))
                else:
                    pe.wait_ge(full[k % RING], i * (16 * per // RING) + 16 * (k // RING + 1))

            def dense_chan(k, m, dst, src=at, nk=DC):
                for c in range(nk):
                    last = nc.tensor.matmul(dst, slot(k)[:, c, m * P:(m + 1) * P], src[:, c, :],
                                            start=(c == 0), stop=(c == nk - 1))
                return last

            def dense_tok(k, s, dst, src=at, c0=0, nk=DC, start=True, stop=True, cols=SLOT_COLS, wc0=0):
                for c in range(nk):
                    last = nc.tensor.matmul(dst, src[:, c0 + c, s * P:(s + 1) * P], slot(k)[:, wc0 + c, 0:cols],
                                            start=(start and c == 0), stop=(stop and c == nk - 1))
                return last

            def out_proj(n, k, src, halves, between=lambda block: None):
                pe.wait_ge(gate_ev, 8 * n + 4)
                for j in range(2):
                    for kk in range(halves):
                        arrive(k)
                        for s in range(S):
                            last = dense_tok(k, s, ps[4 + 2 * j + s][:, :], src, kk * DC, DC, kk == 0, kk == halves - 1)
                            if kk == halves - 1 and s == 0:
                                last.then_inc(o_mm, 1)
                        last.then_inc(slot_done, 1)
                        k += 1 + (between(j * halves + kk) or 0)

            def ada_rows(k):
                for c in range(DC):
                    last = nc.tensor.matmul(ps[4][0:S, :], cond[:, c, :], slot(k)[:, c, :], start=(c == 0), stop=(c == DC - 1))
                last.then_inc(row_mm, 1)

            def ada_turned(dst):
                for m in range(4):
                    last = nc.tensor.transpose(dst[:, m * S:(m + 1) * S], adarow[0:S, 0, m * P:(m + 1) * P],
                                               mats[0:S, MAT_AT["ident"], 0:S])
                last.then_inc(slot_done, 1)

            def ada_sums(dst, sums=adacc):
                for m in range(4):
                    for q in range(S):
                        last = nc.tensor.matmul(dst[:, m * S + q:m * S + q + 1], sums[:, q, m * P:(m + 1) * P],
                                                mats[:, MAT_AT["ones"], 0:1], start=True, stop=True)
                last.then_inc(slot_done, 1)

            def h_steps(n, which, s):
                return 8 * n + ((3, 4)[s] if which else (-2, 0)[s])

            def norm_transposes(n, which):
                t = 2 * n + which
                for s in range(S):
                    pe.wait_ge(xn_ready, S * t + s + 1)
                    for h in range(2):
                        for c in range(4):
                            last = nc.tensor.transpose(bank(2 * s + h, 4, P)[:, c, :],
                                                       xn[:, s, (4 * h + c) * P:(4 * h + c + 1) * P], mat("ident"))
                        last.then_inc(tr_mm, 1)
                    if h_steps(n, which, s) > 0:
                        pe.wait_ge(h_ready, h_steps(n, which, s))
                    for h in range(2):
                        for c in range(4):
                            col = (3 * which + 2) * DC + 4 * h + c
                            last = nc.tensor.matmul(bank(gate_bank(which, s, h), 4, P)[:, c, :],
                                                    modt[:, col, s:s + 1].to_broadcast([P, P]), mat("ident"), start=True, stop=True)
                        last.then_inc(gate_mm, 1)

            pe.wait_ge(vecs_in, 16)
            pe.wait_ge(cond_ready, 1)
            for n, l in enumerate(LAYERS):
                if n == 0:
                    for j in range(ADA_LOADS):
                        if j % 2:
                            pe.wait_ge(ada_step, 16 * (j // 2 + 1))
                            if j == 1:
                                pe.wait_ge(mats_in, 16)
                            ada_sums(bank(3, ADA_LOADS, 4 * S)[:, j, :])
                        else:
                            arrive(j)
                            if j:
                                pe.wait_ge(row_ev, j // 2)
                            ada_rows(j)
                            pe.wait_ge(mats_in, 16)
                            pe.wait_ge(row_ev, j // 2 + 1)
                            ada_turned(bank(3, ADA_LOADS, 4 * S)[:, j, :])
                    pe.wait_ge(consts_in, 16 * 7)
                pe.wait_ge(ada_ev, n + 1)
                norm_transposes(n, 0)
                pe.wait_ge(at_act, S * (2 * n + 1))
                pe.wait_ge(at_dve, S * (2 * n + 1))
                k = mix_base(n)
                if l == 0:
                    def fourier_rows(u):
                        s, gp = divmod(u, 4)
                        if u >= 2:
                            pe.wait_ge(f1_ev, u - 1)
                        for gi in range(2):
                            last = nc.tensor.matmul(bank(u % 2, 2, 256)[:, gi, :], at[:, 2 * gp + gi, s * P:(s + 1) * P],
                                                    mats[:, MAT_AT["dft_c"]:MAT_AT["dft_c"] + 2, :].rearrange("p a b -> p (a b)"),
                                                    start=True, stop=True)
                        last.then_inc(f1_mm, 1)

                    def fourier_cols(u):
                        pe.wait_ge(f1_ev, u + 1)
                        if u >= 2:
                            pe.wait_ge(ft_ready, u - 1)
                        for gi in range(2):
                            dst = bank(2 + u % 2, 2, P)[:, gi, :]
                            src = f1[:, u % 2, :].rearrange("p (g x c) -> p g x c", g=2, x=2)
                            nc.tensor.matmul(dst, src[:, gi, 0, :], mat("seq_c"), start=True, stop=False)
                            last = nc.tensor.matmul(dst, src[:, gi, 1, :], mat("seq_ns"), start=False, stop=True)
                        last.then_inc(f2_mm, 1)
                    for u in range(9):
                        if u < 8:
                            fourier_rows(u)
                        if u >= 1:
                            fourier_cols(u - 1)
                    pe.wait_ge(ft_ready, 8)
                    out_proj(n, k, ft, 1)
                elif l == 1:
                    for j in range(4):
                        arrive(k)
                        for mh in range(2):
                            u = 2 * j + mh
                            if u >= 4:
                                pe.wait_ge(qk_ev, u - 3)
                            for m in range(2):
                                last = dense_chan(k, 2 * mh + m, bank(u % 4, 2, T)[:, m, :])
                            last.then_inc(slot_done if mh else qk_mm, 1)
                        k += 1
                    for j in range(2):
                        arrive(k)
                        for s in range(S):
                            b = 2 * j + s
                            pe.wait_ge(qk_ev, 5 + b)
                            last = dense_tok(k, s, ps[b][:, :])
                            last.then_inc(slot_done if s else v_mm, 1)
                        k += 1
                    pe.wait_ge(gate_ev, 8 * n + 4)
                    for h in range(2):
                        for c in range(4):
                            last = nc.tensor.transpose(bank(4 + h, 4, P)[:, c, :], kT[:, 4 * h + c, 0:P], mat("ident"))
                        last.then_inc(kt_mm, 1)
                    pe.wait_ge(small_in[1], 48)
                    pe.wait_ge(kt_ev, 2)
                    pe.wait_ge(v_ev, 4)

                    def scores(u):
                        s, j = divmod(u, DC)
                        if u >= 2:
                            pe.wait_ge(e_ready, u - 1)
                        dst = psum[:, 2 * (u % 2):2 * (u % 2) + 2, :]
                        for hh in range(2):
                            r = slice(HD * hh, HD * (hh + 1))
                            last = nc.tensor.matmul(dst[:, hh, 0:P], qT[r, j, s * P:(s + 1) * P], kT[r, j, s * P:(s + 1) * P],
                                                    start=True, stop=True)
                            if s:
                                last = nc.tensor.matmul(dst[:, hh, P:2 * P], qT[r, j, P:2 * P], kcT[r, j, :], start=True, stop=True)
                        last.then_inc(s_mm, 1)

                    def prob_transposes(u):
                        s, j = divmod(u, DC)
                        pe.wait_ge(p_ready, u + 1)
                        if u >= 2:
                            pe.wait_ge(pt_ready, u - 1)
                        for b in range(2 * (1 + s)):
                            last = nc.tensor.transpose(bank(4 + u % 2, 4, P)[:, b, :],
                                                       prob[:, u % 3, b * P:(b + 1) * P], mat("ident"))
                        last.then_inc(t_mm, 1)

                    def weighted_values(u):
                        s, j = divmod(u, DC)
                        pe.wait_ge(pt_ready, u + 1)
                        if u >= 2:
                            pe.wait_ge(ot_ready, u - 1)
                        pT = probT[:, u % 2, :].rearrange("p (b q) -> p b q", b=4)
                        for hh in range(2):
                            cols = slice((2 * j + hh) * HD, (2 * j + hh + 1) * HD)
                            dst = ps[6 + u % 2][HD * hh:HD * (hh + 1), 0:P]
                            last = nc.tensor.matmul(dst, vtok[:, s, cols], pT[:, hh * (1 + s), :], start=True, stop=(s == 0))
                            if s:
                                last = nc.tensor.matmul(dst, vctx[:, 0, cols], pT[:, 2 * hh + 1, :], start=False, stop=True)
                        last.then_inc(av_mm, 1)
                    U = S * DC
                    for i in range(U + 3):
                        if i < U:
                            scores(i)
                        if 2 <= i <= U + 1:
                            prob_transposes(i - 2)
                        if i >= 3:
                            weighted_values(i - 3)
                    pe.wait_ge(ot_ready, U)
                    out_proj(n, k, oT, 1)
                elif l == 2:
                    def early_sums(x, b):
                        pe.wait_ge(ada_step, 16 * (dve_blocks(n) + x + 1))
                        ada_sums(bank(b, ADA_LOADS, 4 * S)[:, x, :], adacc2 if x % 2 else adacc)

                    def between(block):
                        q = GMLP_OUT.index(f"O{block}") + 1
                        count = 0
                        while q < len(GMLP_OUT) and GMLP_OUT[q][0] == "A":
                            early_sums(int(GMLP_OUT[q][1:]), 3)
                            count, q = count + 1, q + 1
                        return count
                    for w in GMLP_IN:
                        j = int(w[1:])
                        if w[0] == "A":
                            if j == 0:
                                pe.wait_ge(gate_ev, 8 * n + 4)
                            early_sums(j, 7)
                        else:
                            arrive(k)
                            for x in range(2):
                                u = 2 * j + x
                                if u >= 4:
                                    pe.wait_ge(m_ev, u - 3)
                                if j < 4:
                                    for m in range(2):
                                        last = dense_chan(k, 2 * x + m, bank(u % 4, 2, T)[:, m, :])
                                else:
                                    last = dense_tok(k, x, ps[u % 4][:, :])
                                last.then_inc(slot_done if x else m_mm, 1)
                        k += 1
                    pe.wait_ge(small_in[2], 32)
                    pe.wait_ge(vn_ready, S)
                    for g in range(SG):
                        if g >= 4:
                            pe.wait_ge(sp_ev, g - 3)
                        for ci in range(2):
                            for s in range(S):
                                c = 2 * g + ci
                                last = nc.tensor.matmul(bank(g % 4, 2, T)[:, ci, s * P:(s + 1) * P],
                                                        vg[:, s, c * P:(c + 1) * P], wsT[:, g, :], start=True, stop=True)
                        last.then_inc(sp_mm, 1)
                    pe.wait_ge(sp_ev, SG)
                    pe.wait_ge(ada_kept, 1)
                    out_proj(n, k, uT, 2, between)
                    pe.wait_ge(ada_kept, 2)
                else:
                    for j in range(8):
                        arrive(k)
                        for x in range(2):
                            u = 2 * j + x
                            if u >= 4:
                                pe.wait_ge(x_cv, u - 3)
                            for m in range(2):
                                last = dense_chan(k, 2 * x + m, bank(u % 4, 2, T)[:, m, :])
                            last.then_inc(slot_done if x else x_mm, 1)
                        k += 1
                    arrive(k)
                    pe.wait_ge(gate_ev, 8 * n + 4)
                    for s in range(S):
                        last = dense_tok(k, s, ps[4][:, s * 64:(s + 1) * 64], cols=64)
                    last.then_inc(slot_done, 1)
                    k += 1
                    k_z = k
                    k += 4

                    def z_half(j, s, half, dst):
                        last = dense_tok(k_z + j, s, dst, c0=half * DC // 2, wc0=half * DC // 2, nk=DC // 2,
                                         start=(half == 0), stop=(half == 1))
                        if half:
                            last.then_inc(slot_done if s else z_mm, 1)
                    arrive(k_z)
                    for s in range(S):
                        pe.wait_ge(x_cv, 13 + s)
                        for half in range(2):
                            z_half(0, s, half, ps[s][:, :])
                    pe.wait_ge(adt_ready, 1)
                    cums = [(0, 0, "t_gt"), (0, 1, "t_lt"), (1, 0, "t_le"), (1, 1, "t_ge")]
                    for s, d, m in cums:
                        last = nc.tensor.matmul(ps[5][:, s * 64 + d * SH:s * 64 + (d + 1) * SH], mat(m),
                                                adt[:, s, d * SH:(d + 1) * SH], start=True, stop=True)
                    last.then_inc(cum_mm, 1)
                    pe.wait_ge(x_act, 16)
                    pe.wait_ge(z_ev, 2)
                    pe.wait_ge(edec_ready, 1)
                    tri = [mat("t_le"), mat("t_ge")]

                    def group_inputs(u):
                        s, g = divmod(u, SG)
                        tok = slice(s * P, (s + 1) * P)
                        if u:
                            pe.wait_ge(xt_ev, u)
                        nc.tensor.transpose(ps[0][:, 0:P], xbcT[:, 2 * g, tok], mat("ident"))
                        nc.tensor.transpose(ps[0][:, P:2 * P], xbcT[:, 2 * g + 1, tok], mat("ident"))
                        nc.tensor.transpose(ps[0][:, 2 * P:3 * P], xbcT[:, 16 + g, tok], mat("ident"))
                        nc.tensor.matmul(ps[0][:, 3 * P:4 * P], xbcT[:, 16 + g, tok], xbcT[:, 24 + g, tok],
                                         start=True, stop=True).then_inc(xt_mm, 1)
                        for d in range(2):
                            pe.wait_ge(tt_ready, 2 * u + d + 1)
                            if u:
                                pe.wait_ge(seg_ready, 2 * (u - 1) + d + 1)
                            nc.tensor.matmul(ps[1 + d][:, :], mat("ones"), (ttri2 if u % 2 else ttri)[:, d, :], start=True, stop=False)
                            nc.tensor.matmul(bank(1 + d, HPG, P), tri[d],
                                             nadt[:, s, d * SH + g * HPG:d * SH + (g + 1) * HPG].unsqueeze(2).to_broadcast([P, HPG, P]),
                                             start=False, stop=True).then_inc(seg_mm, 1)

                    def group_outputs(u):
                        s, g = divmod(u, SG)
                        t = 2 * (u % 2)
                        tok = slice(s * P, (s + 1) * P)
                        pe.wait_ge(m_ready, 2 * u + 2)
                        pe.wait_ge(dtx_ready, u + 1)
                        if u:
                            pe.wait_ge(y_done, u)
                            pe.wait_ge(off_ev, min(u, SG))
                        for h in range(HPG):
                            for d in range(2):
                                last = nc.tensor.matmul(ps[3][:, h * HD:(h + 1) * HD], segs[:, t + d, h * P:(h + 1) * P],
                                                        dtx[:, t + d, h * HD:(h + 1) * HD], start=(d == 0), stop=(d == 1))
                        if s == 0:
                            for d in range(2):
                                for hp in range(2):
                                    last = nc.tensor.matmul(bank(4, 4, P)[:, 2 * d + hp, :], dtxw[:, t + d, hp * P:(hp + 1) * P],
                                                            xtok[:, u % 2, 2 * P:3 * P], start=True, stop=True)
                        else:
                            pe.wait_ge(h0_in[g % 2], 16 * (g // 2 + 1))
                            last = nc.tensor.matmul(ps[4][:, :], xbcT[:, 24 + g, tok], h0[:, g % 2, :], start=True, stop=True)
                        last.then_inc(yg_mm, 1)
                    def y_transposes(s):
                        pe.wait_ge(yn_ready, s + 1)
                        for q in range(4):
                            if s == 0 and q == 0:
                                pe.wait_ge(z_ev, 8)
                            if s == 0 and q == 3:
                                pe.wait_ge(yt_ev, 1)
                            for c in range(4):
                                last = nc.tensor.transpose(bank(Y_BANKS[s][q], 4, P)[:, c, :],
                                                           zs[:, s, (4 * q + c) * P:(4 * q + c + 1) * P], mat("ident"))
                            last.then_inc(yt_mm, 1)

                    for i in range(S * SG + 1):
                        if i < S * SG:
                            group_inputs(i)
                        if 1 <= i <= 12:
                            e = (i - 1) // 2
                            s, j = divmod(e, 3)
                            if i % 2:
                                arrive(k_z + j + 1)
                                if e >= 2:
                                    pe.wait_ge(z_ev, e + 1)
                            z_half(j + 1, s, (i - 1) % 2, ps[6 + e % 2][:, :])
                        if i == S * SG:
                            y_transposes(0)
                        if i:
                            group_outputs(i - 1)
                    pe.wait_ge(y_done, S * SG)
                    y_transposes(1)
                    pe.wait_ge(yt_ev, 6)
                    pe.wait_ge(yt_dve, 2)
                    out_proj(n, k, xbcT, 2)
                norm_transposes(n, 1)
                pe.wait_ge(at_act, S * (2 * n + 2))
                pe.wait_ge(at_dve, S * (2 * n + 2))
                pe.wait_ge(gate_ev, 8 * (n + 1))
                for s in range(S):
                    for c in range(DC):
                        last = nc.tensor.matmul(bank(4, S, NR)[:, s, :], at[:, c, s * P:(s + 1) * P], wr[:, l, c, :],
                                                start=(c == 0), stop=(c == DC - 1))
                last.then_inc(route_mm, 1)
                for s in range(S):
                    for h in range(2):
                        for c in range(4):
                            last = nc.tensor.transpose(bank(2 * s + h, 4, P)[:, c, :], at[:, 4 * h + c, s * P:(s + 1) * P], mat("ident"))
                        last.then_inc(tok_mm, 1)
                pe.wait_ge(oh_ready, n + 1)
                oh = [rt[:, 4, s, :] for s in range(S)]
                nc.tensor.matmul(ps[5][:, 0:EG], mat("t_lt"), oh[0], start=True, stop=True)
                nc.tensor.matmul(ps[5][:, EG:2 * EG], mat("t_lt"), oh[1], start=True, stop=False)
                nc.tensor.matmul(ps[5][:, EG:2 * EG], mat("ones"), oh[0], start=False, stop=True)
                nc.tensor.matmul(ps[5][:, 2 * EG:3 * EG], mat("ones"), oh[0], start=True, stop=False)
                nc.tensor.matmul(ps[5][:, 2 * EG:3 * EG], mat("ones"), oh[1], start=False, stop=True).then_inc(pos_mm, 1)

                def gather_rows(rows_done, places_done):
                    for s in range(S):
                        nc.tensor.transpose(ps[2][:, s * P:(s + 1) * P], onehot[:, s, :], mat("ident"))
                    for s in range(S):
                        last = nc.tensor.matmul(ps[2][:, T:T + XG], onehot[:, s, :], rt[:, 12, s, :], start=(s == 0), stop=(s == 1))
                    last.then_inc(places_done, 1)
                    for c in range(DC):
                        for s in range(S):
                            last = nc.tensor.matmul(bank(4 + c // 4, 4, P)[:, c % 4, :], xn[:, s, c * P:(c + 1) * P], onehot[:, s, :],
                                                    start=(s == 0), stop=(s == 1))
                        if c % 4 == 3:
                            last.then_inc(rows_done, 1)

                def gather(i):
                    pe.wait_ge(onehot_ready, i + (EG * n + 1))
                    pe.wait_ge(gt_ev, i + EG * n)
                    if not (isinstance(i, int) and i == 0):
                        pe.wait_ge(actT_ev, i * XG + (E * n - 1))
                    gather_rows(xg_mm, gt_mm)

                def rows_times(dst, blk, cols=slice(0, SLOT_COLS)):
                    for c in range(DC):
                        last = nc.tensor.matmul(dst, xg[:, c, :], blk[:, c, cols], start=(c == 0), stop=(c == DC - 1))
                    return last

                def act_transposes():
                    for c in range(FF // P):
                        last = nc.tensor.transpose(bank(2, 4, P)[:, c, :], actv[:, 0, c * P:(c + 1) * P], mat("ident"))
                    return last

                def down(blk, start, stop):
                    for j in range(2):
                        for c in range(FF // P):
                            last = nc.tensor.matmul(ps[6 + j][:, :], actT[:, c, :], blk[:, c, j * SLOT_COLS:(j + 1) * SLOT_COLS],
                                                    start=(start and c == 0), stop=(stop and c == FF // P - 1))
                    return last

                def group(k, i, last_group):
                    seq = order(n, last_group)
                    per = len(seq)
                    ks = {w: k + q for q, w in enumerate(seq)}

                    def at_hand(w):
                        if last_group:
                            arrive(ks[w])
                        else:
                            arrive(ks[w], i, per)

                    def turned(x):
                        return i * XG + (E * n + x)

                    def gate_product(x):
                        at_hand(f"G{x}")
                        pe.wait_ge(sg_ready, turned(x))
                        rows_times(ps[0][:, :], slot(ks[f"G{x}"])).then_inc(slot_done, 1)

                    def up_product(x):
                        at_hand(f"U{x}")
                        pe.wait_ge(act_ready, turned(x))
                        rows_times(ps[1][:, :], slot(ks[f"U{x}"])).then_inc(slot_done, 1)

                    def transposes(x):
                        pe.wait_ge(act_ready, turned(x + 1))
                        if x == XG - 1:
                            if not last_group:
                                pe.wait_ge(gt_ev, i + (EG * n + 2))
                            else:
                                pe.wait_ge(actT_ev, turned(x))
                        else:
                            pe.wait_ge(actT_ev, turned(x))
                            if x == 0:
                                pe.wait_ge(gt_ev, i + (EG * n + 1))
                        act_transposes().then_inc(actT_mm, 1)

                    def down_product(x):
                        at_hand(f"D{x}")
                        pe.wait_ge(actT_ev, turned(x + 1))
                        if x == 0:
                            pe.wait_ge(y_ev, i + EG * n)
                        down(slot_down(ks[f"D{x}"]), x == 0, x == XG - 1).then_inc(slot_done, 1)

                    def ada_product(x):
                        if f"A{x}" in ks:
                            pe.wait_ge(ada_step, i * (16 * XG) + 16 * (dve_blocks(n) + x + 1))
                            ada_sums(ps[3][:, bass.ds(i * (16 * S) + x * 4 * S, 4 * S)])
                    pe.wait_ge(xg_ready, i + (EG * n + 1))
                    gate_product(0)
                    up_product(0)
                    for x in range(1, XG):
                        gate_product(x)
                        transposes(x - 1)
                        up_product(x)
                        ada_product(x - 1)
                        down_product(x - 1)
                    if not last_group:
                        gather(i + 1)
                    transposes(XG - 1)
                    ada_product(XG - 1)
                    down_product(XG - 1)

                pe.wait_ge(tok_ev, 4 * (n + 1))
                gather(0)
                pe.wait_ge(ov_known, n + 1)
                flag = pe.value_load(ovi[0:1, 0:1], min_val=0, max_val=1)
                k = moe_base(n)
                with pe.Fori(0, EG - 1) as i:
                    group(k, i, False)
                group(k + (EG - 1) * len(order(n, False)), EG - 1, True)
                pe.wait_ge(y_ev, EG * (n + 1))

                def scatter(groups, out_sem):
                    for s in range(S):
                        for j in range(2):
                            for q, g in enumerate(groups):
                                last = nc.tensor.matmul(ps[4 + 2 * s + j][:, :], ghT[:, g, s * P:(s + 1) * P],
                                                        ysb[:, g, j * SLOT_COLS:(j + 1) * SLOT_COLS],
                                                        start=(q == 0), stop=(q == len(groups) - 1))
                            last.then_inc(out_sem, 1)
                with pe.If(flag > 0):
                    pe.wait_ge(v_oh, n + 1)
                    gather_rows(v_xg, v_gt)
                    pe.wait_ge(v_xg_ev, 2 * (n + 1))
                    with pe.Fori(0, XG) as x:
                        for q in range(2):
                            pe.wait_ge(v_w, x * 48 + (16 * 12 * n + 16 * (q + 1)))
                            rows_times(ps[q][:, :], wov).then_inc(v_done, 1)
                        pe.wait_ge(v_act, x + (XG * n + 1))
                        pe.wait_ge(v_gt_ev, n + 1)
                        act_transposes().then_inc(v_t, 1)
                        pe.wait_ge(v_t_ev, x + (XG * n + 1))
                        pe.wait_ge(v_w, x * 48 + (16 * 12 * n + 48))
                        pe.wait_ge(v_y_ev, x + XG * n)
                        down(wov.rearrange("p c n -> p (c n)").rearrange("p (c n) -> p c n", c=FF // P), True, True).then_inc(v_done, 1)
                    pe.wait_ge(v_y_ev, XG * (n + 1))
                    scatter([EG], v_out)
                    pe.wait_ge(v_added, 4 * (n + 1))
                with pe.Else():
                    pe.sem_inc(v_gt, 1)
                    pe.sem_inc(v_xg, 2)
                    pe.sem_inc(v_done, 3 * XG)
                    pe.sem_inc(v_t, XG)
                    pe.sem_inc(v_out, 4)
                scatter(range(EG), out_mm)

        @block.scalar
        def _(act):
            A = nc.scalar.activation
            act.wait_ge(vecs_in, 16)
            A(cond[:, :, :], vec("cond").rearrange("p (c s) -> p c s", s=S), ACT.Silu).then_inc(cond_ready, 1)
            for j in range(ADA_LOADS // 2):
                act.wait_ge(row_mm, j + 1)
                if j:
                    act.wait_ge(slot_done, 2 * j - 1)
                A(adarow[0:S, 0, :], ps[4][0:S, :], ACT.Copy).then_inc(row_ev, 1)
            act.wait_ge(consts_in, 16 * 7)

            def norm(n, which):
                t = 2 * n + which
                for s in range(S):
                    if t:
                        act.wait_ge(h_ready, 8 * n + ((3, 4)[s] if which else (-2, 0)[s]))
                    A(acc[:, s, :], hid[:, s, :], ACT.Square, accum_out=stat[:, s:s + 1]).then_inc(sq_done, 1)
                    act.wait_ge(var_ready, S * t + s + 1)
                    A(stat[:, 4 + s:5 + s], stat[:, 2 + s:3 + s], ACT.Sqrt).then_inc(rstd_ready, 1)
                if n == len(LAYERS):
                    return
                act.wait_ge(gsc_ready, n + 1)
                for s in range(S):
                    act.wait_ge(tr_mm, 4 * t + 2 * s + 1)
                    for c in range(4):
                        last = A(at[:, c, s * P:(s + 1) * P], bank(2 * s, 4, P)[:, c, :], ACT.Identity,
                                 scale=gsc[:, which, c, s:s + 1], bias=modt[:, 3 * which * DC + c, s:s + 1])
                    last.then_inc(at_act, 1)
                    for h in range(2):
                        act.wait_ge(gate_mm, 4 * t + 2 * s + h + 1)
                        A(gate[:, which, s, h * 512:(h + 1) * 512], ps[gate_bank(which, s, h)][:, :], ACT.Copy).then_inc(gate_ev, 1)

            for n, l in enumerate(LAYERS):
                norm(n, 0)
                k = mix_base(n)
                if l == 0:
                    for u in range(8):
                        act.wait_ge(f1_mm, u + 1)
                        if u >= 2:
                            act.wait_ge(f2_mm, u - 1)
                        A(f1[:, u % 2, :], ps[u % 2][:, :], ACT.Copy).then_inc(f1_ev, 1)
                elif l == 1:
                    for u in range(8):
                        j, mh = divmod(u, 2)
                        if mh:
                            act.wait_ge(slot_done, k + j + 1)
                        else:
                            act.wait_ge(qk_mm, j + 1)
                        if u < 4:
                            A(qT[:, 2 * u:2 * u + 2, :], bank(u % 4, 2, T), ACT.Copy, scale=HD ** -0.5).then_inc(qk_ev, 1)
                        else:
                            A(kT[:, 2 * u - 8:2 * u - 6, :], bank(u % 4, 2, T), ACT.Copy).then_inc(qk_ev, 1)
                    U = S * DC
                    for i in range(U + 2):
                        if i < U:
                            w = P * (1 + i // DC)
                            act.wait_ge(nm_ready, i + 1)
                            if i >= 3:
                                act.wait_ge(t_mm, i - 2)
                            for hh in range(2):
                                last = A(prob[:, i % 3, hh * w:(hh + 1) * w], ps[2 * (i % 2) + hh][:, 0:w], ACT.Exp,
                                         bias=nmax[:, i, hh:hh + 1], accum_out=esum[:, i, hh:hh + 1])
                            last.then_inc(e_ready, 1)
                        if i >= 2:
                            v = i - 2
                            act.wait_ge(t_mm, v + 1)
                            if v >= 2:
                                act.wait_ge(av_mm, v - 1)
                            w = 2 * P * (1 + v // DC)
                            A(probT[:, v % 2, 0:w], ps[4 + v % 2][:, 0:w], ACT.Copy).then_inc(pt_ready, 1)
                elif l == 2:
                    for u in range(16):
                        j, x = divmod(u, 2)
                        if x:
                            act.wait_ge(slot_done, k + GMLP_AT[f"I{j}"] + 1)
                        else:
                            act.wait_ge(m_mm, j + 1)
                        if j < 4:
                            A(uT[:, 2 * u:2 * u + 2, :], bank(u % 4, 2, T), ACT.Gelu_apprx_tanh).then_inc(m_ev, 1)
                        else:
                            A(vg[:, x, (j - 4) * 512:(j - 3) * 512], ps[u % 4][:, :], ACT.Gelu_apprx_tanh).then_inc(m_ev, 1)
                    act.wait_ge(m_ev, 16)
                    for s in range(S):
                        A(acc[:, :, :].rearrange("p a b -> p (a b)"), vg[:, s, :], ACT.Square,
                          accum_out=stat[:, 6 + s:7 + s]).then_inc(vsq, 1)
                        act.wait_ge(vsq, s + 1)
                    for s in range(S):
                        act.wait_ge(vvar, s + 1)
                        A(stat[:, 10 + s:11 + s], stat[:, 8 + s:9 + s], ACT.Sqrt).then_inc(vrstd, 1)
                else:
                    cw, cb = vec("conv_w"), vec("conv_b")
                    for u in range(17):
                        if u < 16:
                            j, x = divmod(u, 2)
                            if x:
                                act.wait_ge(slot_done, k + j + 1)
                            else:
                                act.wait_ge(x_mm, j + 1)
                            for m in range(2):
                                c = 2 * u + m
                                last = A(xbcT[:, c, :], bank(u % 4, 2, T)[:, m, :], ACT.Identity,
                                         scale=cw[:, 64 + c:65 + c], bias=cb[:, c:c + 1])
                            last.then_inc(x_b, 1)
                        if u:
                            act.wait_ge(x_cv, u)
                            A(xbcT[:, 2 * u - 2:2 * u, :], xbcT[:, 2 * u - 2:2 * u, :], ACT.Silu).then_inc(x_act, 1)
                    act.wait_ge(small_in[3], 48)
                    A(dtb[:, 1, :], dtb[:, 1, :], ACT.Exp).then_inc(a_exp, 1)
                    act.wait_ge(dt_abs, 1)
                    A(dtw[:, 2, :], dtw[:, 1, :], ACT.Exp).then_inc(dt_exp, 1)
                    act.wait_ge(dt_abs, 2)
                    A(dtw[:, 4, :], dtw[:, 3, :], ACT.Ln).then_inc(dt_ln, 1)
                    def gate_z(j, s, src):
                        if s:
                            act.wait_ge(slot_done, k + 9 + j + 1)
                        else:
                            act.wait_ge(z_mm, j + 1)
                        A(zs[:, s, j * 512:(j + 1) * 512], src, ACT.Silu).then_inc(z_ev, 1)
                    for s in range(S):
                        gate_z(0, s, ps[s][:, :])

                    gn = vec("gn")

                    def y_square(s):
                        act.wait_ge(y_done, SG * (s + 1))
                        if s:
                            act.wait_ge(ysq, 1)
                        A(at[:, :, :].rearrange("p a b -> p (a b)"), zs[:, s, :], ACT.Square,
                          accum_out=stat[:, 12 + s:13 + s]).then_inc(ysq, 1)

                    def y_root(s):
                        act.wait_ge(yvar, s + 1)
                        A(stat[:, 16 + s:17 + s], stat[:, 14 + s:15 + s], ACT.Sqrt).then_inc(yrstd, 1)

                    def y_scaled(s, q):
                        act.wait_ge(yt_mm, 4 * s + q + 1)
                        for c in range(4):
                            last = A(xbcT[:, 4 * q + c, s * P:(s + 1) * P], bank(Y_BANKS[s][q], 4, P)[:, c, :], ACT.Identity,
                                     scale=gn[:, 4 * q + c:4 * q + c + 1])
                        last.then_inc(yt_ev, 1)
                    act.wait_ge(cum_mm, 1)
                    A(edec[:, :, :], bank(5, 2, 64), ACT.Exp).then_inc(edec_ready, 1)
                    for i in range(S * SG + 1):
                        if i < S * SG:
                            act.wait_ge(xt_mm, i + 1)
                            if i >= 2:
                                act.wait_ge(yg_mm, i - 1)
                                act.wait_ge(y_done, i - 1)
                            A(xtok[:, i % 2, :], ps[0][:, :], ACT.Copy).then_inc(xt_ev, 1)
                            for d in range(2):
                                act.wait_ge(seg_ready, 2 * i + d + 1)
                                A(segs[:, 2 * (i % 2) + d, :], segs[:, 2 * (i % 2) + d, :], ACT.Exp).then_inc(dec_ready, 1)
                        if 1 <= i <= SG:
                            act.wait_ge(yg_mm, i)
                            if i > 2:
                                act.wait_ge(st_out[(i - 1) % 2], 32 * ((i - 1) // 2))
                            A(stout[:, (i - 1) % 2, :], ps[4][:, :], ACT.Copy).then_inc(off_ev, 1)
                        if i in range(2, 13, 2):
                            e = i // 2 - 1
                            gate_z(e % 3 + 1, e // 3, ps[6 + e % 2][:, :])
                        if i == 13:
                            y_square(0)
                        if i == 14:
                            y_root(0)
                        if i == S * SG:
                            for q in range(4):
                                y_scaled(0, q)
                    y_square(1)
                    y_root(1)
                    for q in (0, 2):
                        y_scaled(1, q)
                if l == 3:
                    act.wait_ge(seg_mm, 2 * S * SG)
                    for e in range(2):
                        act.wait_ge(st_out[e], 32 * SG // 2)
                norm(n, 1)
                for r in range(2):
                    act.wait_ge(rexp_in, 2 * n + r + 1)
                    A(rt[:, 2 + 5 * r, :, :], rt[:, 1 + 5 * r, :, :], ACT.Exp).then_inc(rexp, 1)
                def group(k, i, last_group):
                    seq = order(n, last_group)
                    ks = {w: k + q for q, w in enumerate(seq)}

                    def product(w):
                        if last_group:
                            act.wait_ge(slot_done, ks[w] + 1)
                        else:
                            act.wait_ge(slot_done, i * len(seq) + (ks[w] + 1))

                    def silu(x):
                        product(f"G{x}")
                        act.wait_ge(act_ready, i * XG + (E * n + x))
                        A(sgl[:, 0, :], ps[0][:, :], ACT.Silu).then_inc(sg_ready, 1)

                    def transposed(x):
                        act.wait_ge(actT_mm, i * XG + (E * n + x + 1))
                        A(actT[:, :, :], bank(2, 4, P), ACT.Copy).then_inc(actT_ev, 1)
                    silu(0)
                    for x in range(1, XG):
                        silu(x)
                        transposed(x - 1)
                    if not last_group:
                        gathered(i + 1)
                    transposed(XG - 1)
                    product("D3")
                    A(ysb[:, bass.ds(i, 1), :].rearrange("p o (j n) -> p (o j) n", j=2), psum[:, 6:8, :], ACT.Copy).then_inc(y_ev, 1)

                def gathered(i):
                    act.wait_ge(gt_mm, i + (EG * n + 1))
                    A(ghT[:, bass.ds(i, 1), :], ps[2][:, 0:T].unsqueeze(1), ACT.Copy)
                    A(wsl[:, bass.ds(i, 1), :], ps[2][:, T:T + XG].unsqueeze(1), ACT.Copy).then_inc(gt_ev, 1)
                    for h in range(2):
                        act.wait_ge(xg_mm, i * 2 + (2 * EG * n + h + 1))
                        last = A(xg[:, 4 * h:4 * h + 4, :], bank(4 + h, 4, P), ACT.Copy)
                    last.then_inc(xg_ready, 1)
                for s in range(S):
                    for h in range(2):
                        act.wait_ge(tok_mm, 4 * n + 2 * s + h + 1)
                        A(xn[:, s, h * 512:(h + 1) * 512], ps[2 * s + h][:, :], ACT.Copy).then_inc(tok_ev, 1)
                gathered(0)
                act.wait_ge(ov_known, n + 1)
                flag = act.value_load(ovi[0:1, 0:1], min_val=0, max_val=1)
                k = moe_base(n)
                with act.Fori(0, EG - 1) as i:
                    group(k, i, False)
                group(k + (EG - 1) * len(order(n, False)), EG - 1, True)
                with act.If(flag > 0):
                    act.wait_ge(v_gt, n + 1)
                    A(ghT[:, EG, :], ps[2][:, 0:T], ACT.Copy)
                    A(wsl[:, EG, :], ps[2][:, T:T + XG], ACT.Copy).then_inc(v_gt_ev, 1)
                    for h in range(2):
                        act.wait_ge(v_xg, 2 * n + h + 1)
                        A(xg[:, 4 * h:4 * h + 4, :], bank(4 + h, 4, P), ACT.Copy).then_inc(v_xg_ev, 1)
                    with act.Fori(0, XG) as x:
                        act.wait_ge(v_done, x * 3 + (3 * XG * n + 1))
                        act.wait_ge(v_act, x + XG * n)
                        A(sgl[:, 0, :], ps[0][:, :], ACT.Silu).then_inc(v_sg, 1)
                        act.wait_ge(v_t, x + (XG * n + 1))
                        A(actT[:, :, :], bank(2, 4, P), ACT.Copy).then_inc(v_t_ev, 1)
                with act.Else():
                    act.sem_inc(v_gt_ev, 1)
                    act.sem_inc(v_xg_ev, 2)
                    act.sem_inc(v_sg, XG)
                    act.sem_inc(v_t_ev, XG)
            norm(len(LAYERS), 0)

        @block.vector
        def _(dve):
            V = nc.vector
            count = [0]

            def link(ins):
                count[0] += 1
                ins.then_inc(dve_chain, 1)
                dve.wait_ge(dve_chain, count[0])


            def sum_block(k, done, i=None, per=0, sums=adacc):
                def step_wait(steps):
                    if i is None:
                        dve.wait_ge(ada_step, 16 * done + steps)
                    else:
                        dve.wait_ge(ada_step, i * (16 * XG) + (16 * done + steps))
                if i is None:
                    dve.wait_ge(full[k % RING], 16 * (k // RING + 1))
                else:
                    dve.wait_ge(full[k % RING], i * (16 * per // RING) + 16 * (k // RING + 1))
                for c in range(DC):
                    for q in range(S):
                        w = slot(k)[:, c, :]
                        if c == 0:
                            last = V.tensor_scalar(sums[:, q, :], w, cond[:, c, q:q + 1], None, ALU.mult)
                        else:
                            step_wait(2 * c - 1 + q)
                            last = V.scalar_tensor_tensor(sums[:, q, :], w, cond[:, c, q:q + 1], sums[:, q, :], ALU.mult, ALU.add)
                        last.then_inc(ada_step, 1)

            dve.wait_ge(cond_ready, 1)
            for j in range(1, ADA_LOADS, 2):
                if j > 1:
                    dve.wait_ge(slot_done, j - 1)
                sum_block(j, j // 2)
            dve.wait_ge(vecs_in, 16)
            dve.wait_ge(mats_in, 16)
            dve.wait_ge(consts_in, 16 * 7)
            dve.wait_ge(pool_chain, EG)

            def root_input(col_in, col_out, width, signal):
                link(V.tensor_scalar(stat[:, col_out:col_out + 1], stat[:, col_in:col_in + 1], 1.0 / width, EPS, ALU.mult, ALU.add))
                V.reciprocal(stat[:, col_out:col_out + 1], stat[:, col_out:col_out + 1]).then_inc(signal, 1)

            def norm_root(t, s):
                dve.wait_ge(sq_done, S * t + s + 1)
                root_input(s, 2 + s, D, var_ready)

            def norm_scale(t, s):
                dve.wait_ge(rstd_ready, S * t + s + 1)
                if t == 2 * len(LAYERS):
                    link(V.tensor_scalar(xn[:, s, :], hid[:, s, :], stat[:, 4 + s:5 + s], None, ALU.mult))
                    V.tensor_tensor(xn[:, s, :], xn[:, s, :], finalg[:, :], ALU.mult).then_inc(fin_ready, 1)
                else:
                    V.tensor_scalar(xn[:, s, :], hid[:, s, :], stat[:, 4 + s:5 + s], None, ALU.mult).then_inc(xn_ready, 1)

            def modulate(n, which):
                t = 2 * n + which
                for s in range(S):
                    dve.wait_ge(tr_mm, 4 * t + 2 * s + 2)
                    for c in range(4, DC):
                        last = V.tensor_scalar(at[:, c, s * P:(s + 1) * P], bank(2 * s + 1, 4, P)[:, c - 4, :],
                                               gsc[:, which, c, s:s + 1], modt[:, 3 * which * DC + c, s:s + 1], ALU.mult, ALU.add)
                    last.then_inc(at_dve, 1)

            def adaln(n):
                l = LAYERS[n]
                early = n - 1 in EARLY
                if not early:
                    dve.wait_ge(slot_done, moe_base(n - 1) + (EG - 1) * len(MIXED) if n else ADA_LOADS)
                if n:
                    dve.wait_ge(at_act, S * 2 * n)
                    dve.wait_ge(gate_mm, 8 * n)
                V.tensor_tensor(modt[:, :, :], adkept[:, :, :] if early else bank(3, NMOD * DC, S),
                                vec("ada_b")[:, l * NMOD * DC:(l + 1) * NMOD * DC].unsqueeze(2).to_broadcast([P, NMOD * DC, S]),
                                ALU.add).then_inc(ada_ev, 1)
                dve.wait_ge(ada_ev, n + 1)
                for w in range(2):
                    g = vec("g1" if w == 0 else "g2")[:, l * DC:(l + 1) * DC]
                    last = V.scalar_tensor_tensor(gsc[:, w, :, :], modt[:, (3 * w + 1) * DC:(3 * w + 2) * DC, :], 1.0,
                                                  g.unsqueeze(2).to_broadcast([P, DC, S]), ALU.add, ALU.mult)
                last.then_inc(gsc_ready, 1)
                dve.wait_ge(gsc_ready, n + 1)

            def add_mixer(n, k_last):
                t = 2 * n + 1
                for j in range(2):
                    for s in range(S):
                        if s:
                            dve.wait_ge(slot_done, k_last[j] + 1)
                        else:
                            dve.wait_ge(o_mm, 2 * n + j + 1)
                        if j == 0 and s == 0:
                            dve.wait_ge(gate_ev, 8 * n + 4)
                        cols = slice(j * 512, (j + 1) * 512)
                        link(V.tensor_tensor(outtmp[:, s, :], ps[4 + 2 * j + s][:, :], gate[:, 0, s, cols], ALU.mult))
                        V.tensor_tensor(hid[:, s, cols], hid[:, s, cols], outtmp[:, s, :], ALU.add).then_inc(h_ready, 1)
                        if j == 1:
                            norm_root(t, s)
                            dve.wait_ge(h_ready, 8 * n + 3 + s)
                            norm_scale(t, s)

            def first_of_max(vals, m, tmp, onehot, signal=None):
                link(V.tensor_tensor(tmp, vals, m.to_broadcast([P, S, EG]), ALU.is_equal))
                link(V.tensor_tensor(tmp, tmp, first[:, :].unsqueeze(1).to_broadcast([P, S, EG]), ALU.mult))
                link(V.tensor_reduce(m, tmp, AX.X, ALU.max))
                last = V.tensor_tensor(onehot, tmp, m.to_broadcast([P, S, EG]), ALU.is_equal)
                if signal is None:
                    link(last)
                else:
                    last.then_inc(signal, 1)

            def route(n, l):
                R = lambda q: rt[:, q, :, :]
                one = lambda q: rt[:, 16 + q, :, 0:1]
                dve.wait_ge(route_mm, n + 1)
                link(V.tensor_tensor(rlog[:, :, :], bank(4, S, NR), rbias[:, l, :].unsqueeze(1).to_broadcast([P, S, NR]), ALU.add))
                gl = rlog[:, :, 0:EG]
                link(V.tensor_reduce(one(0), gl, AX.X, ALU.max))
                V.tensor_tensor(R(1), gl, one(0).to_broadcast([P, S, EG]), ALU.subtract).then_inc(rexp_in, 1)
                first_of_max(gl, one(0), R(3), R(4), oh_ready)
                dve.wait_ge(rexp, 2 * n + 1)
                link(V.tensor_reduce(one(1), R(2), AX.X, ALU.add))
                link(V.reciprocal(one(1), one(1)))
                dve.wait_ge(oh_ready, n + 1)
                link(V.tensor_tensor(rsel[:, :, :, :], rlog[:, :, EG:NR].rearrange("p s (g e) -> p s g e", g=EG),
                                     R(4).unsqueeze(3).to_broadcast([P, S, EG, EG]), ALU.mult))
                link(V.tensor_reduce(R(5), rsel[:, :, :, :].rearrange("p s g e -> p s e g"), AX.X, ALU.add))
                link(V.tensor_reduce(one(2), R(5), AX.X, ALU.max))
                V.tensor_tensor(R(6), R(5), one(2).to_broadcast([P, S, EG]), ALU.subtract).then_inc(rexp_in, 1)
                dve.wait_ge(rexp, 2 * n + 2)
                link(V.tensor_reduce(one(3), R(7), AX.X, ALU.max))
                first_of_max(R(7), one(3), R(8), R(9))
                link(V.scalar_tensor_tensor(R(10), R(9), -4.0, R(7), ALU.mult, ALU.add))
                link(V.tensor_reduce(one(4), R(10), AX.X, ALU.max))
                first_of_max(R(10), one(4), R(8), R(11))
                link(V.tensor_tensor(R(12), R(9), R(11), ALU.add))
                link(V.tensor_tensor(R(12), R(12), R(7), ALU.mult))
                link(V.tensor_reduce(one(5), R(12), AX.X, ALU.add))
                link(V.reciprocal(one(5), one(5)))
                link(V.tensor_tensor(one(5), one(5), one(1), ALU.mult))
                link(V.tensor_tensor(R(12), R(12), one(5).to_broadcast([P, S, EG]), ALU.mult))
                dve.wait_ge(pos_mm, n + 1)
                link(V.tensor_copy(posr[:, :, :], bank(5, S + 1, EG)))
                O = lambda q: ovs[:, q, :]
                link(V.tensor_scalar(O(0), posr[:, S, :], float(P), None, ALU.is_gt))
                link(V.tensor_tensor(O(1), O(0), first[:, :], ALU.mult))
                link(V.tensor_reduce(O(2)[:, 0:1], O(0), AX.X, ALU.max))
                link(V.tensor_reduce(O(2)[:, 1:2], O(1), AX.X, ALU.add))
                link(V.tensor_scalar(O(2)[:, 2:3], O(2)[:, 0:1], float(EG), None, ALU.mult))
                link(V.tensor_tensor(O(2)[:, 2:3], O(2)[:, 2:3], O(2)[:, 1:2], ALU.subtract))
                link(V.tensor_scalar(O(2)[:, 1:2], O(2)[:, 2:3], float(XG), None, ALU.mult))
                V.tensor_copy(ovi[:, :], O(2)[:, 0:2]).then_inc(ov_known, 1)

            def build_onehot(n, i):
                for s in range(S):
                    last = V.tensor_scalar(onehot[:, s, :], mat("iota"), posr[:, s, bass.ds(i, 1)], rt[:, 4, s, bass.ds(i, 1)],
                                           ALU.is_equal, ALU.mult)
                last.then_inc(onehot_ready, 1)

            for n, l in enumerate(LAYERS):
                if n == 0:
                    adaln(0)
                    for s in range(S):
                        norm_root(0, s)
                        norm_scale(0, s)
                modulate(n, 0)
                k = mix_base(n)
                if l == 0:
                    for u in range(8):
                        s, gp = divmod(u, 4)
                        dve.wait_ge(f2_mm, u + 1)
                        V.tensor_copy(ft[:, 2 * gp:2 * gp + 2, s * P:(s + 1) * P], bank(2 + u % 2, 2, P)).then_inc(ft_ready, 1)
                    add_mixer(n, [k, k + 1])
                elif l == 1:
                    dve.wait_ge(small_in[1], 48)
                    link(V.tensor_tensor(rpb, rpb, mat("na_mask").unsqueeze(1).to_broadcast([P, HEADS, P]), ALU.add))
                    for j in range(2):
                        for s in range(S):
                            if s:
                                dve.wait_ge(slot_done, k + 4 + j + 1)
                            else:
                                dve.wait_ge(v_mm, j + 1)
                            V.tensor_copy(vtok[:, s, j * 512:(j + 1) * 512], ps[2 * j + s][:, :]).then_inc(v_ev, 1)
                    for h in range(2):
                        dve.wait_ge(kt_mm, h + 1)
                        V.tensor_copy(xn[:, 0, h * 512:(h + 1) * 512], ps[4 + h][:, :]).then_inc(kt_ev, 1)
                    U = S * DC
                    for i in range(U + 4):
                        if i < U:
                            s, j = divmod(i, DC)
                            dve.wait_ge(s_mm, i + 1)
                            sc = psum[:, 2 * (i % 2):2 * (i % 2) + 2, 0:P * (1 + s)]
                            if s:
                                link(V.tensor_tensor(sc[:, :, 0:P], sc[:, :, 0:P], rpb[:, 2 * j:2 * j + 2, :], ALU.add))
                            V.tensor_reduce(nmax[:, i, :], sc, AX.X, ALU.max, negate=True).then_inc(nm_ready, 1)
                        if 1 <= i <= U:
                            v = i - 1
                            w = P * (1 + v // DC)
                            dve.wait_ge(e_ready, v + 1)
                            link(V.reciprocal(rsum[:, v, :], esum[:, v, :]))
                            pr = prob[:, v % 3, 0:2 * w].rearrange("p (h k) -> p h k", h=2)
                            V.tensor_tensor(pr, pr, rsum[:, v, :].unsqueeze(2).to_broadcast([P, 2, w]), ALU.mult).then_inc(p_ready, 1)
                        if i >= 4:
                            v = i - 4
                            s, j = divmod(v, DC)
                            dve.wait_ge(av_mm, v + 1)
                            V.tensor_copy(oT[:, j, s * P:(s + 1) * P], ps[6 + v % 2][:, 0:P]).then_inc(ot_ready, 1)
                    dve.wait_ge(kv_out, 32)
                    add_mixer(n, [k + 6, k + 7])
                elif l == 2:
                    def early_blocks(xs, b):
                        for x in xs:
                            dve.wait_ge(slot_done, k + GMLP_AT[f"A{x - 2}"] + 1 if x >= 2 else k)
                            sum_block(k + GMLP_AT[f"A{x}"], dve_blocks(n) + x, sums=adacc2 if x % 2 else adacc)
                        dve.wait_ge(slot_done, k + GMLP_AT[f"A{xs[-1]}"] + 1)
                        cols = slice(4 * xs[0], 4 * xs[-1] + 4)
                        V.tensor_copy(adkept[:, cols, :], bank(b, NMOD * DC, S)[:, cols, :]).then_inc(ada_kept, 1)
                    early_blocks(range(8), 7)
                    for s in range(S):
                        dve.wait_ge(vsq, s + 1)
                        root_input(6 + s, 8 + s, GDFF, vvar)
                    for s in range(S):
                        dve.wait_ge(vrstd, s + 1)
                        V.tensor_scalar(vg[:, s, :], vg[:, s, :], stat[:, 10 + s:11 + s], None, ALU.mult).then_inc(vn_ready, 1)
                    dve.wait_ge(small_in[2], 32)
                    gv = vec("gv")
                    for g in range(SG):
                        dve.wait_ge(sp_mm, g + 1)
                        for ci in range(2):
                            c = 2 * g + ci
                            link(V.scalar_tensor_tensor(
                                gt[:, ci, :].rearrange("p (s t) -> p s t", s=S),
                                bank(g % 4, 2, T)[:, ci, :].rearrange("p (s t) -> p s t", s=S), gv[:, c:c + 1],
                                bs[:, g, :].unsqueeze(1).to_broadcast([P, S, P]), ALU.mult, ALU.add))
                            last = V.tensor_tensor(uT[:, c, :], uT[:, c, :], gt[:, ci, :], ALU.mult)
                        last.then_inc(sp_ev, 1)
                    early_blocks(range(8, ADA_LOADS), 3)
                    dve.wait_ge(ada_kept, 2)
                    add_mixer(n, [k + GMLP_AT["O1"], k + GMLP_AT["O3"]])
                else:
                    cw = vec("conv_w")
                    for u in range(16):
                        dve.wait_ge(x_b, u + 1)
                        for tap, (o0, i0, w) in ((0, (2, 0, P - 2)), (1, (1, 0, P - 1)), (3, (0, 1, P - 1))):
                            for m in range(2):
                                c = 2 * u + m
                                x = xbcT[:, c, :].rearrange("p (s t) -> p s t", s=S)
                                src = bank(u % 4, 2, T)[:, m, :].rearrange("p (s t) -> p s t", s=S)
                                last = V.scalar_tensor_tensor(x[:, :, o0:o0 + w], src[:, :, i0:i0 + w], cw[:, tap * 32 + c:tap * 32 + c + 1],
                                                              x[:, :, o0:o0 + w], ALU.mult, ALU.add)
                                if tap < 3:
                                    link(last)
                        last.then_inc(x_cv, 1)
                    dve.wait_ge(slot_done, k + 9)
                    dve.wait_ge(small_in[3], 48)
                    W = lambda q: dtw[:, q, :]
                    W2 = lambda q: dtw[:, q, :].rearrange("p (s h) -> p s h", s=S)
                    both = lambda r: dtb[:, r, :].unsqueeze(1).to_broadcast([P, S, 64])
                    link(V.tensor_tensor(W2(0), bank(4, S, 64), both(0), ALU.add))
                    V.scalar_tensor_tensor(W(1), W(0), -1.0, W(0), ALU.mult, ALU.min).then_inc(dt_abs, 1)
                    dve.wait_ge(dt_exp, 1)
                    V.tensor_scalar(W(3), W(2), 1.0, None, ALU.add).then_inc(dt_abs, 1)
                    dve.wait_ge(dt_abs, 2)
                    link(V.tensor_scalar(W(5), W(3), -1.0, None, ALU.add))
                    link(V.tensor_scalar(W(6), W(5), 0.0, None, ALU.is_equal))
                    link(V.tensor_tensor(W(5), W(5), W(6), ALU.add))
                    link(V.reciprocal(W(5), W(5)))
                    dve.wait_ge(dt_ln, 1)
                    link(V.tensor_tensor(W(4), W(4), W(6), ALU.add))
                    link(V.tensor_tensor(W(4), W(4), W(5), ALU.mult))
                    link(V.tensor_tensor(W(4), W(4), W(2), ALU.mult))
                    link(V.scalar_tensor_tensor(W(7), W(0), 0.0, W(4), ALU.max, ALU.add))
                    dve.wait_ge(a_exp, 1)
                    link(V.tensor_tensor(nadt[:, :, :], W2(7), both(1), ALU.mult))
                    V.tensor_scalar(adt[:, :, :], nadt[:, :, :], -1.0, None, ALU.mult).then_inc(adt_ready, 1)
                    dve.wait_ge(edec_ready, 1)
                    tri = [mat("t_le"), mat("t_ge")]
                    heads = lambda x: x.rearrange("p (h e) -> p h e", h=HPG)
                    over = lambda x: x.unsqueeze(2).to_broadcast([P, HPG, HD])

                    def of_group(u):
                        s, g = divmod(u, SG)
                        return s, g, 2 * (u % 2), [slice(d * SH + g * HPG, d * SH + (g + 1) * HPG) for d in range(2)]

                    def group_operands(u):
                        s, g, t, hs = of_group(u)
                        if u >= 2:
                            dve.wait_ge(yg_mm, u - 1)
                        for d in range(2):
                            dve.wait_ge(seg_mm, 2 * u + d + 1)
                            V.tensor_scalar(segs[:, t + d, :], ps[1 + d][:, :], 0.0, None, ALU.min).then_inc(seg_ready, 1)
                        dve.wait_ge(xt_ev, u + 1)
                        x = heads(xtok[:, u % 2, 0:256])
                        for d in range(2):
                            last = V.tensor_tensor(heads(dtx[:, t + d, :]), x, over(W2(7)[:, s, hs[d]]), ALU.mult)
                            if d:
                                last.then_inc(dtx_step, 1)
                        for d in range(2):
                            V.tensor_tensor(cbm[:, t + d, :], xtok[:, u % 2, 384:512], tri[d], ALU.mult).then_inc(cbm_step, 1)
                        dve.wait_ge(dtx_step, u + 1)
                        if s == 0:
                            for d in range(2):
                                last = V.tensor_tensor(heads(dtxw[:, t + d, :]), heads(dtx[:, t + d, :]), over(edec[:, 0, hs[d]]), ALU.mult)
                            last.then_inc(dtx_ready, 1)
                        else:
                            V.memset(stat[:, 27:28], 0.0).then_inc(dtx_ready, 1)
                        for d in range(2):
                            dve.wait_ge(dec_ready, 2 * u + d + 1)
                            dve.wait_ge(cbm_step, 2 * u + d + 1)
                            V.tensor_tensor(heads(segs[:, t + d, :]), heads(segs[:, t + d, :]),
                                            cbm[:, t + d, :].unsqueeze(1).to_broadcast([P, HPG, P]), ALU.mult).then_inc(m_ready, 1)

                    def group_gated(u):
                        s, g, t, hs = of_group(u)
                        if u:
                            dve.wait_ge(y_done, u)
                        link(V.tensor_tensor(heads(yfix[:, 0, :]), heads(xtok[:, u % 2, 0:256]), over(dtb[:, 2, g * HPG:(g + 1) * HPG]), ALU.mult))
                        dve.wait_ge(yg_mm, u + 1)
                        link(V.tensor_tensor(yfix[:, 0, :], yfix[:, 0, :], ps[3][:, 0:256], ALU.add))
                        if s == 1:
                            for d in range(2):
                                cols = slice(d * 256, (d + 1) * 256)
                                last = V.tensor_tensor(heads(offs[:, 0, cols]), heads(ps[4][:, cols]), over(edec[:, 1, hs[d]]), ALU.mult)
                            link(last)
                            for d in range(2):
                                link(V.tensor_tensor(yfix[:, 0, :], yfix[:, 0, :], offs[:, 0, d * 256:(d + 1) * 256], ALU.add))
                        j = g // 2
                        dve.wait_ge(z_ev, (1 + s) if j == 0 else 2 + 3 * s + j)
                        zg = zs[:, s, g * 256:(g + 1) * 256]
                        V.tensor_tensor(zg, zg, yfix[:, 0, :], ALU.mult).then_inc(y_done, 1)
                    def y_root_input(s):
                        dve.wait_ge(ysq, s + 1)
                        root_input(12 + s, 14 + s, 2 * D, yvar)

                    def y_normalised(s):
                        dve.wait_ge(y_done, SG * (s + 1))
                        dve.wait_ge(yrstd, s + 1)
                        V.tensor_scalar(zs[:, s, :], zs[:, s, :], stat[:, 16 + s:17 + s], None, ALU.mult).then_inc(yn_ready, 1)
                    for i in range(S * SG + 1):
                        if i < S * SG:
                            group_operands(i)
                        if i:
                            group_gated(i - 1)
                        if i == 14:
                            y_root_input(0)
                        if i == 15:
                            y_normalised(0)
                    y_root_input(1)
                    y_normalised(1)
                    gn = vec("gn")
                    for q in (1, 3):
                        dve.wait_ge(yt_mm, 4 + q + 1)
                        for c in range(4):
                            last = V.tensor_scalar(xbcT[:, 4 * q + c, P:2 * P], bank(Y_BANKS[1][q], 4, P)[:, c, :],
                                                   gn[:, 4 * q + c:4 * q + c + 1], None, ALU.mult)
                        last.then_inc(yt_dve, 1)
                    add_mixer(n, [k + 14, k + 16])
                modulate(n, 1)
                route(n, l)
                build_onehot(n, 0)
                dve.wait_ge(ov_known, n + 1)
                flag = dve.value_load(ovi[0:1, 0:1], min_val=0, max_val=1)
                k = moe_base(n)

                def group(k, i, last_group):
                    seq = order(n, last_group)
                    ks = {w: k + q for q, w in enumerate(seq)}
                    if not last_group:
                        dve.wait_ge(xg_ready, i + (EG * n + 1))
                        build_onehot(n, i + 1)
                    for x in range(XG):
                        dve.wait_ge(sg_ready, i * XG + (E * n + x + 1))
                        if last_group:
                            dve.wait_ge(slot_done, ks[f"U{x}"] + 1)
                        else:
                            dve.wait_ge(slot_done, i * len(seq) + (ks[f"U{x}"] + 1))
                        if x or n:
                            dve.wait_ge(actT_mm, i * XG + (E * n + x))
                        V.scalar_tensor_tensor(actv[:, 0, :], sgl[:, 0, :], weight(i, x), ps[1][:, :], ALU.mult, ALU.mult)\
                            .then_inc(act_ready, 1)
                        if f"A{x}" in ks:
                            per = len(seq)
                            if x:
                                dve.wait_ge(slot_done, i * per + (ks[f"A{x - 1}"] + 1))
                            else:
                                dve.wait_ge(slot_done, i * per + k)
                            sum_block(ks[f"A{x}"], dve_blocks(n) + x, i, per)

                def weight(i, x):
                    return wsl[:, bass.ds(i, 1), x:x + 1].rearrange("p o x -> p (o x)")
                with dve.Fori(0, EG - 1) as i:
                    group(k, i, False)
                if n + 1 < len(LAYERS):
                    adaln(n + 1)
                group(k + (EG - 1) * len(order(n, False)), EG - 1, True)

                dve.wait_ge(gate_ev, 8 * (n + 1))

                def add_moe(out_sem, base, signal, linked, streams=range(S), halves=range(2)):
                    for s in streams:
                        for j in halves:
                            dve.wait_ge(out_sem, base + 2 * s + j + 1)
                            cols = slice(j * 512, (j + 1) * 512)
                            linked(V.tensor_tensor(outtmp[:, j, :], ps[4 + 2 * s + j][:, :], gate[:, 1, s, cols], ALU.mult))
                            V.tensor_tensor(hid[:, s, cols], hid[:, s, cols], outtmp[:, j, :], ALU.add).then_inc(signal, 1)
                with dve.If(flag > 0):
                    O = lambda q: ovs[:, q, :]
                    ch = [n * 64]

                    def vlink(ins):
                        ch[0] += 1
                        ins.then_inc(v_chain, 1)
                        dve.wait_ge(v_chain, ch[0])
                    vlink(V.tensor_tensor(ovs[:, 4:6, :], posr[:, 0:S, :], O(0).unsqueeze(1).to_broadcast([P, S, EG]), ALU.mult))
                    vlink(V.tensor_tensor(ovs[:, 6:8, :], rt[:, 4, :, :], O(0).unsqueeze(1).to_broadcast([P, S, EG]), ALU.mult))
                    vlink(V.tensor_reduce(O(3)[:, 0:2], ovs[:, 4:6, :], AX.X, ALU.add))
                    vlink(V.tensor_reduce(O(3)[:, 2:4], ovs[:, 6:8, :], AX.X, ALU.add))
                    vlink(V.tensor_scalar(O(3)[:, 0:2], O(3)[:, 0:2], -float(P), None, ALU.add))
                    vlink(V.memset(ysb[:, EG, :], 0.0))
                    dve.wait_ge(y_ev, EG * (n + 1))
                    for s in range(S):
                        last = V.tensor_scalar(onehot[:, s, :], mat("iota"), O(3)[:, s:s + 1], O(3)[:, 2 + s:3 + s],
                                               ALU.is_equal, ALU.mult)
                    last.then_inc(v_oh, 1)
                    with dve.Fori(0, XG) as x:
                        dve.wait_ge(v_sg, x + (XG * n + 1))
                        dve.wait_ge(v_gt_ev, n + 1)
                        dve.wait_ge(v_done, x * 3 + (3 * XG * n + 2))
                        dve.wait_ge(v_t, x + XG * n)
                        V.scalar_tensor_tensor(actv[:, 0, :], sgl[:, 0, :], wsl[:, EG, bass.ds(x, 1)], ps[1][:, :], ALU.mult, ALU.mult)\
                            .then_inc(v_act, 1)
                        dve.wait_ge(v_done, x * 3 + (3 * XG * n + 3))
                        dve.wait_ge(v_y_ev, x + XG * n)
                        ys = ysb[:, EG, :].rearrange("p (j n) -> p j n", j=2)
                        V.tensor_tensor(ys, ys, psum[:, 6:8, :], ALU.add).then_inc(v_y_ev, 1)
                    add_moe(v_out, 4 * n, v_added, vlink)
                    dve.wait_ge(v_added, 4 * (n + 1))
                    vlink(V.tensor_copy(O(3), O(0)))
                    V_LINKS = ch[0] - n * 64
                    V.nop().then_inc(v_chain, 64 - V_LINKS)
                with dve.Else():
                    dve.sem_inc(v_oh, 1)
                    dve.sem_inc(v_act, XG)
                    dve.sem_inc(v_y_ev, XG)
                    dve.sem_inc(v_added, 4)
                    dve.sem_inc(v_chain, 64)
                t = 2 * (n + 1)
                add_moe(out_mm, 4 * n, h_ready, link, [0])
                norm_root(t, 0)
                add_moe(out_mm, 4 * n, h_ready, link, [1], [0])
                dve.wait_ge(h_ready, 8 * n + 6)
                norm_scale(t, 0)
                add_moe(out_mm, 4 * n, h_ready, link, [1], [1])
                norm_root(t, 1)
                dve.wait_ge(h_ready, 8 * (n + 1))
                norm_scale(t, 1)


_AS_GIVEN = ["x_prompt", "x_sample", "cache_v", "ada_w", "final_g", "fnet_w_o", "na_w_qkv", "na_w_o",
             "gmlp_w_in", "gmlp_b_s", "gmlp_w_out", "ssd_w_in", "ssd_a_log", "ssd_dt_bias", "ssd_d_skip", "ssd_w_out",
             "moe_b_gr", "moe_b_er", "moe_w_gate", "moe_w_up", "moe_w_down"]
_OUTS = [("y_prompt", (1, P, D)), ("y_sample", (1, P, D)),
         ("new_cache_k", (1, 1, HEADS, P, HD)), ("new_cache_v", (1, 1, HEADS, P, HD)),
         ("new_state_ssm_fwd", (1, 1, SH, HD, P)), ("new_state_ssm_bwd", (1, 1, SH, HD, P))]


def constant_matrices():
    i = np.arange(P)
    r, c = i[:, None], i[None, :]
    angle = 2 * np.pi * ((r * c) % P) / P
    grid_w, win = 64, 16
    qc, kc = r % grid_w, c % grid_w
    w0 = np.clip(qc - win // 2, 0, grid_w - win)
    m = {"iota": c + 0 * r, "ident": r == c, "ones": r >= 0 * c, "t_le": r <= c, "t_ge": r >= c, "t_gt": r > c, "t_lt": r < c,
         "dft_c": np.cos(angle), "dft_s": np.sin(angle), "seq_c": np.cos(angle) / P, "seq_ns": -np.sin(angle) / P,
         "na_mask": np.where((kc >= w0) & (kc < w0 + win), 0.0, -1e30)}
    return np.ascontiguousarray(np.stack([np.broadcast_to(m[k], (P, P)).astype(np.float32) for k in MATS], 1))


def columns(x):
    return np.asarray(x).reshape(-1, P).T


def lay_out(x):
    x = {k: np.asarray(v) for k, v in x.items()}
    arrays = {k: np.ascontiguousarray(x[k]) for k in _AS_GIVEN}
    cond = np.stack([x["c_ctx"].reshape(DC, P), x["c"][0].reshape(DC, P)], 1)
    packed = {"g1": columns(x["norm1_g"]), "g2": columns(x["norm2_g"]), "ada_b": columns(x["ada_b"]),
              "cond": columns(cond), "gv": columns(x["gmlp_g_v"]), "gn": columns(x["ssd_g_norm"]),
              "conv_w": columns(x["ssd_conv_w"]), "conv_b": columns(x["ssd_conv_b"])}
    arrays["vecs"] = np.ascontiguousarray(np.concatenate([packed[k] for k, _ in VECS], 1))
    arrays["mats"] = constant_matrices()
    arrays["wgr"] = np.ascontiguousarray(x["moe_w_gr"].reshape(DEPTH, DC, P, EG).transpose(2, 0, 1, 3))
    arrays["wer"] = np.ascontiguousarray(x["moe_w_er"].reshape(DEPTH, DC, P, E).transpose(2, 0, 1, 3))
    i = np.arange(P)
    rr = (i[None, :] // 64) - (i[:, None] // 64) + 7
    cc = np.clip((i[None, :] % 64) - (i[:, None] % 64), -15, 15) + 15
    arrays["rpb_band"] = np.ascontiguousarray(x["na_rpb"][0][:, rr, cc].transpose(1, 0, 2))
    arrays["cache_kT"] = np.ascontiguousarray(x["cache_k"][0, 0].reshape(DC, 2, P, HD).transpose(1, 3, 0, 2).reshape(P, DC, P))
    arrays["wsT"] = np.ascontiguousarray(x["gmlp_w_s"][0].transpose(2, 0, 1))
    arrays["h0T"] = np.ascontiguousarray(
        np.stack([x["state_ssm_fwd"][0, 0].reshape(2 * D, P).T, x["state_ssm_bwd"][0, 0].reshape(2 * D, P).T], 1))
    return arrays


def kernel(**inputs):
    import concourse.bacc as _bacc
    from concourse.bass_utils import run_bass_kernel_spmd as _run

    nc = _bacc.Bacc("TRN2", target_bir_lowering=False, num_devices=1)
    given = lay_out(inputs)
    arrays = {f"in_{k}": v for k, v in given.items()}
    a = {k: nc.dram_tensor(f"in_{k}", v.shape, mybir.dt.from_np(v.dtype), kind="ExternalInput").ap() for k, v in given.items()}
    o = {k: nc.dram_tensor(f"out_{k}", shape, FP32, kind="ExternalOutput").ap() for k, shape in _OUTS}
    build(nc, a, o)
    r = _run(nc, [arrays], core_ids=[0])
    return tuple(r.results[0][f"out_{k}"] for k, _ in _OUTS)
```
